# Optimizing a Trainium2 kernel written in Bass

```python
import jax, jax.numpy as jnp
from jax import lax
import numpy as np

D_MODEL = 2048
BATCH = 1
SEQ = 256
DEPTH = 1
DEC_BATCH = 8
DEC_SEQ = 8
PAST_LEN = 2048
PAGE_SIZE = 128

RWKV_WIDTH = D_MODEL // 2
HEAD_DIM = 64
N_HEADS = RWKV_WIDTH // HEAD_DIM
POOL_WIDTH = D_MODEL // 2
POOL_WINDOWS = (2, 4, 8, 16)
N_POOL_GROUPS = len(POOL_WINDOWS)
POOL_GROUP = POOL_WIDTH // N_POOL_GROUPS
POOL_BUF = max(POOL_WINDOWS) - 1
PLE_DIM = 256
DECAY_RANK = max(32, int(round(1.8 * D_MODEL ** 0.5 / 32)) * 32)
AAA_RANK = max(32, int(round(1.8 * D_MODEL ** 0.5 / 32)) * 32)
MV_RANK = max(32, int(round(1.3 * D_MODEL ** 0.5 / 32)) * 32)
N_BRANCH = 2
IN_COLS = 4 * RWKV_WIDTH + 2 * POOL_WIDTH + N_BRANCH * D_MODEL
RMS_EPS = 1e-6
GN_EPS = 64e-5
DECAY_SCALE = 0.606531

kernel_name = "rwkv7_pool_gated_hybrid_step"

def _rmsnorm(x, g):
    xf = x.astype(jnp.float32)
    y = xf * lax.rsqrt(jnp.mean(xf * xf, axis=-1, keepdims=True) + RMS_EPS)
    return (y * g.astype(jnp.float32)).astype(x.dtype)

def _wkv7_scan(S0, r, decay, k, v, a_vec, b_vec):
    def step(S, inp):
        r_t, w_t, k_t, v_t, a_t, b_t = inp
        sa = jnp.einsum('bhij,bhj->bhi', S, a_t)
        S = S * w_t[..., None, :] + sa[..., :, None] * b_t[..., None, :] + v_t[..., :, None] * k_t[..., None, :]
        o = jnp.einsum('bhij,bhj->bhi', S, r_t)
        return S, o
    xs = tuple(jnp.swapaxes(t.astype(jnp.float32), 0, 1) for t in (r, decay, k, v, a_vec, b_vec))
    S, o = lax.scan(step, S0.astype(jnp.float32), xs)
    return S, jnp.swapaxes(o, 0, 1)

def _causal_pool(u, buf, n_past):
    T = u.shape[1]
    u_ext = jnp.concatenate([buf.astype(u.dtype), u], axis=1)
    cs = jnp.cumsum(u_ext.astype(jnp.float32), axis=1)
    cs = jnp.concatenate([jnp.zeros_like(cs[:, :1]), cs], axis=1)
    hi = cs[:, POOL_BUF + 1:]
    pos = jnp.arange(T) + n_past + 1
    outs = []
    for gi, win in enumerate(POOL_WINDOWS):
        sl = slice(gi * POOL_GROUP, (gi + 1) * POOL_GROUP)
        lo = cs[:, POOL_BUF + 1 - win: POOL_BUF + 1 - win + T, sl]
        cnt = jnp.minimum(pos, win).astype(jnp.float32)[None, :, None]
        outs.append((hi[..., sl] - lo) / cnt)
    mean = jnp.stack(outs, axis=2)
    return mean, u_ext[:, -POOL_BUF:]

def _hybrid_layer(x, p, wkv0, shift0, pool0, n_past, v_first, lw):
    B, T, _ = x.shape
    R, P, H, N, D = RWKV_WIDTH, POOL_WIDTH, N_HEADS, HEAD_DIM, D_MODEL
    f32 = jnp.float32
    h = _rmsnorm(x, lw['norm_pre'])
    z = h @ lw['w_in']
    z_rkv = z[..., :3 * R]
    prev0 = (shift0.astype(h.dtype) @ lw['w_in'][:, :3 * R])[:, None]
    z_rkv_prev = jnp.concatenate([prev0, z_rkv[:, :-1]], axis=1)
    z_rkv = z_rkv + (z_rkv_prev - z_rkv) * lw['mu_rkv'].reshape(3 * R)
    r, k, v = z_rkv[..., :R], z_rkv[..., R:2 * R], z_rkv[..., 2 * R:]
    o_ = 3 * R
    g_rwkv = z[..., o_:o_ + R]; o_ += R
    u = z[..., o_:o_ + P]; o_ += P
    g_pool = z[..., o_:o_ + P]; o_ += P
    gate_a = z[..., o_:o_ + D]; o_ += D
    gate_b = z[..., o_:o_ + D]
    h_prev = jnp.concatenate([shift0.astype(h.dtype)[:, None], h[:, :-1]], axis=1)
    dh = h_prev - h
    xw = h + dh * lw['mu_lora'][0]
    xa = h + dh * lw['mu_lora'][1]
    decay = jnp.exp(-DECAY_SCALE * jax.nn.sigmoid(
        (lw['w0'] + jnp.tanh(xw @ lw['w1']) @ lw['w2']).astype(f32)))
    a = jax.nn.sigmoid((lw['a0'] + (xa @ lw['a1']) @ lw['a2']).astype(f32))
    if v_first is None:
        v_first = v
    else:
        xv = h + dh * lw['mu_lora'][2]
        v = v + (v_first - v) * jax.nn.sigmoid(lw['v0'] + (xv @ lw['v1']) @ lw['v2'])
    kf = k.astype(f32)
    kk = (kf * lw['k_k']).reshape(B, T, H, N)
    kk = kk / jnp.maximum(jnp.linalg.norm(kk, axis=-1, keepdims=True), 1e-12)
    kf = kf * (1.0 + (a - 1.0) * lw['k_a'])
    rh = r.astype(f32).reshape(B, T, H, N)
    kh = kf.reshape(B, T, H, N)
    vh = v.astype(f32).reshape(B, T, H, N)
    ah = a.reshape(B, T, H, N)
    S, o = _wkv7_scan(wkv0, rh, decay.reshape(B, T, H, N), kh, vh, -kk, kk * ah)
    mu = jnp.mean(o, axis=-1, keepdims=True)
    var = jnp.mean(jnp.square(o - mu), axis=-1, keepdims=True)
    on = ((o - mu) * lax.rsqrt(var + GN_EPS)).reshape(B, T, R) * lw['ln_w'] + lw['ln_b']
    bonus = jnp.sum(rh * kh * lw['r_k'].astype(f32).reshape(H, N), axis=-1, keepdims=True) * vh
    y_a = (on + bonus.reshape(B, T, R)).astype(x.dtype) * jax.nn.silu(g_rwkv)
    mean, pool_new = _causal_pool(u, pool0, n_past)
    mixed = (mean - u.astype(f32).reshape(B, T, N_POOL_GROUPS, POOL_GROUP)).astype(x.dtype)
    y_b = jnp.einsum('btgc,gcd->btgd', mixed, lw['pool_w']).reshape(B, T, P)
    y_b = y_b * lw['pool_scale'] * jax.nn.silu(g_pool)
    m = jax.nn.sigmoid(gate_a) * (y_a @ lw['w_branch'][0]) + jax.nn.sigmoid(gate_b) * (y_b @ lw['w_branch'][1])
    x = x + _rmsnorm(m @ lw['w_out'], lw['norm_post'])
    x = x + jax.nn.sigmoid(x @ lw['w_ple_gate']) * (p.astype(x.dtype) @ lw['w_ple'])
    return x, v_first, S.astype(x.dtype), h[:, -1], pool_new

def setup_inputs(seed: int = 0) -> dict:
    key = jax.random.key(seed)
    ks = iter(jax.random.split(key, 48))
    nrm = lambda shape, s: jax.random.normal(next(ks), shape, jnp.float32) * s
    uni = lambda shape: jax.random.uniform(next(ks), shape, jnp.float32)
    L, R, P, D = DEPTH, RWKV_WIDTH, POOL_WIDTH, D_MODEL
    return {
        "x_prompt": nrm((BATCH, SEQ, D), 1.0),
        "x_sample": nrm((DEC_BATCH, DEC_SEQ, D), 1.0),
        "state_wkv": nrm((L, DEC_BATCH, N_HEADS, HEAD_DIM, HEAD_DIM), 0.3),
        "state_shift": nrm((L, DEC_BATCH, D), 1.0),
        "state_pool": nrm((L, DEC_BATCH, POOL_BUF, P), 1.0),
        "p_prompt": nrm((L, BATCH, SEQ, PLE_DIM), 1.0),
        "p_sample": nrm((L, DEC_BATCH, DEC_SEQ, PLE_DIM), 1.0),
        "norm_pre": 1.0 + nrm((L, D), 0.05),
        "norm_post": 1.0 + nrm((L, D), 0.05),
        "w_in": nrm((L, D, IN_COLS), D ** -0.5),
        "mu_rkv": uni((L, 3, R)),
        "mu_lora": uni((L, 3, D)),
        "w0": nrm((L, R), 1.0),
        "w1": nrm((L, D, DECAY_RANK), D ** -0.5),
        "w2": nrm((L, DECAY_RANK, R), 0.5 * DECAY_RANK ** -0.5),
        "a0": nrm((L, R), 0.1),
        "a1": nrm((L, D, AAA_RANK), D ** -0.5),
        "a2": nrm((L, AAA_RANK, R), 0.5 * AAA_RANK ** -0.5),
        "v0": nrm((L - 1, R), 0.1),
        "v1": nrm((L - 1, D, MV_RANK), D ** -0.5),
        "v2": nrm((L - 1, MV_RANK, R), 0.5 * MV_RANK ** -0.5),
        "k_k": 0.85 + nrm((L, R), 0.05),
        "k_a": 1.0 + nrm((L, R), 0.05),
        "r_k": nrm((L, R), 0.1),
        "ln_w": 1.0 + nrm((L, R), 0.05),
        "ln_b": nrm((L, R), 0.01),
        "pool_w": nrm((L, N_POOL_GROUPS, POOL_GROUP, POOL_GROUP), POOL_GROUP ** -0.5),
        "pool_scale": 1.0 + nrm((L, P), 0.05),
        "w_branch": nrm((L, N_BRANCH, R, D), R ** -0.5),
        "w_out": nrm((L, D, D), D ** -0.5),
        "w_ple": nrm((L, PLE_DIM, D), PLE_DIM ** -0.5),
        "w_ple_gate": nrm((L, D, D), D ** -0.5),
    }

def reference(x_prompt, x_sample, state_wkv, state_shift, state_pool, p_prompt, p_sample,
              norm_pre, norm_post, w_in, mu_rkv, mu_lora, w0, w1, w2, a0, a1, a2, v0, v1, v2,
              k_k, k_a, r_k, ln_w, ln_b, pool_w, pool_scale, w_branch, w_out, w_ple, w_ple_gate):
    def layer_weights(i):
        return dict(
            norm_pre=norm_pre[i], norm_post=norm_post[i], w_in=w_in[i], mu_rkv=mu_rkv[i],
            mu_lora=mu_lora[i], w0=w0[i], w1=w1[i], w2=w2[i], a0=a0[i], a1=a1[i], a2=a2[i],
            v0=v0[i - 1] if i > 0 else None, v1=v1[i - 1] if i > 0 else None,
            v2=v2[i - 1] if i > 0 else None,
            k_k=k_k[i], k_a=k_a[i], r_k=r_k[i], ln_w=ln_w[i], ln_b=ln_b[i],
            pool_w=pool_w[i], pool_scale=pool_scale[i], w_branch=w_branch[i], w_out=w_out[i],
            w_ple=w_ple[i], w_ple_gate=w_ple_gate[i])

    def run_group(x, p, wkv, shift, pool, n_past):
        v_first = None
        wkv_out, shift_out, pool_out = [], [], []
        for i in range(DEPTH):
            x, v_first, S, h_last, pool_new = _hybrid_layer(
                x, p[i], wkv[i], shift[i], pool[i], n_past, v_first, layer_weights(i))
            wkv_out.append(S); shift_out.append(h_last); pool_out.append(pool_new)
        return x, jnp.stack(wkv_out), jnp.stack(shift_out), jnp.stack(pool_out)

    dt = x_prompt.dtype
    zeros_wkv = jnp.zeros((DEPTH, BATCH, N_HEADS, HEAD_DIM, HEAD_DIM), dt)
    zeros_shift = jnp.zeros((DEPTH, BATCH, D_MODEL), dt)
    zeros_pool = jnp.zeros((DEPTH, BATCH, POOL_BUF, POOL_WIDTH), dt)
    y_prompt, wkv_p, shift_p, pool_p = run_group(x_prompt, p_prompt, zeros_wkv, zeros_shift, zeros_pool, 0)
    y_sample, wkv_s, shift_s, pool_s = run_group(x_sample, p_sample, state_wkv, state_shift, state_pool, PAST_LEN)
    return (y_prompt, y_sample, wkv_p, shift_p, pool_p, wkv_s, shift_s, pool_s)


_drawn_inputs = setup_inputs


def setup_inputs(seed=0):
    import zlib

    import numpy as np

    out = dict(_drawn_inputs(seed))
    spreads = {}
    factors = {'k_k': 19.081, 'ln_b': 21.841, 'pool_scale': 2.856, 'ln_w': 4.417}
    for name, (base, spread) in spreads.items():
        noise = np.random.default_rng([zlib.crc32(name.encode()), seed]).standard_normal(out[name].shape)
        drawn = base * np.exp(spread * noise) if base else spread * noise
        out[name] = __import__('jax').numpy.asarray(drawn.astype(out[name].dtype))
    for name, factor in factors.items():
        out[name] = (out[name] * factor).astype(out[name].dtype)
    return out
```

```python
from contextlib import ExitStack

import numpy as np
import concourse.bass as bass
from concourse import mybir

F32 = mybir.dt.float32
F32R = mybir.dt.float32r
BF16 = mybir.dt.bfloat16
ALU = mybir.AluOpType
ACT = mybir.ActivationFunctionType
ds = bass.ds

P = 128
D = 2048
KT = D // P
R = 1024
PAIRS = R // P
HD = 64
TP = 256
NB = 8
TB = 8
T = TP + NB * TB
TS = T + NB
C = 64
G = T // C
GP = TP // C
RANK = 96
PLE = 256
BUF = 15
WINDOWS = (2, 4, 8, 16)
PGROUP = R // len(WINDOWS)
DECAY = 0.606531
RMS_EPS = 1e-6
GN_EPS = 64e-5
LEVELS = 5

KC = 8
SLOTS = 4
AHEAD = 3
CH_PAIR = 8
CH_POOL = 4
CH_MERGE = 6
BASE_POOL = CH_PAIR * PAIRS
BASE_MERGE = BASE_POOL + 2 * 2 * (R // P)
BASE_OUT = BASE_MERGE + CH_MERGE * KT
BASE_GATE = BASE_OUT + 2 * KT
CHUNKS = BASE_GATE + 2 * KT

COL_R, COL_K, COL_V, COL_G = 0, R, 2 * R, 3 * R
COL_U, COL_GP, COL_GA, COL_GB = 4 * R, 5 * R, 6 * R, 6 * R + D

MU_R, MU_K, MU_V, W0, A0, K_K, K_A, R_K, LN_W, LN_B, OM_R, OM_K, OM_V, OM_KA = range(14)
NPAR, NROW = 14, 10
NPRE, NPOST, MUW, MUA, PSC = 0, 16, 32, 48, 64
NPAR2 = 72

EXT = BUF + TP + NB * (BUF + TB)

CF = {}
CM = {}


def _columns(table, *widths):
    at = 0
    for name, width in widths:
        table[name] = (at, at + width)
        at += width
    return at


N_CF = _columns(CF, ("ident", P), ("istk", HD), ("ones2", P), ("mean2", P), ("meand", P), ("segment", T),
                ("batch", NB), ("eps", 2), ("count", 4 * 16))
N_CM = _columns(CM, ("pairs", T), ("incl", T), ("strict", 2 * T), ("lower", 2 * T), ("level", LEVELS * T))


def shape_constants():
    f = np.zeros((P, N_CF), np.float32)
    p = np.arange(P)
    head, row = p // HD, p % HD

    def put(table, arr, name, value):
        a, b = table[name]
        arr[:, a:b] = value.reshape(P, b - a)

    put(CF, f, "ident", np.eye(P))
    put(CF, f, "istk", (row[:, None] == np.arange(HD)[None]))
    same = head[:, None] == head[None]
    put(CF, f, "ones2", same * 1.0)
    put(CF, f, "mean2", same / HD)
    put(CF, f, "meand", np.full((P, P), 1.0 / D))
    tok = np.arange(T)
    first = np.where(tok < TP, tok % C == 0, tok % TB == 0)
    put(CF, f, "segment", np.broadcast_to(1.0 - first, (P, T)))
    put(CF, f, "batch", (row // TB)[:, None] == np.arange(NB)[None])
    put(CF, f, "eps", np.broadcast_to(np.array([RMS_EPS, GN_EPS]), (P, 2)))
    put(CF, f, "count", np.broadcast_to(np.array([[1.0 / min(t + 1, w) for t in range(16)] for w in WINDOWS]), (P, 4, 16)))

    m = np.zeros((P, N_CM), np.float32)
    s, t = row[:, None, None], np.arange(C)[None, None, :]
    g = np.arange(G)[None, :, None]
    seq = (g < GP) | (s // TB == t // TB)
    put(CM, m, "incl", (s <= t) & seq)

    def level(b):
        inside = (s // (2 * b) == t // (2 * b)) & ((s // b) % 2 == 0) & ((t // b) % 2 == 1)
        return inside & ((g < GP) | (2 * b <= TB))

    put(CM, m, "pairs", level(1))
    a = CM["level"][0]
    for n in range(LEVELS):
        m[:, a + n * T:a + (n + 1) * T] = level(2 ** (n + 1)).reshape(P, T)

    def diagonal(x):
        x = np.broadcast_to(x, (P, G, C))[:, :, None, :] & (head[:, None, None, None] == np.arange(2)[None, None, :, None])
        return x

    put(CM, m, "strict", diagonal((s < t) & seq))
    put(CM, m, "lower", diagonal((s > t) & seq))
    return f, m


def build(nc, x_prompt, x_sample, state_wkv, state_shift, state_pool, p_prompt, p_sample, norm_pre, norm_post,
          w_in, mu_rkv, mu_lora, w0, w1, w2, a0, a1, a2, k_k, k_a, r_k, ln_w, ln_b, pool_w, pool_scale,
          w_branch, w_out, w_ple, w_ple_gate, const_f, const_m,
          y_prompt, y_sample, wkv_prompt, shift_prompt, pool_prompt, wkv_sample, shift_sample, pool_sample):
    with ExitStack() as ctx:
        base = (nc.sbuf_base + 31) // 32 * 32
        used = {}

        def at(word, name, shape, dt=F32):
            size = int(np.prod(shape[1:])) * (2 if dt == BF16 else 4)
            used[name] = (word, word + (size + 3) // 4)
            return nc.alloc_sbuf_tensor_at(name, list(shape), dt, offset=base + 4 * word)

        class Region:
            def __init__(self, start):
                self.next = start

            def take(self, name, shape, dt=F32):
                t = at(self.next, name, shape, dt)
                self.next = (used[name][1] + 7) // 8 * 8
                return t

        fixed = Region(0)
        cf = fixed.take("cf", [P, N_CF])
        cm = fixed.take("cm", [P, N_CM], BF16)
        par = fixed.take("par", [P, NPAR * PAIRS])
        par2 = fixed.take("par2", [P, NPAR2])
        hh = fixed.take("hh", [P, KT * TS], F32R)
        hl = fixed.take("hl", [P, KT * TS], F32R)
        wraw = fixed.take("wraw", [P, SLOTS, KC * P])
        wh = fixed.take("wh", [P, SLOTS, KC * P], F32R)
        wl = fixed.take("wl", [P, SLOTS, KC * P], F32R)
        ya_start = fixed.next
        yah = fixed.take("yah", [P, PAIRS * T], F32R)
        yal = fixed.take("yal", [P, PAIRS * T], F32R)
        t1 = fixed.take("t1", [RANK, T])
        la = fixed.take("la", [RANK, T])
        arena = fixed.next

        r1 = Region(arena)
        zsh = r1.take("zsh", [P, T])
        kS = r1.take("kS", [P, T])
        rS = r1.take("rS", [P, T])
        vS = r1.take("vS", [P, T])
        gS = r1.take("gS", [P, T])
        cur_p = r1.take("cur_p", [P, NPAR])
        cur_m = r1.take("cur_m", [P, NPAR])
        lw2 = r1.take("lw2", [RANK, P])
        la2 = r1.take("la2", [RANK, P])
        start_overlay = r1.next
        r0 = Region(start_overlay)
        xt = r0.take("xt", [P, 3, D])
        dh = at(used["xt"][0], "dh", [P, KT * T])
        ht = r0.take("ht", [P, 2, D])
        xw = at(used["ht"][0], "xw", [P, 4, T])
        hT = r0.take("hT", [P, KT * TS])
        rows = r0.take("rows", [P, 2, P])
        stat = r0.take("stat", [P, 4])
        hlast = r0.take("hlast", [P, 2 * 72])
        hlastT = r0.take("hlastT", [72, 2 * P])
        lw1 = at(ya_start, "lw1", [P, KT, RANK])
        la1 = at(used["lw1"][1], "la1", [P, KT, RANK])
        aBD = r1.take("aBD", [P, G, 2, C])
        bBD = r1.take("bBD", [P, G, 2, C])
        kBD = r1.take("kBD", [P, G, 2, C])
        vBD = r1.take("vBD", [P, G, 2, C])
        ABD = r1.take("ABD", [P, G, 2, C])
        AKBD = r1.take("AKBD", [P, G, 2, C])
        YBD = r1.take("YBD", [P, G, 2, C])
        BtBD = r1.take("BtBD", [P, G, 2, C])
        KtBD = r1.take("KtBD", [P, G, 2, C])
        VtBD = r1.take("VtBD", [P, G, 2, C])
        ZaBD = r1.take("ZaBD", [P, 2, C])
        EndBD = r1.take("EndBD", [P, 2, C])
        S0n = r1.take("S0n", [P, NB, P])
        UBD, SBD, XBD = bBD, kBD, vBD
        S0T = r1.take("S0T", [P, NB, P])
        sq = r1.take("sq", [P, T])
        pm = r1.take("pm", [P, T])
        aS = r1.take("aS", [P, T])
        sg = r1.take("sg", [P, T])
        cl = r1.take("cl", [P, T])
        rn = r1.take("rn", [P, T])
        pd = r1.take("pd", [P, T])
        pi = r1.take("pi", [P, T])
        kf = r1.take("kf", [P, T])
        bv = r1.take("bv", [P, T])
        kkn = r1.take("kkn", [P, T])
        bU = r1.take("bU", [P, T])
        ar = r1.take("ar", [P, 2, T])
        Y = r1.take("Y", [P, G, C])
        Tm = r1.take("Tm", [P, G, C])
        ARB = r1.take("ARB", [P, G, C])
        ARK = r1.take("ARK", [P, G, C])
        Vs = r1.take("Vs", [P, G, C])
        Us = r1.take("Us", [P, G, C])
        Ss = r1.take("Ss", [P, G, C])
        Sd = r1.take("Sd", [P, C])
        RHS = r1.take("RHS", [P, 2, C])
        Zs = r1.take("Zs", [P, 2, C])
        tail4 = r1.take("tail4", [P, 2, 2, C])
        tails = r1.take("tails", [P, 2, C])
        xpB = r1.take("xpB", [P, NB, C])
        xpK = r1.take("xpK", [P, NB, C])
        dPL = r1.take("dPL", [P, NB, C])
        so = at(used["xpB"][0], "so", [P, NB, C])
        eo = r1.take("eo", [P, P])
        O_s, dO, dsq, sd, yv = cl, pd, pi, kf, kkn
        r2 = Region(arena)
        ybh = r2.take("ybh", [P, 8 * T], F32R)
        ybl = r2.take("ybl", [P, 8 * T], F32R)
        ue = r2.take("ue", [P, 8, EXT])
        win_a = r2.take("win_a", [P, 8, EXT])
        win_b = r2.take("win_b", [P, 6, EXT])
        gp = r2.take("gp", [P, 8, T])
        uS = r2.take("uS", [P, 8, T])
        utok = r2.take("utok", [NB * TB + BUF, R])
        spt = at(used["win_b"][0], "spt", [NB * BUF, R])
        pw = at(used["ue"][0], "pw", [P, 8, PGROUP])
        sgp = at(used["win_a"][0], "sgp", [P, T])
        head = r2.take("head", [P, 8, 16])
        ytmp = at(used["t1"][0], "ytmp", [P, 2, T])
        r3 = Region(used["ybl"][1])
        mh = r3.take("mh", [P, KT * T], F32R)
        ml = r3.take("ml", [P, KT * T], F32R)
        ga = r3.take("ga", [P, 2, T])
        gb = r3.take("gb", [P, 2, T])
        mm_ = at(used["t1"][0], "mm", [P, 2, T])
        o2 = at(arena, "o2", [P, KT * T])
        sacc = r3.take("sacc", [P, T])
        sqo = r3.take("sqo", [P, 2, T])
        pT = r3.take("pT", [P, 2, T])
        wple = r3.take("wple", [P, 2, 2 * P])
        yo = r3.take("yo", [P, 2, T])
        g3 = ga
        ytk = at(used["mh"][0], "ytk", [P, 2, 3 * P])
        xT = at(ya_start, "xT", [P, KT * T])
        xt2 = at(used["hh"][0], "xt2", [P, 3, D])
        pt = at(used["xt2"][1], "pt", [P, 3, PLE])
        x1h = at(used["hh"][0], "x1h", [P, KT * T], F32R)
        x1l = at(used["hl"][0], "x1l", [P, KT * T], F32R)
        end = max(b for _, b in used.values())
        room = (nc.sbuf_usable_end if not callable(nc.sbuf_usable_end) else nc.sbuf_usable_end())
        assert base + 4 * end <= room, (base + 4 * end, room)
        assert used["pt"][1] <= used["hl"][1] and used["la1"][1] <= used["yal"][1]
        assert used["o2"][1] <= used["mh"][0] and used["spt"][1] <= used["win_b"][1]

        acc = [ctx.enter_context(nc.psum_tensor(f"acc{i}", [P, 512], F32)) for i in range(2)]
        B01, B23, B45 = [ctx.enter_context(nc.psum_tensor(f"wide{i}", [P, 1024], F32)) for i in range(3)]
        B = [w[:, 512 * i:512 * (i + 1)] for w in (B01, B23, B45) for i in range(2)]

        sems = {}
        for name in """y_out0 y_out1 wple_in0 wple_in1 lo_ready x_in0 x_in1 x_in2 eout sout const_in rows_in map_in zeroed
            last_done rows_out cur_p_ready lw2_in s0_in par_done xw_ready xw_used cur_m_ready acc_free vbd_ready
            a_ready kf_ready sg_ready sgs_ready exp_ready api_ready kbd_ready bbd_ready tail_ready dpl_ready
            tails_ready xpk_ready end_ready send_ready lora2_ps s0_ps yal_ready pool_in win utok_ev chunk_used x2_in
            xT_ready x1a x1b ytk_ready ple_ps hi_ready zsh_ready hT_ps x_stat hT_done hh_done dh_done last_ps lora_act
            s0t_ready ksq_ready decay_in kk_max kk_norm cum_ready cumx_ready ah_ready bh_ready z_ps zabd_ready vt_ps
            vs_ready bt_ps bt_ready y_ready ybd_ready x_ps x_ready kt_ps kt_ready tail_ps s_ready sd_ready endbd_ready
            sbd_ready ubd_ready end_ps o_ps o_ready send_ps dev_ready dsq_ready var_ps sd_done y_done yah_ready sil
            psg yb_done utok_ps sb_ready m_ready mh_ready so_ready xT_ps pT_ps pT_ready sacc_ready ssq_ps srt
            x1h_ready g3_ready yt_ps par_ready chain h_rows h_split kk_ps kk_rn rk_ready kkn_ready rh_ready rk_ps
            bv_ready score_ps y_init akbd_ready arb_ready ark_ready t_ps t_ready m_ps rhs_ps rhs_ready u_ps u_ready
            s_ps xpb_ready mean_ps mixed pyb_ps ybl_ready mb_ready ml_ready o2_ready x1l_ready g3m yo_ready raw0 raw1
            raw2 raw3 norm_step waits""".split():
            sems[name] = ctx.enter_context(nc.semaphore(name))
        s = sems

        def cfs(name):
            a, b = CF[name]
            return cf[:, a:b]

        def cms(name):
            a, b = CM[name]
            return cm[:, a:b]

        ident, istk, ones2, mean2, meand = [cfs(n) for n in ("ident", "istk", "ones2", "mean2", "meand")]

        def half(q):
            return slice(HD * q, HD * q + HD)

        def grp(t):
            return t[:, :].rearrange("p (g c) -> p g c", g=G)

        def flat(t, g):
            return t[:, g].rearrange("p h c -> p (h c)")

        def tok(g):
            return slice(C * g, C * g + C)

        w_in_v = w_in[0].rearrange("(k p) n -> p k n", p=P)
        wa_v = w_branch[0, 0].rearrange("(k p) n -> p k n", p=P)
        wb_v = w_branch[0, 1].rearrange("(k p) n -> p k n", p=P)
        wo_v = w_out[0].rearrange("(k p) n -> p k n", p=P)
        wg_v = w_ple_gate[0].rearrange("(k p) n -> p k n", p=P)
        wple_v = w_ple[0].rearrange("(k p) n -> p k n", p=P)

        block = ctx.enter_context(nc.Block())

        @block.sync
        def _(sp):
            def load(view, k0, col, count, j, free=True):
                slot = j % SLOTS
                if free:
                    sp.wait_ge(s["lo_ready"], count + j - (SLOTS - 1))
                    sp.sem_inc(s["waits"], 1)
                sp.dma_start(wraw[:, slot, :].rearrange("p (k n) -> p k n", k=KC),
                             view[:, k0:k0 + KC, ds(col, P)]).then_inc(s[f"raw{slot}"], 16)

            def load_pair(q, count, first=False):
                for n, col in enumerate((COL_K, COL_R, COL_V, COL_G)):
                    for h in range(2):
                        j = 2 * n + h
                        load(w_in_v, KC * h, q * P + col, count, j, free=not (first and j < SLOTS))

            sp.dma_start(xt[:, 0, :], x_prompt[0, 0:P, :]).then_inc(s["x_in0"], 16)
            sp.dma_start(xt[:, 1, :], x_prompt[0, P:TP, :]).then_inc(s["x_in1"], 16)
            sp.dma_start(xt[0:NB * TB, 2, :], x_sample.rearrange("b t d -> (b t) d")).then_inc(s["x_in2"], 16)
            sp.dma_start(xt[NB * TB:NB * TB + NB, 2, :], state_shift[0]).then_inc(s["x_in2"], 16)
            load_pair(0, 0, first=True)
            with sp.Fori(1, PAIRS) as q:
                load_pair(q, q * CH_PAIR)
            with sp.Fori(0, 8) as n:
                for t, col in enumerate((COL_U, COL_GP)):
                    for h in range(2):
                        load(w_in_v, KC * h, n * P + col, n * CH_POOL + BASE_POOL, 2 * t + h)
            with sp.Fori(0, KT // 2) as n:
                for m in range(2):
                    for j, (view, k0, col) in enumerate(((w_in_v, 0, COL_GA), (w_in_v, KC, COL_GA), (w_in_v, 0, COL_GB),
                                                         (w_in_v, KC, COL_GB), (wa_v, 0, 0), (wb_v, 0, 0))):
                        load(view, k0, n * (2 * P) + (m * P + col), n * (2 * CH_MERGE) + BASE_MERGE, CH_MERGE * m + j)
            for view, start in ((wo_v, BASE_OUT), (wg_v, BASE_GATE)):
                with sp.Fori(0, KT // 2) as n:
                    for m in range(2):
                        for h in range(2):
                            load(view, KC * h, n * (2 * P) + m * P, n * 4 + start, 2 * m + h)

        @block.gpsimd
        def _(pool):
            gp_ = nc.gpsimd

            def wait_alone(name, value):
                pool.wait_ge(s[name], value)
                pool.sem_inc(s["waits"], 1)

            pool.dma_start(cf[:, :], const_f).then_inc(s["const_in"], 16)
            pool.dma_start(cm[:, :], const_m).then_inc(s["const_in"], 16)
            rv = [mu_rkv[0].rearrange("a (q p) -> (a q) p", p=P)] + [
                v[0].rearrange("(q p) -> q p", p=P) for v in (w0, a0, k_k, k_a, r_k, ln_w, ln_b)]
            row = 0
            for v in rv:
                n = v.shape[0]
                pool.dma_start(rows[row:row + n, 0, :], v).then_inc(s["rows_in"], 16)
                row += n
            row = 0
            for v in (norm_pre[0].rearrange("(q p) -> q p", p=P), norm_post[0].rearrange("(q p) -> q p", p=P),
                      mu_lora[0].rearrange("a (q p) -> (a q) p", p=P)[0:32, :], pool_scale[0].rearrange("(q p) -> q p", p=P)):
                n = v.shape[0]
                pool.dma_start(rows[row:row + n, 1, :], v).then_inc(s["rows_in"], 16)
                row += n
            pool.dma_start(lw1[:, :, :], w1[0].rearrange("(k p) n -> p k n", p=P)).then_inc(s["map_in"], 16)
            pool.dma_start(la1[:, :, :], a1[0].rearrange("(k p) n -> p k n", p=P)).then_inc(s["map_in"], 16)
            gp_.memset(zsh[:, 0:1], 0.0).then_inc(s["zeroed"], 1)
            pool.wait_ge(s["last_done"], 2)
            for n in range(2):
                src = hlastT[:, P * n:P * (n + 1)]
                pool.dma_start(shift_prompt[0, 0].rearrange("(k p) -> k p", p=P)[8 * n:8 * n + 8, :],
                               src[0:8, :]).then_inc(s["rows_out"], 16)
                for k in range(8):
                    pool.dma_start(shift_sample[0, :, P * (8 * n + k):P * (8 * n + k + 1)],
                                   src[8 + NB * k:8 + NB * (k + 1), :]).then_inc(s["rows_out"], 16)

            def pair_params(q):
                gp_.tensor_copy(cur_p[:, :], par[:, :].rearrange("p (n q) -> p n q", q=PAIRS)[:, :, ds(q, 1)]
                                .rearrange("p n q -> p (n q)")).then_inc(s["cur_p_ready"], 1)

            def pair_loads(q):
                pool.dma_start(lw2[:, :], w2[0][:, ds(q * P, P)]).then_inc(s["lw2_in"], 16)
                pool.dma_start(la2[:, :], a2[0][:, ds(q * P, P)]).then_inc(s["lw2_in"], 16)
                for h in range(2):
                    pool.dma_start(S0n[half(h), :, half(h)],
                                   state_wkv[0].rearrange("b h i j -> i b h j")[:, :, ds(q * 2 + h, 1), :]
                                   .rearrange("i b h j -> i b (h j)")).then_inc(s["s0_in"], 16)

            pool.wait_ge(s["par_done"], 4)
            pair_params(0)
            pool.wait_ge(s["xw_ready"], 2 * KT)
            pool.wait_ge(s["xw_used"], 2 * KT)
            blocks = (S0n, aBD, bBD, kBD, vBD, ABD, AKBD, YBD, BtBD, KtBD, VtBD, ZaBD, EndBD)
            for t in blocks:
                gp_.memset(t[:], 0.0).then_inc(s["zeroed"], 1)
            pool.wait_ge(s["zeroed"], 1 + len(blocks))
            pair_loads(0)

            def mix(r):
                gp_.tensor_copy(cur_m[:, :], par[:, :].rearrange("p (n q) -> p n q", q=PAIRS)[:, :, ds(r, 1)]
                                .rearrange("p n q -> p (n q)")).then_inc(s["cur_m_ready"], 1)
                wait_alone("cur_m_ready", r + 1)
                wait_alone("acc_free", r * 4 + 4)
                for h in range(2):
                    gp_.tensor_copy(vBD[half(h), :, h, :], grp(vS)[half(h)]).then_inc(s["vbd_ready"], 1)
                wait_alone("vbd_ready", r * 2 + 2)
                wait_alone("a_ready", r + 1)
                gp_.tensor_scalar(kf[:, :], aS[:, :], cur_m[:, K_A:K_A + 1], cur_m[:, OM_KA:OM_KA + 1],
                                  ALU.mult, ALU.add).then_inc(s["kf_ready"], 1)
                wait_alone("kf_ready", r * 2 + 1)
                gp_.tensor_tensor(kf[:, :], kf[:, :], kS[:, :], ALU.mult).then_inc(s["kf_ready"], 1)
                wait_alone("sg_ready", r + 1)
                gp_.tensor_tensor(sg[:, :], sg[:, :], gS[:, :], ALU.mult).then_inc(s["sgs_ready"], 1)
                wait_alone("exp_ready", r * 3 + 3)
                gp_.tensor_tensor(aS[:, :], aS[:, :], pi[:, :], ALU.mult).then_inc(s["api_ready"], 1)
                wait_alone("api_ready", r + 1)
                for h in range(2):
                    gp_.tensor_tensor(kBD[half(h), :, h, :], grp(kf)[half(h)], grp(pi)[half(h)],
                                      ALU.mult).then_inc(s["kbd_ready"], 1)
                wait_alone("kbd_ready", r * 2 + 2)

            def mix_sample(r):
                wait_alone("bbd_ready", r * 2 + 2)
                pl = pd[:, TP:T].rearrange("p (b t) -> p b t", t=TB)[:, :, TB - 1:TB]
                for n, t in enumerate((bBD, kBD)):
                    gp_.tensor_tensor(tail4[:, n].rearrange("p h (b t) -> p h b t", t=TB),
                                      t[:, G - 1].rearrange("p h (b t) -> p h b t", t=TB),
                                      pl.unsqueeze(1).to_broadcast([P, 2, NB, TB]), ALU.mult).then_inc(s["tail_ready"], 1)
                gp_.tensor_tensor(dPL[:, :, :], istk.unsqueeze(1).to_broadcast([P, NB, C]),
                                  pl.to_broadcast([P, NB, C]), ALU.mult).then_inc(s["dpl_ready"], 1)

            def mix_out(r):
                wait_alone("tails_ready", r * 2 + 2)
                bm = cfs("batch").unsqueeze(2).to_broadcast([P, NB, C])
                gp_.tensor_tensor(xpK[:, :, :], tails[:, 1, :].unsqueeze(1).to_broadcast([P, NB, C]), bm,
                                  ALU.mult).then_inc(s["xpk_ready"], 1)
                wait_alone("end_ready", r + 1)
                for h in range(2):
                    pool.dma_start(wkv_prompt[0, 0][ds(r * 2 + h, 1)].rearrange("h i j -> (h i) j"),
                                   eo[half(h), half(h)]).then_inc(s["eout"], 16)
                wait_alone("send_ready", r + 1)
                for h in range(2):
                    pool.dma_start(wkv_sample[0].rearrange("b h i j -> i b h j")[:, :, ds(r * 2 + h, 1), :]
                                   .rearrange("i b h j -> i b (h j)"), so[half(h), :, :]).then_inc(s["sout"], 16)
                wait_alone("eout", r * 32 + 32)
                wait_alone("sout", r * 32 + 32)

            with pool.Fori(1, PAIRS) as q:
                r = q - 1
                wait_alone("acc_free", q * 4)
                pair_params(q)
                mix(r)
                mix_sample(r)
                wait_alone("lora2_ps", q)
                wait_alone("s0_ps", q)
                pair_loads(q)
                mix_out(r)
            pool.wait_ge(s["acc_free"], 4 * PAIRS)
            mix(PAIRS - 1)
            mix_sample(PAIRS - 1)
            mix_out(PAIRS - 1)

            pool.wait_ge(s["yal_ready"], PAIRS)
            gp_.memset(ue[:, :, 0:BUF], 0.0).then_inc(s["zeroed"], 1)
            pool.dma_start(spt[:, :], state_pool[0].rearrange("b t c -> (b t) c")).then_inc(s["pool_in"], 16)
            pool.dma_start(pool_sample[0, :, 0:BUF - TB, :], state_pool[0, :, TB:BUF, :]).then_inc(s["rows_out"], 16)
            pool.wait_ge(s["win"], 1)
            pool.dma_start(pw[:, :, :], pool_w[0].rearrange("g (k p) n -> p (g k) n", p=P)).then_inc(s["map_in"], 16)
            pool.wait_ge(s["utok_ev"], 2)
            pool.dma_start(pool_prompt[0, 0], utok[0:BUF, :]).then_inc(s["rows_out"], 16)
            for b in range(NB):
                pool.dma_start(pool_sample[0, b, BUF - TB:BUF, :],
                               utok[BUF + TB * b:BUF + TB * (b + 1), :]).then_inc(s["rows_out"], 16)
            pool.wait_ge(s["rows_out"], 16 * (18 + 1 + 1 + NB))

            pool.wait_ge(s["chunk_used"], BASE_OUT)
            pool.dma_start(xt2[:, 0, :], x_prompt[0, 0:P, :]).then_inc(s["x2_in"], 16)
            pool.dma_start(xt2[:, 1, :], x_prompt[0, P:TP, :]).then_inc(s["x2_in"], 16)
            pool.dma_start(xt2[0:NB * TB, 2, :], x_sample.rearrange("b t d -> (b t) d")).then_inc(s["x2_in"], 16)
            pool.dma_start(pt[:, 0, :], p_prompt[0, 0, 0:P, :]).then_inc(s["x2_in"], 16)
            pool.dma_start(pt[:, 1, :], p_prompt[0, 0, P:TP, :]).then_inc(s["x2_in"], 16)
            pool.dma_start(pt[0:NB * TB, 2, :], p_sample[0].rearrange("b t d -> (b t) d")).then_inc(s["x2_in"], 16)
            for m in range(2):
                pool.dma_start(wple[:, m, :].rearrange("p (k n) -> p k n", k=2),
                               wple_v[:, :, m * P:(m + 1) * P]).then_inc(s[f"wple_in{m}"], 16)
            for k in range(KT):
                pool.wait_ge(s["xT_ready"], k + 1)
                pool.wait_ge(s["x1a"], k + 1)
                gp_.tensor_tensor(xT[:, T * k:T * (k + 1)], xT[:, T * k:T * (k + 1)], o2[:, T * k:T * (k + 1)],
                                  ALU.add).then_inc(s["x1b"], 1)

            def store(n, m):
                wait_alone("ytk_ready", n * 4 + 2 * m + 2)
                col = n * (2 * P) + m * P
                pool.dma_start(y_prompt[0].rearrange("(a p) d -> p a d", p=P)[:, :, ds(col, P)],
                               ytk[:, m, 0:2 * P].rearrange("p (a n) -> p a n", a=2)).then_inc(s[f"y_out{m}"], 16)
                pool.dma_start(y_sample.rearrange("b t d -> (b t) d")[:, ds(col, P)],
                               ytk[0:NB * TB, m, 2 * P:3 * P]).then_inc(s[f"y_out{m}"], 16)

            with pool.Fori(0, KT // 2 - 1) as n:
                for m in range(2):
                    wait_alone("ple_ps", n * 2 + m + 1)
                    pool.dma_start(wple[:, m, :].rearrange("p (k n) -> p k n", k=2),
                                   wple_v[:, :, ds(n * (2 * P) + (m + 2) * P, P)]).then_inc(s[f"wple_in{m}"], 16)
                    store(n, m)
            for m in range(2):
                store(KT // 2 - 1, m)
            pool.wait_ge(s["y_out0"], 16 * KT)
            pool.wait_ge(s["y_out1"], 16 * KT)

        @block.scalar
        def _(act):
            A = nc.scalar

            def split_hi(count, j, rounds):
                slot = j % SLOTS
                act.wait_ge(s[f"raw{slot}"], rounds * 16 + 16)
                if not (isinstance(count, int) and count + j < SLOTS):
                    act.wait_ge(s["chunk_used"], count + j - (SLOTS - 1))
                A.copy(wh[:, slot, :], wraw[:, slot, :]).then_inc(s["hi_ready"], 1)

            def ahead(count, rounds, j):
                jj = j + AHEAD
                split_hi(count, jj, rounds + jj // SLOTS)

            def evac_mixed(mu, bank, used_chunks, last):
                act.wait_ge(s["chunk_used"], used_chunks)
                act.wait_ge(s["acc_free"], last)
                act.wait_ge(s["cur_p_ready"], mu[1])
                m = cur_p[:, mu[0]:mu[0] + 1]
                A.mul(zsh[:, 1:TP], bank[:, 0:TP - 1], m)
                zb = zsh[:, TP:T].rearrange("p (b t) -> p b t", t=TB)
                A.mul(zb[:, :, 1:TB], bank[:, TP:T].rearrange("p (b t) -> p b t", t=TB)[:, :, 0:TB - 1], m)
                A.mul(zb[:, :, 0], bank[:, T:TS], m).then_inc(s["zsh_ready"], 1)

            act.wait_ge(s["const_in"], 32)
            for t in range(3):
                n = P if t < 2 else NB * TB
                act.wait_ge(s[f"x_in{t}"], 16 if t < 2 else 32)
                if t == 2:
                    act.wait_ge(s["hT_ps"], 4)
                A.activation(ht[0:n, t % 2, :], xt[0:n, t, :], ACT.Square, accum_out=stat[0:n, t:t + 1]).then_inc(s["x_stat"], 1)
                act.wait_ge(s["x_stat"], 2 * t + 1)
                A.activation(stat[0:n, t:t + 1], stat[0:n, t:t + 1], ACT.Sqrt, scale=1.0 / D,
                             bias=cfs("eps")[0:n, 0:1]).then_inc(s["x_stat"], 1)
            for t in range(3):
                act.wait_ge(s["hT_done"], 4 * (t + 1) if t < 2 else 16)
                a, b = P * t, min(P * (t + 1), TS)
                if t == 2:
                    b = TS
                A.copy(hh[:, :].rearrange("p (k t) -> p k t", t=TS)[:, :, a:b],
                       hT[:, :].rearrange("p (k t) -> p k t", t=TS)[:, :, a:b]).then_inc(s["hh_done"], 1)
            for j in range(AHEAD):
                split_hi(0, j, 0)
            act.wait_ge(s["dh_done"], 4)
            act.wait_ge(s["last_ps"], 2)
            A.copy(hlastT[:, 0:P], B[4][0:72, 0:P]).then_inc(s["last_done"], 1)
            A.copy(hlastT[:, P:2 * P], B[5][0:72, 0:P]).then_inc(s["last_done"], 1)

            def tile_out(q, n):
                if n < 3:
                    evac_mixed((( MU_K, MU_R, MU_V)[n], q + 1), acc[n % 2], q * CH_PAIR + 2 * n + 2, q * 4 + n)

            for j in range(CH_PAIR):
                ahead(0, 0, j)
                if j % 2 == 1 and j < 7:
                    n = j // 2
                    act.wait_ge(s["chunk_used"], 2 * n + 2)
                    if n:
                        act.wait_ge(s["acc_free"], n)
                    act.wait_ge(s["cur_p_ready"], 1)
                    act.wait_ge(s["zeroed"], 1)
                    m = cur_p[:, (MU_K, MU_R, MU_V)[n]:(MU_K, MU_R, MU_V)[n] + 1]
                    bank = acc[n % 2]
                    A.mul(zsh[:, 1:TP], bank[:, 0:TP - 1], m)
                    zb = zsh[:, TP:T].rearrange("p (b t) -> p b t", t=TB)
                    A.mul(zb[:, :, 1:TB], bank[:, TP:T].rearrange("p (b t) -> p b t", t=TB)[:, :, 0:TB - 1], m)
                    A.mul(zb[:, :, 0], bank[:, T:TS], m).then_inc(s["zsh_ready"], 1)
            act.wait_ge(s["xw_used"], 2 * KT)
            A.activation(t1[:, :], B[0][0:RANK, 0:T], ACT.Tanh).then_inc(s["lora_act"], 1)
            A.copy(la[:, :], B[1][0:RANK, 0:T]).then_inc(s["lora_act"], 1)

            def mix(r, q=None):
                def go(j):
                    if q is not None:
                        ahead(q * CH_PAIR, q * (CH_PAIR // SLOTS), j)

                def out(n):
                    if q is not None:
                        tile_out(q, n)

                act.wait_ge(s["s0_ps"], r + 1)
                A.copy(S0T[:, :, :].rearrange("p b c -> p (b c)"), B45[:, :]).then_inc(s["s0t_ready"], 1)
                act.wait_ge(s["cur_m_ready"], r + 1)
                A.activation(sq[:, :], kS[:, :], ACT.Square, scale=cur_m[:, K_K:K_K + 1]).then_inc(s["ksq_ready"], 1)
                act.wait_ge(s["lora2_ps"], r + 1)
                A.activation(pm[:, :], B[0][:, 0:T], ACT.Sigmoid, bias=cur_m[:, W0:W0 + 1]).then_inc(s["decay_in"], 1)
                A.activation(aS[:, :], B[1][:, 0:T], ACT.Sigmoid, bias=cur_m[:, A0:A0 + 1]).then_inc(s["a_ready"], 1)
                A.activation(sg[:, :], gS[:, :], ACT.Sigmoid).then_inc(s["sg_ready"], 1)
                go(0)
                act.wait_ge(s["kk_max"], r + 1)
                A.activation(rn[:, :], rn[:, :], ACT.Sqrt).then_inc(s["kk_norm"], 1)
                act.wait_ge(s["cum_ready"], r + 1)
                A.activation(pi[:, :], cl[:, :], ACT.Exp, scale=DECAY).then_inc(s["exp_ready"], 1)
                A.activation(pd[:, :], cl[:, :], ACT.Exp, scale=-DECAY).then_inc(s["exp_ready"], 1)
                act.wait_ge(s["cumx_ready"], r + 1)
                A.activation(pm[:, :], pm[:, :], ACT.Exp, scale=-DECAY).then_inc(s["exp_ready"], 1)
                go(1)
                act.wait_ge(s["ah_ready"], r + 1)
                for h in range(2):
                    A.copy(aBD[half(h), :, h, :], ar[half(h), 0, :].rearrange("p (g c) -> p g c", g=G))
                act.wait_ge(s["bh_ready"], r + 1)
                for h in range(2):
                    A.copy(bBD[half(h), :, h, :], grp(bU)[half(h)]).then_inc(s["bbd_ready"], 1)
                act.wait_ge(s["z_ps"], r + 1)
                A.copy(Zs[:, :, :].rearrange("p a c -> p (a c)"), B[5][:, 0:2 * C])
                for h in range(2):
                    A.copy(ZaBD[half(h), h, :], B[5][half(h), 0:C]).then_inc(s["zabd_ready"], 1)
                out(0)
                go(2)
                act.wait_ge(s["vt_ps"], r + 1)
                A.copy(VtBD[:, :, :, :].rearrange("p g h c -> p (g h c)"), B23[:, 0:2 * T])
                for h in range(2):
                    A.copy(Vs[half(h)], B23[half(h), 0:2 * T].rearrange("p (g h c) -> p g h c", g=G, h=2)[:, :, h, :]
                           ).then_inc(s["vs_ready"], 1)
                act.wait_ge(s["bt_ps"], r + 1)
                A.copy(BtBD[:, :, :, :].rearrange("p g h c -> p (g h c)"), B45[:, 0:2 * T]).then_inc(s["bt_ready"], 1)

                def ybd(n):
                    act.wait_ge(s["y_ready"], r * (LEVELS + 1) + n + 1)
                    for h in range(2):
                        A.copy(YBD[half(h), :, h, :], Y[half(h)]).then_inc(s["ybd_ready"], 1)

                def xbd(n):
                    act.wait_ge(s["x_ps"], r * LEVELS + n + 1)
                    A.copy(XBD[:, :, :, :].rearrange("p g h c -> p (g h c)"), B45[:, 0:2 * T]).then_inc(s["x_ready"], 1)

                ybd(0)
                go(3)
                xbd(0)
                act.wait_ge(s["kt_ps"], r + 1)
                A.copy(KtBD[:, :, :, :].rearrange("p g h c -> p (g h c)"), B01[:, 0:2 * T]).then_inc(s["kt_ready"], 1)
                for n in range(1, LEVELS):
                    ybd(n)
                    xbd(n)
                    if n == 1:
                        out(1)
                    if n in (2, 4):
                        go(3 + n // 2)
                    
                ybd(LEVELS)
                act.wait_ge(s["tail_ps"], r + 1)
                for h in range(2):
                    A.copy(tails[half(h)], B[5][half(h), 0:4 * C].rearrange("p (n h c) -> p n h c", n=2, h=2)[:, :, h, :]
                           ).then_inc(s["tails_ready"], 1)
                for g in range(GP):
                    if g:
                        act.wait_ge(s["s_ready"], r * GP + g)
                        A.mul(Sd[:, :], Ss[:, g - 1 + 0, :], pd[:, C * g + C - 1:C * g + C]).then_inc(s["sd_ready"], 1)
                    if g == 1:
                        out(2)
                    if g == 1:
                        go(6)
                act.wait_ge(s["s_ready"], r * GP + GP)
                for h in range(2):
                    A.copy(EndBD[half(h), h, :], Ss[half(h), GP - 1, :]).then_inc(s["endbd_ready"], 1)
                for h in range(2):
                    A.copy(SBD[half(h), 0:GP - 1, h, :], Ss[half(h), 0:GP - 1, :]).then_inc(s["sbd_ready"], 1)
                for h in range(2):
                    A.copy(UBD[half(h), :, h, :], Us[half(h)]).then_inc(s["ubd_ready"], 1)
                go(7)
                act.wait_ge(s["end_ps"], r + 1)
                A.copy(eo[:, :], B[0][:, 0:P]).then_inc(s["end_ready"], 1)
                act.wait_ge(s["o_ps"], r + 1)
                A.copy(O_s[:, :], B[4][:, 0:T]).then_inc(s["o_ready"], 1)
                act.wait_ge(s["send_ps"], r + 1)
                A.copy(so[:, :, :].rearrange("p b c -> p (b c)"), B[3][:, :]).then_inc(s["send_ready"], 1)
                act.wait_ge(s["dev_ready"], r + 1)
                A.activation(dsq[:, :], dO[:, :], ACT.Square).then_inc(s["dsq_ready"], 1)
                act.wait_ge(s["var_ps"], r + 1)
                A.activation(sd[:, :], B[1][:, 0:T], ACT.Sqrt, bias=cfs("eps")[:, 1:2]).then_inc(s["sd_done"], 1)
                act.wait_ge(s["y_done"], r + 1)
                A.copy(yah[:, ds(r * T, T)], yv[:, :]).then_inc(s["yah_ready"], 1)

            with act.Fori(1, PAIRS) as q:
                mix(q - 1, q)
            mix(PAIRS - 1)

            def pool_round(n):
                for j in range(CH_POOL):
                    ahead(n * CH_POOL + BASE_POOL, n + BASE_POOL // SLOTS, j)

            with act.Fori(0, 8) as n:
                pool_round(n)
            act.wait_ge(s["mixed"], 4 * len(WINDOWS))
            for g in range(8):
                if g >= 1:
                    act.wait_ge(s["sil"], 2 * g)
                A.activation(sgp[:, :], gp[:, g, :], ACT.Sigmoid).then_inc(s["psg"], 1)
                act.wait_ge(s["sil"], 2 * g + 2)
                A.copy(ybh[:, g * T:(g + 1) * T], ytmp[:, g % 2, :]).then_inc(s["yb_done"], 1)
            for n in range(2):
                act.wait_ge(s["utok_ps"], n + 3)
                A.copy(utok[:, 512 * n:512 * (n + 1)], B[4 + n][0:NB * TB + BUF, :]).then_inc(s["utok_ev"], 1)

            with act.Fori(0, KT // 2) as n:
                for m in range(2):
                    i = n * 2 + m
                    bank = [acc[0], acc[1]] if m == 0 else [B[2], B[3]]
                    for j in range(CH_MERGE):
                        ahead(n * (2 * CH_MERGE) + BASE_MERGE, n * (2 * CH_MERGE // SLOTS) + BASE_MERGE // SLOTS,
                              CH_MERGE * m + j)
                        if j == 2:
                            act.wait_ge(s["chunk_used"], i * CH_MERGE + BASE_MERGE + 2)
                            A.activation(ga[:, m, :], bank[0][:, 0:T], ACT.Sigmoid)
                        if j == 4:
                            act.wait_ge(s["chunk_used"], i * CH_MERGE + BASE_MERGE + 4)
                            A.activation(gb[:, m, :], bank[1][:, 0:T], ACT.Sigmoid).then_inc(s["sb_ready"], 1)
                    act.wait_ge(s["m_ready"], i + 1)
                    A.copy(mh[:, ds(n * (2 * T) + m * T, T)], mm_[:, m, :]).then_inc(s["mh_ready"], 1)

            def square_tile(n, m):
                i = n * 2 + m
                for h in range(2):
                    ahead(n * 4 + BASE_OUT, n + BASE_OUT // SLOTS, 2 * m + h)
                act.wait_ge(s["chunk_used"], i * 2 + (BASE_OUT + 2))
                A.activation(sqo[:, m, :], acc[m][:, 0:T], ACT.Square).then_inc(s["so_ready"], 1)

            for m in range(2):
                square_tile(0, m)
            for k in range(KT):
                act.wait_ge(s["xT_ps"], k + 1)
                A.copy(xT[:, T * k:T * (k + 1)], B[k % 4][:, 0:T]).then_inc(s["xT_ready"], 1)
            for k in range(2):
                act.wait_ge(s["pT_ps"], k + 1)
                A.copy(pT[:, k, :], B[4 + k][:, 0:T]).then_inc(s["pT_ready"], 1)
            with act.Fori(1, KT // 2) as n:
                for m in range(2):
                    act.wait_ge(s["sacc_ready"], n * 2 + m - 1)
                    square_tile(n, m)
            act.wait_ge(s["ssq_ps"], 1)
            A.activation(sacc[:, :], B[5][:, 0:T], ACT.Sqrt, bias=cfs("eps")[:, 0:1]).then_inc(s["srt"], 1)
            for k in range(KT):
                act.wait_ge(s["x1b"], k + 1)
                A.copy(x1h[:, T * k:T * (k + 1)], xT[:, T * k:T * (k + 1)]).then_inc(s["x1h_ready"], 1)

            def gate_tile(n, m, last=False):
                i = n * 2 + m
                for h in range(2):
                    if not last or 2 * m + h + AHEAD < 4:
                        ahead(n * 4 + BASE_GATE, n + BASE_GATE // SLOTS, 2 * m + h)
                act.wait_ge(s["chunk_used"], i * 2 + (BASE_GATE + 2))
                A.activation(g3[:, m, :], acc[m][:, 0:T], ACT.Sigmoid).then_inc(s["g3_ready"], 1)

            def token_tile(i, m, stored=None):
                act.wait_ge(s["yt_ps"], i + 1)
                if stored is not None:
                    act.wait_ge(s[f"y_out{m}"], stored)
                A.copy(ytk[:, m, 0:2 * P], B[2 + m][:, 0:2 * P]).then_inc(s["ytk_ready"], 1)
                A.copy(ytk[0:NB * TB, m, 2 * P:3 * P], B[2 + m][0:NB * TB, 2 * P:3 * P]).then_inc(s["ytk_ready"], 1)

            gate_tile(0, 0)
            gate_tile(0, 1)
            token_tile(0, 0)
            gate_tile(1, 0)
            token_tile(1, 1)
            gate_tile(1, 1)
            token_tile(2, 0, 32)
            with act.Fori(2, KT // 2 - 1) as n:
                gate_tile(n, 0)
                token_tile(n * 2 - 1, 1, n * 32 - 32)
                gate_tile(n, 1)
                token_tile(n * 2, 0, n * 32)
            n = KT // 2 - 1
            gate_tile(n, 0, last=True)
            token_tile(n * 2 - 1, 1, n * 32 - 32)
            gate_tile(n, 1, last=True)
            token_tile(n * 2, 0, n * 32)
            token_tile(n * 2 + 1, 1, n * 32)

        @block.vector
        def _(dve):
            V = nc.vector

            def split_lo(count, j):
                slot = j % SLOTS
                dve.wait_ge(s["hi_ready"], count + j + 1)
                V.tensor_tensor(wl[:, slot, :], wraw[:, slot, :], wh[:, slot, :].bitcast(F32), ALU.subtract
                                ).then_inc(s["lo_ready"], 1)

            def ahead(count, j):
                split_lo(count, j + AHEAD)

            def tile_out(q, n):
                dve.wait_ge(s["chunk_used"], q * CH_PAIR + 2 * n + 2)
                bank = acc[n % 2][:, 0:T]
                if n < 3:
                    dve.wait_ge(s["zsh_ready"], q * 3 + n + 1)
                    V.scalar_tensor_tensor((kS, rS, vS)[n][:, :], bank, cur_p[:, (OM_K, OM_R, OM_V)[n]:(OM_K, OM_R, OM_V)[n] + 1],
                                           zsh[:, :], ALU.mult, ALU.add).then_inc(s["acc_free"], 1)
                else:
                    V.tensor_copy(gS[:, :], bank).then_inc(s["acc_free"], 1)

            dve.wait_ge(s["par_ready"], 2)
            V.tensor_copy(par[:, 0:NROW * PAIRS], B[4][:, 0:NROW * PAIRS]).then_inc(s["par_done"], 1)
            V.tensor_copy(par2[:, :], B[5][:, 0:NPAR2]).then_inc(s["par_done"], 1)
            dve.wait_ge(s["par_done"], 2)
            V.tensor_scalar(par[:, OM_R * PAIRS:(OM_V + 1) * PAIRS], par[:, 0:3 * PAIRS], -1.0, 1.0,
                            ALU.mult, ALU.add).then_inc(s["par_done"], 1)
            V.tensor_scalar(par[:, OM_KA * PAIRS:(OM_KA + 1) * PAIRS], par[:, K_A * PAIRS:(K_A + 1) * PAIRS], -1.0, 1.0,
                            ALU.mult, ALU.add).then_inc(s["par_done"], 1)
            hTv = hT[:, :].rearrange("p (k t) -> p k t", t=TS)
            hhv = hh[:, :].rearrange("p (k t) -> p k t", t=TS)
            hlv = hl[:, :].rearrange("p (k t) -> p k t", t=TS)

            def h_rows(t):
                n = P if t < 2 else NB * TB
                dve.wait_ge(s["x_stat"], 2 * t + 2)
                V.reciprocal(stat[0:n, t:t + 1], stat[0:n, t:t + 1]).then_inc(s["chain"], 1)
                dve.wait_ge(s["chain"], t + 1)
                V.tensor_scalar(ht[0:n, t % 2, :], xt[0:n, t, :], stat[0:n, t:t + 1], None, ALU.mult).then_inc(s["h_rows"], 1)
                if t == 2:
                    V.tensor_copy(ht[n:n + NB, 0, :], xt[n:n + NB, 2, :]).then_inc(s["h_rows"], 1)

            def h_columns(t):
                for c in range(4):
                    dve.wait_ge(s["hT_ps"], 4 * t + c + 1)
                    n = P if t < 2 else NB * TB
                    src = B[c][:, :].rearrange("p (k t) -> p k t", t=P)
                    V.tensor_tensor(hTv[:, 4 * c:4 * c + 4, P * t:P * t + n], src[:, :, 0:n],
                                    par2[:, NPRE + 4 * c:NPRE + 4 * c + 4].unsqueeze(2).to_broadcast([P, 4, n]),
                                    ALU.mult).then_inc(s["hT_done"], 1)
                    if t == 2:
                        V.tensor_copy(hTv[:, 4 * c:4 * c + 4, T:TS], src[:, :, n:n + NB]).then_inc(s["hT_done"], 1)

            h_rows(0)
            h_rows(1)
            dve.wait_ge(s["par_done"], 4)
            h_columns(0)
            h_rows(2)
            h_columns(1)
            h_columns(2)
            for t in range(3):
                a, b = P * t, (P * (t + 1) if t < 2 else TS)
                dve.wait_ge(s["hh_done"], t + 1)
                V.tensor_tensor(hlv[:, :, a:b], hTv[:, :, a:b], hhv[:, :, a:b].bitcast(F32), ALU.subtract).then_inc(s["h_split"], 1)
            for j in range(AHEAD):
                split_lo(0, j)
            dve.wait_ge(s["hT_done"], 16)
            for n in range(2):
                V.tensor_copy(hlast[:, 72 * n:72 * n + 8], hTv[:, 8 * n:8 * n + 8, TP - 1]).then_inc(s["dh_done"], 1)
                V.tensor_copy(hlast[:, 72 * n + 8:72 * n + 72].rearrange("p (k b) -> p k b", b=NB),
                              hTv[:, 8 * n:8 * n + 8, TP + TB - 1:T:TB]).then_inc(s["dh_done"], 1)
            dhv = dh[:, :].rearrange("p (k t) -> p k t", t=T)
            V.tensor_scalar(dhv[:, :, 0:1], hTv[:, :, 0:1], -1.0, None, ALU.mult).then_inc(s["dh_done"], 1)
            V.tensor_tensor(dhv[:, :, 1:TP], hTv[:, :, 0:TP - 1], hTv[:, :, 1:TP], ALU.subtract).then_inc(s["dh_done"], 1)
            for b in range(NB):
                a = TP + TB * b
                V.tensor_tensor(dhv[:, :, a + 1:a + TB], hTv[:, :, a:a + TB - 1], hTv[:, :, a + 1:a + TB],
                                ALU.subtract).then_inc(s["dh_done"], 1)
            V.tensor_tensor(dhv[:, :, TP:T:TB], hTv[:, :, T:TS], hTv[:, :, TP:T:TB], ALU.subtract).then_inc(s["dh_done"], 1)
            dve.wait_ge(s["dh_done"], 4 + NB + 3)
            for j in range(CH_PAIR):
                ahead(0, j)
                for k in (2 * j, 2 * j + 1):
                    for m, mu in enumerate((MUW, MUA)):
                        n = 2 * k + m
                        if n >= 4:
                            dve.wait_ge(s["xw_used"], n - 3)
                        V.scalar_tensor_tensor(xw[:, n % 4, :], dhv[:, k, :], par2[:, mu + k:mu + k + 1], hTv[:, k, 0:T],
                                               ALU.mult, ALU.add).then_inc(s["xw_ready"], 1)
                if j % 2 == 1:
                    tile_out(0, j // 2)

            def mix(r, q=None):
                def go(j):
                    if q is not None:
                        ahead(q * CH_PAIR, j)

                def out(n):
                    if q is not None:
                        tile_out(q, n)

                dve.wait_ge(s["kk_ps"], r + 1)
                V.tensor_scalar(rn[:, :], B[2][:, 0:T], 1e-24, None, ALU.max).then_inc(s["kk_max"], 1)
                dve.wait_ge(s["decay_in"], r + 1)
                V.tensor_tensor_scan(cl[:, :], cfs("segment"), pm[:, :], 0.0, ALU.mult, ALU.add).then_inc(s["cum_ready"], 1)
                dve.wait_ge(s["cum_ready"], r + 1)
                V.tensor_tensor(pm[:, :], cl[:, :], pm[:, :], ALU.subtract).then_inc(s["cumx_ready"], 1)
                go(0)
                dve.wait_ge(s["kk_norm"], r + 1)
                V.reciprocal(rn[:, :], rn[:, :]).then_inc(s["kk_rn"], 1)
                dve.wait_ge(s["cur_m_ready"], r + 1)
                dve.wait_ge(s["kf_ready"], r * 2 + 2)
                V.scalar_tensor_tensor(sq[:, :], rS[:, :], cur_m[:, R_K:R_K + 1], kf[:, :], ALU.mult, ALU.mult
                                       ).then_inc(s["rk_ready"], 1)
                dve.wait_ge(s["kk_rn"], r + 1)
                V.scalar_tensor_tensor(kkn[:, :], kS[:, :], cur_m[:, K_K:K_K + 1], rn[:, :], ALU.mult, ALU.mult
                                       ).then_inc(s["kkn_ready"], 1)
                dve.wait_ge(s["kkn_ready"], r + 1)
                dve.wait_ge(s["exp_ready"], r * 3 + 3)
                V.scalar_tensor_tensor(ar[:, 0, :], kkn[:, :], -1.0, pm[:, :], ALU.mult, ALU.mult).then_inc(s["ah_ready"], 1)
                dve.wait_ge(s["api_ready"], r + 1)
                V.tensor_tensor(bU[:, :], kkn[:, :], aS[:, :], ALU.mult).then_inc(s["bh_ready"], 1)
                V.tensor_tensor(ar[:, 1, :], rS[:, :], pd[:, :], ALU.mult).then_inc(s["rh_ready"], 1)
                dve.wait_ge(s["rk_ps"], r + 1)
                V.tensor_tensor(bv[:, :], B[3][:, 0:T], vS[:, :], ALU.mult).then_inc(s["bv_ready"], 1)
                go(1)
                bd = [P, G, 2, C]
                dve.wait_ge(s["score_ps"], r * 5 + 1)
                V.tensor_tensor(Tm[:, :, :].rearrange("p g c -> p (g c)"), B[0][:, 0:T], cms("pairs"), ALU.mult).then_inc(s["y_init"], 1)
                dve.wait_ge(s["y_init"], r + 1)
                V.tensor_tensor(Y[:, :, :], Tm[:, :, :], istk.unsqueeze(1).to_broadcast([P, G, C]), ALU.add).then_inc(s["y_ready"], 1)
                dve.wait_ge(s["score_ps"], r * 5 + 3)
                V.tensor_tensor(AKBD[:, :, :, :], B[2][:, 0:T].rearrange("p (g c) -> p g c", g=G).unsqueeze(2).to_broadcast(bd),
                                cms("strict").rearrange("p (g h c) -> p g h c", g=G, h=2), ALU.mult).then_inc(s["akbd_ready"], 1)
                dve.wait_ge(s["score_ps"], r * 5 + 4)
                V.tensor_tensor(ARB[:, :, :].rearrange("p g c -> p (g c)"), B[3][:, 0:T], cms("incl"), ALU.mult).then_inc(s["arb_ready"], 1)
                V.tensor_tensor(ABD[:, :, :, :], B[1][:, 0:T].rearrange("p (g c) -> p g c", g=G).unsqueeze(2).to_broadcast(bd),
                                cms("lower").rearrange("p (g h c) -> p g h c", g=G, h=2), ALU.mult)
                dve.wait_ge(s["score_ps"], r * 5 + 5)
                V.tensor_tensor(ARK[:, :, :].rearrange("p g c -> p (g c)"), B[4][:, 0:T], cms("incl"), ALU.mult).then_inc(s["ark_ready"], 1)
                out(0)
                go(2)
                go(3)
                lv = CM["level"][0]
                for n in range(LEVELS):
                    dve.wait_ge(s["t_ps"], r * LEVELS + n + 1)
                    V.tensor_tensor(Tm[:, :, :].rearrange("p g c -> p (g c)"), B[0][:, 0:T],
                                    cm[:, lv + n * T:lv + (n + 1) * T], ALU.mult).then_inc(s["t_ready"], 1)
                    dve.wait_ge(s["m_ps"], r * LEVELS + n + 1)
                    dve.wait_ge(s["ybd_ready"], r * (2 * LEVELS + 2) + 2 * n + 2)
                    V.tensor_tensor(Y[:, :, :].rearrange("p g c -> p (g c)"), B[1][:, 0:T],
                                    Y[:, :, :].rearrange("p g c -> p (g c)"), ALU.add).then_inc(s["y_ready"], 1)
                    if n == 1:
                        out(1)
                    if n in (2, 4):
                        go(3 + n // 2)
                for g in range(GP):
                    dve.wait_ge(s["rhs_ps"], r * GP + g + 1)
                    w = 2 * C if g == 0 else C
                    V.tensor_copy(RHS[:, :, :].rearrange("p a c -> p (a c)")[:, 0:w], B[2][:, 0:w]).then_inc(s["rhs_ready"], 1)
                    dve.wait_ge(s["u_ps"], r * GP + g + 1)
                    if g == 0:
                        V.tensor_copy(Us[:, 0:G:G - 1, :], B[3][:, 0:2 * C].rearrange("p (a c) -> p a c", a=2)).then_inc(s["u_ready"], 1)
                    else:
                        V.tensor_copy(Us[:, g, :], B[3][:, 0:C]).then_inc(s["u_ready"], 1)
                    dve.wait_ge(s["s_ps"], r * GP + g + 1)
                    decay = pd[:, C * g + C - 1:C * g + C]
                    if g == 0:
                        V.tensor_scalar(Ss[:, 0, :], B[0][:, 0:C], decay, None, ALU.mult).then_inc(s["s_ready"], 1)
                    else:
                        dve.wait_ge(s["sd_ready"], r * (GP - 1) + g)
                        V.scalar_tensor_tensor(Ss[:, g, :], B[0][:, 0:C], decay, Sd[:, :], ALU.mult, ALU.add).then_inc(s["s_ready"], 1)
                    if g == 1:
                        out(2)
                        go(6)
                dve.wait_ge(s["tails_ready"], r * 2 + 2)
                V.tensor_tensor(xpB[:, :, :], tails[:, 0, :].unsqueeze(1).to_broadcast([P, NB, C]),
                                cfs("batch").unsqueeze(2).to_broadcast([P, NB, C]), ALU.mult).then_inc(s["xpb_ready"], 1)
                go(7)
                dve.wait_ge(s["mean_ps"], r + 1)
                V.tensor_tensor(dO[:, :], O_s[:, :], B[5][:, 0:T], ALU.subtract).then_inc(s["dev_ready"], 1)
                dve.wait_ge(s["sd_done"], r + 1)
                V.reciprocal(sd[:, :], sd[:, :]).then_inc(s["norm_step"], 1)
                dve.wait_ge(s["norm_step"], r * 3 + 1)
                V.scalar_tensor_tensor(dO[:, :], dO[:, :], cur_m[:, LN_W:LN_W + 1], sd[:, :], ALU.mult, ALU.mult).then_inc(s["norm_step"], 1)
                dve.wait_ge(s["norm_step"], r * 3 + 2)
                V.scalar_tensor_tensor(dO[:, :], dO[:, :], cur_m[:, LN_B:LN_B + 1], bv[:, :], ALU.add, ALU.add).then_inc(s["norm_step"], 1)
                dve.wait_ge(s["norm_step"], r * 3 + 3)
                dve.wait_ge(s["sgs_ready"], r + 1)
                V.tensor_tensor(yv[:, :], dO[:, :], sg[:, :], ALU.mult).then_inc(s["y_done"], 1)
                dve.wait_ge(s["yah_ready"], r + 1)
                V.tensor_tensor(yal[:, ds(r * T, T)], yv[:, :], yah[:, ds(r * T, T)].bitcast(F32), ALU.subtract).then_inc(s["yal_ready"], 1)
                if q is not None:
                    tile_out(q, 3)

            with dve.Fori(1, PAIRS) as q:
                mix(q - 1, q)
            mix(PAIRS - 1)

            dve.wait_ge(s["zeroed"], 15)
            for c in range(2):
                dve.wait_ge(s["utok_ps"], c + 1)
                for k in range(4):
                    V.tensor_copy(ue[:, 4 * c + k, BUF + TP:EXT].rearrange("p (b t) -> p b t", b=NB)[:, :, 0:BUF],
                                  B[c][:, NB * BUF * k:NB * BUF * (k + 1)].rearrange("p (b t) -> p b t", b=NB)
                                  )
            uef = ue[:, :, :].rearrange("p k e -> p (k e)")
            uSf = uS[:, :, :].rearrange("p k t -> p (k t)")
            with dve.Fori(0, 8) as n:
                for j in range(CH_POOL):
                    ahead(n * CH_POOL + BASE_POOL, j)
                    if j == 1:
                        dve.wait_ge(s["chunk_used"], n * CH_POOL + (BASE_POOL + 2))
                        V.tensor_copy(uSf[:, ds(n * T, T)], acc[0][:, 0:T])
                        V.tensor_copy(uef[:, ds(n * EXT + BUF, TP)], acc[0][:, 0:TP])
                        V.tensor_copy(uef[:, ds(n * EXT + (BUF + TP), NB * (BUF + TB))]
                                      .rearrange("p (b t) -> p b t", b=NB)[:, :, BUF:BUF + TB],
                                      acc[0][:, TP:T].rearrange("p (b t) -> p b t", b=NB)).then_inc(s["acc_free"], 1)
                dve.wait_ge(s["chunk_used"], n * CH_POOL + (BASE_POOL + 4))
                V.tensor_copy(gp[:, :, :].rearrange("p k t -> p (k t)")[:, ds(n * T, T)], acc[1][:, 0:T]).then_inc(s["acc_free"], 1)
            dve.wait_ge(s["acc_free"], 4 * PAIRS + 16)
            E = EXT
            V.tensor_tensor(win_a[:, :, 1:E], ue[:, :, 1:E], ue[:, :, 0:E - 1], ALU.add).then_inc(s["win"], 1)
            dve.wait_ge(s["win"], 1)
            V.tensor_tensor(win_b[:, :, 3:E], win_a[:, 2:8, 3:E], win_a[:, 2:8, 1:E - 2], ALU.add).then_inc(s["win"], 1)
            dve.wait_ge(s["win"], 2)
            V.tensor_tensor(win_a[:, 4:8, 7:E], win_b[:, 2:6, 7:E], win_b[:, 2:6, 3:E - 4], ALU.add).then_inc(s["win"], 1)
            dve.wait_ge(s["win"], 3)
            V.tensor_tensor(win_b[:, 4:6, 15:E], win_a[:, 6:8, 15:E], win_a[:, 6:8, 7:E - 8], ALU.add).then_inc(s["win"], 1)
            dve.wait_ge(s["win"], 4)
            dve.wait_ge(s["utok_ps"], 4)
            count = cfs("count").rearrange("p (g t) -> p g t", t=16)
            sources = [win_a[:, 0:2, :], win_b[:, 0:2, :], win_a[:, 4:6, :], win_b[:, 4:6, :]]
            for g, w in enumerate(WINDOWS):
                inv = 1.0 / w
                src, u = sources[g], uS[:, 2 * g:2 * g + 2, :]
                V.tensor_tensor(head[:, 2 * g:2 * g + 2, :], src[:, :, BUF:BUF + 16],
                                count[:, g].unsqueeze(1).to_broadcast([P, 2, 16]), ALU.mult).then_inc(s["chain"], 1)
                dve.wait_ge(s["chain"], 4 + g)
                V.tensor_tensor(u[:, :, 0:16], head[:, 2 * g:2 * g + 2, :], u[:, :, 0:16], ALU.subtract).then_inc(s["mixed"], 1)
                V.scalar_tensor_tensor(u[:, :, 16:TP], src[:, :, BUF + 16:BUF + TP], inv, u[:, :, 16:TP],
                                       ALU.mult, ALU.subtract).then_inc(s["mixed"], 1)
                for k in range(2):
                    us = u[:, k, TP:T].rearrange("p (b t) -> p b t", b=NB)
                    V.scalar_tensor_tensor(us, src[:, k, BUF + TP:E].rearrange("p (b t) -> p b t", b=NB)[:, :, BUF:BUF + TB],
                                           inv, us, ALU.mult, ALU.subtract).then_inc(s["mixed"], 1)
            for m in range(8):
                dve.wait_ge(s["pyb_ps"], m + 1)
                if m >= 2:
                    dve.wait_ge(s["ybl_ready"], m - 1)
                V.scalar_tensor_tensor(ytmp[:, m % 2, :], B[m % 4][:, 0:T], par2[:, PSC + m:PSC + m + 1], gp[:, m, :],
                                       ALU.mult, ALU.mult).then_inc(s["sil"], 1)
                dve.wait_ge(s["sil"], 2 * m + 1)
                dve.wait_ge(s["psg"], m + 1)
                V.tensor_tensor(ytmp[:, m % 2, :], ytmp[:, m % 2, :], sgp[:, :], ALU.mult).then_inc(s["sil"], 1)
                dve.wait_ge(s["yb_done"], m + 1)
                V.tensor_tensor(ybl[:, m * T:(m + 1) * T], ytmp[:, m % 2, :], ybh[:, m * T:(m + 1) * T].bitcast(F32),
                                ALU.subtract).then_inc(s["ybl_ready"], 1)

            dve.wait_ge(s["ybl_ready"], 8)
            with dve.Fori(0, KT // 2) as n:
                for m in range(2):
                    i = n * 2 + m
                    banks = (B[0], B[1]) if m == 0 else (B[4], B[5])
                    for j in range(CH_MERGE):
                        ahead(n * (2 * CH_MERGE) + BASE_MERGE, CH_MERGE * m + j)
                    dve.wait_ge(s["chunk_used"], i * CH_MERGE + (BASE_MERGE + 6))
                    dve.wait_ge(s["sb_ready"], i + 1)
                    V.tensor_tensor(ga[:, m, :], ga[:, m, :], banks[0][:, 0:T], ALU.mult)
                    V.tensor_tensor(gb[:, m, :], gb[:, m, :], banks[1][:, 0:T], ALU.mult).then_inc(s["mb_ready"], 1)
                    dve.wait_ge(s["mb_ready"], i + 1)
                    V.tensor_tensor(mm_[:, m, :], ga[:, m, :], gb[:, m, :], ALU.add).then_inc(s["m_ready"], 1)
                    dve.wait_ge(s["mh_ready"], i + 1)
                    V.tensor_tensor(ml[:, ds(n * (2 * T) + m * T, T)], mm_[:, m, :],
                                    mh[:, ds(n * (2 * T) + m * T, T)].bitcast(F32), ALU.subtract).then_inc(s["ml_ready"], 1)

            def out_tile(n, m, first=False):
                i = n * 2 + m
                for h in range(2):
                    ahead(n * 4 + BASE_OUT, 2 * m + h)
                dve.wait_ge(s["so_ready"], i + 1)
                V.tensor_tensor(o2[:, ds(n * (2 * T) + m * T, T)], acc[m][:, 0:T],
                                par2[:, ds(n * 2 + (NPOST + m), 1)].to_broadcast([P, T]), ALU.mult).then_inc(s["o2_ready"], 1)
                if first:
                    V.tensor_copy(sacc[:, :], sqo[:, m, :]).then_inc(s["sacc_ready"], 1)
                else:
                    dve.wait_ge(s["sacc_ready"], i)
                    V.tensor_tensor(sacc[:, :], sacc[:, :], sqo[:, m, :], ALU.add).then_inc(s["sacc_ready"], 1)

            out_tile(0, 0, first=True)
            out_tile(0, 1)
            with dve.Fori(1, KT // 2) as n:
                for m in range(2):
                    out_tile(n, m)
            dve.wait_ge(s["srt"], 1)
            V.reciprocal(sacc[:, :], sacc[:, :]).then_inc(s["chain"], 1)
            dve.wait_ge(s["chain"], 8)
            dve.wait_ge(s["o2_ready"], KT)

            def lower_part(k):
                dve.wait_ge(s["x1h_ready"], k + 1)
                V.tensor_tensor(x1l[:, T * k:T * (k + 1)], xT[:, T * k:T * (k + 1)],
                                x1h[:, T * k:T * (k + 1)].bitcast(F32), ALU.subtract).then_inc(s["x1l_ready"], 1)

            for k in range(KT):
                V.tensor_tensor(o2[:, T * k:T * (k + 1)], o2[:, T * k:T * (k + 1)], sacc[:, :], ALU.mult).then_inc(s["x1a"], 1)
                if k >= 3:
                    lower_part(k - 3)
            for k in range(KT - 3, KT):
                lower_part(k)

            def gate_tile(n, m, last=False):
                i = n * 2 + m
                for h in range(2):
                    if not last or 2 * m + h + AHEAD < 4:
                        ahead(n * 4 + BASE_GATE, 2 * m + h)
                dve.wait_ge(s["g3_ready"], i + 1)
                dve.wait_ge(s["ple_ps"], i + 1)
                V.tensor_tensor(g3[:, m, :], g3[:, m, :], B[m][:, 0:T], ALU.mult).then_inc(s["g3m"], 1)
                dve.wait_ge(s["g3m"], i + 1)
                V.tensor_tensor(yo[:, m, :], g3[:, m, :], xT[:, ds(n * (2 * T) + m * T, T)], ALU.add).then_inc(s["yo_ready"], 1)

            with dve.Fori(0, KT // 2 - 1) as n:
                for m in range(2):
                    gate_tile(n, m)
            for m in range(2):
                gate_tile(KT // 2 - 1, m, last=True)

        @block.tensor
        def _(pe):
            M = nc.tensor

            def passes(out, slot, k, hi, lo, width, first, last):
                wcol = slice(P * k, P * (k + 1))
                M.matmul(out[:, 0:width], wh[:, slot, wcol], hi, start=first, stop=False)
                M.matmul(out[:, 0:width], wh[:, slot, wcol], lo, start=False, stop=False)
                return M.matmul(out[:, 0:width], wl[:, slot, wcol], hi, start=False, stop=last)

            def chunk(count, j, out, hi, lo, pitch, width, k0, first, last, part=None):
                slot = j % SLOTS
                ks = range(KC) if part is None else part
                for k in ks:
                    if k == 0:
                        pe.wait_ge(s["lo_ready"], count + j + 1)
                    a = (k0 + k) * pitch
                    mm = passes(out, slot, k, hi[:, a:a + width], lo[:, a:a + width], width,
                                first and k == 0, last and k == KC - 1)
                    if k == KC - 1:
                        mm.then_inc(s["chunk_used"], 1)

            def transpose(out, in_):
                rows = in_.shape[0]
                return M.transpose(out, in_, ident[0:rows, 0:rows])

            pe.wait_ge(s["const_in"], 32)
            pe.wait_ge(s["rows_in"], 12 * 16)
            transpose(B[4][:, 0:NROW * PAIRS], rows[0:NROW * PAIRS, 0, :]).then_inc(s["par_ready"], 1)
            transpose(B[5][:, 0:NPAR2], rows[0:NPAR2, 1, :]).then_inc(s["par_ready"], 1)
            for t in range(3):
                n = P if t < 2 else NB * TB + NB
                pe.wait_ge(s["h_rows"], (1, 2, 4)[t])
                for c in range(4):
                    if t:
                        pe.wait_ge(s["hT_done"], 4 * (t - 1) + c + 1)
                    for k in range(4):
                        col = P * (4 * c + k)
                        last = transpose(B[c][:, P * k:P * k + n], ht[0:n, t % 2, col:col + P])
                    last.then_inc(s["hT_ps"], 1)

            class Stream:

                def __init__(self, q):
                    self.q, self.at = q, 0

                def advance(self, n):
                    if self.q is None:
                        return
                    for _ in range(n):
                        tile, kt = self.at // KT, self.at % KT
                        if kt == 0 and not (isinstance(self.q, int) and tile < 2):
                            pe.wait_ge(s["acc_free"], self.q * 4 + (tile - 1))
                        width = TS if tile < 3 else T
                        chunk(self.q * CH_PAIR, 2 * tile + kt // KC, acc[tile % 2], hh, hl, TS, width,
                              KC * (kt // KC), kt // KC == 0, kt // KC == 1, part=[kt % KC])
                        self.at += 1

            pe.wait_ge(s["h_split"], 3)
            first = Stream(0)
            for j in range(CH_PAIR):
                first.advance(KC)
                if j == 0:
                    pe.wait_ge(s["par_done"], 4)
                    pe.wait_ge(s["dh_done"], 4)
                    transpose(B[4][0:72, 0:P], hlast[:, 0:72]).then_inc(s["last_ps"], 1)
                    transpose(B[5][0:72, 0:P], hlast[:, 72:144]).then_inc(s["last_ps"], 1)
                    pe.wait_ge(s["map_in"], 32)
                for n in range(4 * j, 4 * j + 4):
                    k = n // 2
                    pe.wait_ge(s["xw_ready"], n + 1)
                    M.matmul(B[n % 2][0:RANK, 0:T], (lw1, la1)[n % 2][:, k, :], xw[:, n % 4, :],
                             start=k == 0, stop=k == KT - 1).then_inc(s["xw_used"], 1)

            def mix(r, q=None):
                st = Stream(q)
                st.advance(6)
                pe.wait_ge(s["acc_free"], r * 4 + 4)
                pe.wait_ge(s["s0_in"], r * 32 + 32)
                pe.wait_ge(s["last_done"], 2)
                for b in range(NB):
                    last = transpose(B45[:, P * b:P * (b + 1)], S0n[:, b, :])
                last.then_inc(s["s0_ps"], 1)
                pe.wait_ge(s["lw2_in"], r * 32 + 32)
                pe.wait_ge(s["lora_act"], 2)
                M.matmul(B[0][:, 0:T], lw2[:, :], t1[:, :], start=True, stop=True)
                M.matmul(B[1][:, 0:T], la2[:, :], la[:, :], start=True, stop=True).then_inc(s["lora2_ps"], 1)
                st.advance(2)
                pe.wait_ge(s["ksq_ready"], r + 1)
                M.matmul(B[2][:, 0:T], ones2, sq[:, :], start=True, stop=True).then_inc(s["kk_ps"], 1)
                st.advance(4)
                pe.wait_ge(s["rk_ready"], r + 1)
                M.matmul(B[3][:, 0:T], ones2, sq[:, :], start=True, stop=True).then_inc(s["rk_ps"], 1)
                st.advance(4)
                pe.wait_ge(s["s0t_ready"], r + 1)
                pe.wait_ge(s["rh_ready"], r + 1)
                z = B[5][:, 0:2 * C].rearrange("p (a c) -> p a c", a=2)
                for b in range(NB):
                    last = M.matmul(z[:, :, TB * b:TB * (b + 1)], S0T[:, b, :], ar[:, :, TP + TB * b:TP + TB * (b + 1)],
                                    start=True, stop=True)
                last.then_inc(s["z_ps"], 1)
                pe.wait_ge(s["bbd_ready"], r * 2 + 2)
                pe.wait_ge(s["kbd_ready"], r * 2 + 2)
                pe.wait_ge(s["bv_ready"], r + 1)
                for out, left, right in ((B[0], bBD, ar[:, 0, :]), (B[1], aBD, bU[:, :]), (B[2], kBD, ar[:, 0, :]),
                                         (B[3], bBD, ar[:, 1, :]), (B[4], kBD, ar[:, 1, :])):
                    for g in range(G):
                        last = M.matmul(out[:, tok(g)], flat(left, g), right[:, tok(g)], start=True, stop=True)
                    last.then_inc(s["score_ps"], 1)
                st.advance(4)
                pe.wait_ge(s["vbd_ready"], r * 2 + 2)
                pe.wait_ge(s["akbd_ready"], r + 1)
                pe.wait_ge(s["arb_ready"], r + 1)
                for g in range(G):
                    last = transpose(B23[:, P * g:P * (g + 1)], flat(vBD, g))
                last.then_inc(s["vt_ps"], 1)
                pe.wait_ge(s["ark_ready"], r + 1)
                pe.wait_ge(s["zabd_ready"], r * 2 + 2)
                for g in range(G):
                    last = transpose(B45[:, P * g:P * (g + 1)], flat(bBD, g))
                last.then_inc(s["bt_ps"], 1)
                for g in range(G):
                    last = transpose(B01[:, P * g:P * (g + 1)], flat(kBD, g))
                last.then_inc(s["kt_ps"], 1)
                st.advance(4)

                def products(n):
                    pe.wait_ge(s["y_ready"], r * (LEVELS + 1) + n + 1)
                    if n == 0:
                        pe.wait_ge(s["kt_ready"], r + 1)
                    for g in range(G):
                        last = M.matmul(B[0][:, tok(g)], flat(ABD, g), Y[:, g, :], start=True, stop=True)
                    last.then_inc(s["t_ps"], 1)

                def inverse_transpose(n):
                    pe.wait_ge(s["ybd_ready"], r * (2 * LEVELS + 2) + 2 * n + 2)
                    if n == 0:
                        pe.wait_ge(s["bt_ready"], r + 1)
                    for g in range(G):
                        last = transpose(B45[:, P * g:P * (g + 1)], flat(YBD, g))
                    last.then_inc(s["x_ps"], 1)

                def update(n):
                    pe.wait_ge(s["t_ready"], r * LEVELS + n + 1)
                    pe.wait_ge(s["x_ready"], r * LEVELS + n + 1)
                    for g in range(G):
                        last = M.matmul(B[1][:, tok(g)], flat(XBD, g), Tm[:, g, :], start=True, stop=True)
                    last.then_inc(s["m_ps"], 1)

                inverse_transpose(0)
                products(0)
                st.advance(2)
                update(0)
                st.advance(3)
                for n, (x, y, z_) in zip(range(1, LEVELS), ((2, 1, 3), (2, 1, 2), (2, 1, 2), (1, 1, 1))):
                    products(n)
                    st.advance(x)
                    inverse_transpose(n)
                    st.advance(y)
                    update(n)
                    st.advance(z_)
                pe.wait_ge(s["tail_ready"], r * 2 + 2)
                pe.wait_ge(s["x_ready"], r * LEVELS + LEVELS)
                for n in range(2):
                    last = transpose(B[5][:, P * n:P * (n + 1)], tail4[:, n].rearrange("p h c -> p (h c)"))
                last.then_inc(s["tail_ps"], 1)
                for g in range(GP):
                    pe.wait_ge(s["vs_ready"], r * 2 + 2)
                    M.matmul(B[2][:, 0:C], flat(AKBD, g), Vs[:, g, :], start=True, stop=g == 0)
                    if g == 0:
                        M.matmul(B[2][:, C:2 * C], flat(AKBD, G - 1), Vs[:, G - 1, :], start=True, stop=False)
                        last = M.matmul(B[2][:, C:2 * C], ZaBD[:, :, :].rearrange("p h c -> p (h c)"), istk, start=False, stop=True)
                    else:
                        pe.wait_ge(s["s_ready"], r * GP + g)
                        last = M.matmul(B[2][:, 0:C], flat(aBD, g), Ss[:, g - 1, :], start=False, stop=True)
                    last.then_inc(s["rhs_ps"], 1)
                    st.advance(1)
                    pe.wait_ge(s["ybd_ready"], r * (2 * LEVELS + 2) + 2 * LEVELS + 2)
                    pe.wait_ge(s["rhs_ready"], r * GP + g + 1)
                    last = M.matmul(B[3][:, 0:C], flat(YBD, g), RHS[:, 0, :], start=True, stop=True)
                    if g == 0:
                        last = M.matmul(B[3][:, C:2 * C], flat(YBD, G - 1), RHS[:, 1, :], start=True, stop=True)
                    last.then_inc(s["u_ps"], 1)
                    st.advance(1)
                    M.matmul(B[0][:, 0:C], flat(KtBD, g), Vs[:, g, :], start=True, stop=False)
                    pe.wait_ge(s["u_ready"], r * GP + g + 1)
                    M.matmul(B[0][:, 0:C], flat(BtBD, g), Us[:, g, :], start=False, stop=True).then_inc(s["s_ps"], 1)
                    st.advance(1)
                pe.wait_ge(s["endbd_ready"], r * 2 + 2)
                transpose(B[0][:, 0:P], EndBD[:, :, :].rearrange("p h c -> p (h c)")).then_inc(s["end_ps"], 1)
                pe.wait_ge(s["sbd_ready"], r * 2 + 2)
                pe.wait_ge(s["ubd_ready"], r * 2 + 2)
                for g in range(G):
                    o = B[4][:, tok(g)]
                    M.matmul(o, flat(VtBD, g), ARK[:, g, :], start=True, stop=False)
                    if g == G - 1:
                        M.matmul(o, ident, Zs[:, 1, :], start=False, stop=False)
                    elif g:
                        M.matmul(o, flat(SBD, g - 1), ar[:, 1, tok(g)], start=False, stop=False)
                    last = M.matmul(o, flat(UBD, g), ARB[:, g, :], start=False, stop=True)
                last.then_inc(s["o_ps"], 1)
                st.advance(2)
                for name in ("xpb_ready", "xpk_ready", "dpl_ready"):
                    pe.wait_ge(s[name], r + 1)
                M.matmul(B[3][:, :], flat(UBD, G - 1), xpB[:, :, :].rearrange("p b c -> p (b c)"), start=True, stop=False)
                M.matmul(B[3][:, :], flat(VtBD, G - 1), xpK[:, :, :].rearrange("p b c -> p (b c)"), start=False, stop=False)
                for b in range(NB):
                    last = M.matmul(B[3][:, C * b:C * (b + 1)], S0T[:, b, :], dPL[:, b, :], start=False, stop=b == NB - 1)
                last.then_inc(s["send_ps"], 1)
                pe.wait_ge(s["o_ready"], r + 1)
                pe.wait_ge(s["tails_ready"], r * 2 + 2)
                M.matmul(B[5][:, 0:T], mean2, O_s[:, :], start=True, stop=True).then_inc(s["mean_ps"], 1)
                st.advance(2)
                pe.wait_ge(s["dsq_ready"], r + 1)
                M.matmul(B[1][:, 0:T], mean2, dsq[:, :], start=True, stop=True).then_inc(s["var_ps"], 1)
                if q is not None:
                    st.advance(4 * KT - st.at)

            with pe.Fori(1, PAIRS) as q:
                mix(q - 1, q)
            mix(PAIRS - 1)

            pe.wait_ge(s["yal_ready"], PAIRS)
            pe.wait_ge(s["end_ready"], PAIRS)
            pe.wait_ge(s["pool_in"], 16)
            for k in range(8):
                w = NB * BUF
                last = transpose(B[k // 4][:, w * (k % 4):w * (k % 4 + 1)], spt[:, P * k:P * (k + 1)])
                if k % 4 == 3:
                    last.then_inc(s["utok_ps"], 1)
            with pe.Fori(0, 8) as n:
                for t in range(2):
                    pe.wait_ge(s["acc_free"], n * 2 + (4 * PAIRS + t - 1))
                    for h in range(2):
                        chunk(n * CH_POOL + BASE_POOL, 2 * t + h, acc[t], hh, hl, TS, T, KC * h, h == 0, h == 1)
            pe.wait_ge(s["acc_free"], 4 * PAIRS + 16)
            for k in range(8):
                last = transpose(B[4 + k // 4][0:NB * TB + BUF, P * (k % 4):P * (k % 4 + 1)], uS[:, k, TP - BUF:T])
                if k % 4 == 3:
                    last.then_inc(s["utok_ps"], 1)
            pe.wait_ge(s["map_in"], 48)
            for m in range(8):
                g = m // 2
                pe.wait_ge(s["mixed"], 4 * g + 4)
                if m >= 4:
                    pe.wait_ge(s["sil"], 2 * (m - 4) + 1)
                for k in range(2):
                    last = M.matmul(B[m % 4][:, 0:T], pw[:, 2 * g + k, P * (m % 2):P * (m % 2) + P], uS[:, 2 * g + k, :],
                                    start=k == 0, stop=k == 1)
                last.then_inc(s["pyb_ps"], 1)

            pe.wait_ge(s["ybl_ready"], 8)
            pe.wait_ge(s["utok_ev"], 2)

            def merge_tile(n, m, free):
                banks = (acc[0], acc[1], B[0], B[1]) if m == 0 else (B[2], B[3], B[4], B[5])
                count = n * (2 * CH_MERGE) + BASE_MERGE
                if free:
                    pe.wait_ge(s["m_ready"], n * 2 + m - 1)
                for g in range(2):
                    for h in range(2):
                        chunk(count, CH_MERGE * m + 2 * g + h, banks[g], hh, hl, TS, T, KC * h, h == 0, h == 1)
                chunk(count, CH_MERGE * m + 4, banks[2], yah, yal, T, T, 0, True, True)
                chunk(count, CH_MERGE * m + 5, banks[3], ybh, ybl, T, T, 0, True, True)

            for m in range(2):
                merge_tile(0, m, False)
            with pe.Fori(1, KT // 2) as n:
                for m in range(2):
                    merge_tile(n, m, True)

            pe.wait_ge(s["ml_ready"], KT)

            def out_tile(n, m, free):
                if free:
                    pe.wait_ge(s["o2_ready"], n * 2 + m - 1)
                for h in range(2):
                    chunk(n * 4 + BASE_OUT, 2 * m + h, acc[m], mh, ml, T, T, KC * h, h == 0, h == 1)

            for m in range(2):
                out_tile(0, m, False)
            sizes = (P, P, NB * TB)
            pe.wait_ge(s["x2_in"], 96)
            for k in range(KT):
                if k >= 4:
                    pe.wait_ge(s["xT_ready"], k - 3)
                for t in range(3):
                    last = transpose(B[k % 4][:, P * t:P * t + sizes[t]], xt2[0:sizes[t], t, P * k:P * (k + 1)])
                last.then_inc(s["xT_ps"], 1)
            pe.wait_ge(s["x2_in"], 96)
            for k in range(2):
                for t in range(3):
                    last = transpose(B[4 + k][:, P * t:P * t + sizes[t]], pt[0:sizes[t], t, P * k:P * (k + 1)])
                last.then_inc(s["pT_ps"], 1)
            with pe.Fori(1, KT // 2) as n:
                for m in range(2):
                    out_tile(n, m, True)
            pe.wait_ge(s["sacc_ready"], KT)
            pe.wait_ge(s["pT_ready"], 2)
            M.matmul(B[5][:, 0:T], meand, sacc[:, :], start=True, stop=True).then_inc(s["ssq_ps"], 1)

            def gate_tile(n, m, pace=False):
                if pace:
                    for h in range(2):
                        for k in range(KC):
                            pe.wait_ge(s["x1l_ready"], KC * h + k + 1)
                            chunk(n * 4 + BASE_GATE, 2 * m + h, acc[m], x1h, x1l, T, T, KC * h, h == 0, h == 1, part=[k])
                else:
                    for h in range(2):
                        chunk(n * 4 + BASE_GATE, 2 * m + h, acc[m], x1h, x1l, T, T, KC * h, h == 0, h == 1)
                pe.wait_ge(s[f"wple_in{m}"], n * 16 + 16)
                for k in range(2):
                    last = M.matmul(B[m][:, 0:T], wple[:, m, P * k:P * (k + 1)], pT[:, k, :], start=k == 0, stop=k == 1)
                last.then_inc(s["ple_ps"], 1)

            def tokens(i, m, free):
                pe.wait_ge(s["yo_ready"], i + 1)
                if free is not None:
                    pe.wait_ge(s["ytk_ready"], free)
                for t in range(3):
                    last = transpose(B[2 + m][0:sizes[t], P * t:P * (t + 1)], yo[:, m, P * t:P * t + sizes[t]])
                last.then_inc(s["yt_ps"], 1)

            pe.wait_ge(s["o2_ready"], KT)
            gate_tile(0, 0, pace=True)
            gate_tile(0, 1)
            tokens(0, 0, None)
            pe.wait_ge(s["yo_ready"], 1)
            gate_tile(1, 0)
            tokens(1, 1, None)
            gate_tile(1, 1)
            tokens(2, 0, 2)
            with pe.Fori(2, KT // 2) as n:
                gate_tile(n, 0)
                tokens(n * 2 - 1, 1, n * 4 - 4)
                gate_tile(n, 1)
                tokens(n * 2, 0, n * 4 - 2)
            tokens(KT - 1, 1, 2 * KT - 4)


OUTS = [((1, TP, D), "float32"), ((NB, TB, D), "float32"), ((1, 1, 16, HD, HD), "float32"), ((1, 1, D), "float32"),
        ((1, 1, BUF, R), "float32"), ((1, NB, 16, HD, HD), "float32"), ((1, NB, D), "float32"), ((1, NB, BUF, R), "float32")]
INS = ["x_prompt", "x_sample", "state_wkv", "state_shift", "state_pool", "p_prompt", "p_sample", "norm_pre", "norm_post",
       "w_in", "mu_rkv", "mu_lora", "w0", "w1", "w2", "a0", "a1", "a2", "k_k", "k_a", "r_k", "ln_w", "ln_b", "pool_w",
       "pool_scale", "w_branch", "w_out", "w_ple", "w_ple_gate"]


def kernel(**inputs):
    import ml_dtypes
    from concourse import bacc
    from concourse.bass_utils import run_bass_kernel_spmd

    nc = bacc.Bacc("TRN2", target_bir_lowering=False, num_devices=1)
    const_f, const_m = shape_constants()
    arrays = {f"in_{n}": np.ascontiguousarray(inputs[n]) for n in INS}
    arrays["in_const_f"] = const_f
    arrays["in_const_m"] = const_m.astype(ml_dtypes.bfloat16)
    args = [nc.dram_tensor(n, a.shape, mybir.dt.from_np(a.dtype), kind="ExternalInput").ap() for n, a in arrays.items()]
    for i, (shape, dtype) in enumerate(OUTS):
        args.append(nc.dram_tensor(f"out_{i}", shape, mybir.dt.from_np(np.dtype(dtype)), kind="ExternalOutput").ap())
    build(nc, *args)
    r = run_bass_kernel_spmd(nc, [arrays], core_ids=[0])
    return tuple(r.results[0][f"out_{i}"] for i in range(len(OUTS)))
```

```python
from contextlib import ExitStack

import numpy as np
import concourse.bass as bass
from concourse import mybir

F32 = mybir.dt.float32
F32R = mybir.dt.float32r
BF16 = mybir.dt.bfloat16
ALU = mybir.AluOpType
ACT = mybir.ActivationFunctionType
ds = bass.ds

P = 128
D = 2048
KT = D // P
R = 1024
PAIRS = R // P
HD = 64
TP = 256
NB = 8
TB = 8
T = TP + NB * TB
TS = T + NB
C = 64
G = T // C
GP = TP // C
RANK = 96
PLE = 256
BUF = 15
WINDOWS = (2, 4, 8, 16)
PGROUP = R // len(WINDOWS)
DECAY = 0.606531
RMS_EPS = 1e-6
GN_EPS = 64e-5
LEVELS = 5
SMALL = 2

MAP_TILES = [(), (), (0, 1, 2), (3, 4, 5), (6, 7, 8), (9, 10, 11), (12, 13), (14, 15)]
KC = 8
SLOTS = 4
AHEAD = 3
CH_FIRST = 8
CH_STEP = 12
CH_MERGE = 6
BASE_STEP = CH_FIRST - CH_STEP
BASE_EARLY = BASE_STEP + CH_STEP * (PAIRS + 1)
EARLY = 4
BASE_MERGE = BASE_EARLY + 4 * EARLY - CH_MERGE * EARLY
BASE_OUT = BASE_MERGE + CH_MERGE * KT
TILES_STEP = 6
ACC_STEP = 4 - TILES_STEP
ACC_ALL = ACC_STEP + TILES_STEP * (PAIRS + 1)
BASE_GATE = BASE_OUT + 2 * KT
CHUNKS = BASE_GATE + 2 * KT

COL_R, COL_K, COL_V, COL_G = 0, R, 2 * R, 3 * R
COL_U, COL_GP, COL_GA, COL_GB = 4 * R, 5 * R, 6 * R, 6 * R + D

MU_R, MU_K, MU_V, W0, A0, K_K, K_A, R_K, LN_W, LN_B, OM_R, OM_K, OM_V, OM_KA = range(14)
NPAR, NROW = 14, 10
NPRE, NPOST, MUW, MUA, PSC = 0, 16, 32, 48, 64
NPAR2 = 72

EXT = BUF + TP + NB * (BUF + TB)

CF = {}
CM = {}


def _columns(table, *widths):
    at = 0
    for name, width in widths:
        table[name] = (at, at + width)
        at += width
    return at


N_CF = _columns(CF, ("ident", P), ("istk", HD), ("ones2", P), ("mean2", P), ("meand", P), ("segment", T),
                ("batch", NB), ("eps", 2), ("count", 4 * 16))
N_CM = _columns(CM, ("pairs", T), ("incl", T), ("strict", 2 * T), ("lower", 2 * T), ("level", LEVELS * T))


def shape_constants():
    f = np.zeros((P, N_CF), np.float32)
    p = np.arange(P)
    head, row = p // HD, p % HD

    def put(table, arr, name, value):
        a, b = table[name]
        arr[:, a:b] = value.reshape(P, b - a)

    put(CF, f, "ident", np.eye(P))
    put(CF, f, "istk", (row[:, None] == np.arange(HD)[None]))
    same = head[:, None] == head[None]
    put(CF, f, "ones2", same * 1.0)
    put(CF, f, "mean2", same / HD)
    put(CF, f, "meand", np.full((P, P), 1.0 / D))
    tok = np.arange(T)
    first = np.where(tok < TP, tok % C == 0, tok % TB == 0)
    put(CF, f, "segment", np.broadcast_to(1.0 - first, (P, T)))
    put(CF, f, "batch", (row // TB)[:, None] == np.arange(NB)[None])
    put(CF, f, "eps", np.broadcast_to(np.array([RMS_EPS, GN_EPS]), (P, 2)))
    put(CF, f, "count", np.broadcast_to(np.array([[1.0 / min(t + 1, w) for t in range(16)] for w in WINDOWS]), (P, 4, 16)))

    m = np.zeros((P, N_CM), np.float32)
    s, t = row[:, None, None], np.arange(C)[None, None, :]
    g = np.arange(G)[None, :, None]
    seq = (g < GP) | (s // TB == t // TB)
    put(CM, m, "incl", (s <= t) & seq)

    def level(b):
        inside = (s // (2 * b) == t // (2 * b)) & ((s // b) % 2 == 0) & ((t // b) % 2 == 1)
        return inside & ((g < GP) | (2 * b <= TB))

    put(CM, m, "pairs", level(1))
    a = CM["level"][0]
    for n in range(LEVELS):
        m[:, a + n * T:a + (n + 1) * T] = level(2 ** (n + 1)).reshape(P, T)

    def diagonal(x):
        x = np.broadcast_to(x, (P, G, C))[:, :, None, :] & (head[:, None, None, None] == np.arange(2)[None, None, :, None])
        return x

    put(CM, m, "strict", diagonal((s < t) & seq))
    put(CM, m, "lower", diagonal((s > t) & seq))
    return f, m


def build(nc, x_prompt, x_sample, state_wkv, state_shift, state_pool, p_prompt, p_sample, norm_pre, norm_post,
          w_in, mu_rkv, mu_lora, w0, w1, w2, a0, a1, a2, k_k, k_a, r_k, ln_w, ln_b, pool_w, pool_scale,
          w_branch, w_out, w_ple, w_ple_gate, const_f, const_m,
          y_prompt, y_sample, wkv_prompt, shift_prompt, pool_prompt, wkv_sample, shift_sample, pool_sample):
    with ExitStack() as ctx:
        base = (nc.sbuf_base + 31) // 32 * 32
        used = {}

        def at(word, name, shape, dt=F32):
            size = int(np.prod(shape[1:])) * (2 if dt == BF16 else 4)
            used[name] = (word, word + (size + 3) // 4)
            return nc.alloc_sbuf_tensor_at(name, list(shape), dt, offset=base + 4 * word)

        class Region:
            def __init__(self, start):
                self.next = start

            def take(self, name, shape, dt=F32):
                t = at(self.next, name, shape, dt)
                self.next = (used[name][1] + 7) // 8 * 8
                return t

        fixed = Region(0)
        cf = fixed.take("cf", [P, N_CF])
        cm = fixed.take("cm", [P, N_CM], BF16)
        par = fixed.take("par", [P, NPAR * PAIRS])
        par2 = fixed.take("par2", [P, NPAR2])
        hh = fixed.take("hh", [P, KT * TS], F32R)
        hl = fixed.take("hl", [P, KT * TS], F32R)
        wraw = fixed.take("wraw", [P, SLOTS, KC * P])
        wh = fixed.take("wh", [P, SLOTS, KC * P], F32R)
        wl = fixed.take("wl", [P, SLOTS, KC * P], F32R)
        ya_start = fixed.next
        yf = fixed.take("yf", [P, PAIRS * T])
        gp = fixed.take("gp", [P, 8, T])
        t1 = fixed.take("t1", [RANK, T])
        la = fixed.take("la", [RANK, T])
        arena = fixed.next

        r1 = Region(arena)
        zsh = r1.take("zsh", [P, T])
        kS = r1.take("kS", [P, T])
        rS = r1.take("rS", [P, T])
        vS = r1.take("vS", [P, T])
        gS = r1.take("gS", [P, T])
        cur_p = r1.take("cur_p", [P, NPAR])
        cur_m = r1.take("cur_m", [P, NPAR])
        lw2 = r1.take("lw2", [RANK, P])
        la2 = r1.take("la2", [RANK, P])
        start_overlay = r1.next
        r0 = Region(start_overlay)
        xt = r0.take("xt", [P, 3, D])
        dh = at(used["xt"][0], "dh", [P, KT * T])
        ht = r0.take("ht", [P, 2, D])
        xw = at(used["ht"][0], "xw", [P, 4, T])
        hT = r0.take("hT", [P, KT * TS])
        rows = r0.take("rows", [P, 2, P])
        stat = r0.take("stat", [P, 4])
        hlast = r0.take("hlast", [P, 2 * 72])
        hlastT = r0.take("hlastT", [72, 2 * P])
        lw1 = at(ya_start, "lw1", [P, KT, RANK])
        la1 = at(used["lw1"][1], "la1", [P, KT, RANK])
        aBD = r1.take("aBD", [P, G, 2, C])
        bBD = r1.take("bBD", [P, G, 2, C])
        kBD = r1.take("kBD", [P, G, 2, C])
        vBD = r1.take("vBD", [P, G, 2, C])
        ABD = r1.take("ABD", [P, G, 2, C])
        AKBD = r1.take("AKBD", [P, G, 2, C])
        YBD = r1.take("YBD", [P, G, 2, C])
        BtBD = r1.take("BtBD", [P, G, 2, C])
        KtBD = r1.take("KtBD", [P, G, 2, C])
        VtBD = r1.take("VtBD", [P, G, 2, C])
        ZaBD = r1.take("ZaBD", [P, 2, C])
        EndBD = r1.take("EndBD", [P, 2, C])
        S0T = r1.take("S0T", [P, NB, P])
        S0n = r1.take("S0n", [P, NB, P])
        UBD, SBD, XBD = bBD, kBD, vBD
        sq = r1.take("sq", [P, T])
        pm = r1.take("pm", [P, T])
        aS = r1.take("aS", [P, T])
        sg = r1.take("sg", [P, T])
        cl = r1.take("cl", [P, T])
        rn = r1.take("rn", [P, T])
        pd = r1.take("pd", [P, T])
        pi = r1.take("pi", [P, T])
        kf = r1.take("kf", [P, T])
        bv = r1.take("bv", [P, T])
        kkn = r1.take("kkn", [P, T])
        bU = r1.take("bU", [P, T])
        ar = r1.take("ar", [P, 2, T])
        Y = r1.take("Y", [P, G, C])
        Tm = r1.take("Tm", [P, G, C])
        ARB = r1.take("ARB", [P, G, C])
        ARK = r1.take("ARK", [P, G, C])
        Vs = r1.take("Vs", [P, G, C])
        Us = r1.take("Us", [P, G, C])
        Ss = r1.take("Ss", [P, G, C])
        Sd = r1.take("Sd", [P, C])
        RHS = r1.take("RHS", [P, 2, C])
        Zs = r1.take("Zs", [P, 2, C])
        tail4 = r1.take("tail4", [P, 2, 2, C])
        tails = r1.take("tails", [P, 2, C])
        xpB = at(used["sq"][0], "xpB", [P, NB, C])
        xpK = r1.take("xpK", [P, NB, C])
        dPL = r1.take("dPL", [P, NB, C])
        so = at(used["dPL"][0], "so", [P, NB, C])
        eo = r1.take("eo", [P, P])
        O_s, dO, dsq, sd = cl, pd, pi, kf
        uS = r1.take("uS", [P, 8, T])
        r2 = Region(used["gS"][1])
        gt = r2.take("gt", [P, 4, T])
        ue = r2.take("ue", [P, 2, EXT])
        win_a = r2.take("win_a", [P, 2, EXT])
        win_b = r2.take("win_b", [P, 2, EXT])
        spt = r2.take("spt", [NB * BUF, R])
        utok = at(used["spt"][0], "utok", [NB * TB + BUF, R])
        pw = r2.take("pw", [P, 8, PGROUP])
        head = r2.take("head", [P, 2, 16])
        yah = r2.take("yah", [P, PAIRS * T], F32R)
        yal = r2.take("yal", [P, PAIRS * T], F32R)
        ybh = r2.take("ybh", [P, 8 * T], F32R)
        ybl = r2.take("ybl", [P, 8 * T], F32R)
        gsig = at(used["ybl"][0], "gsig", [P, 8 * T])
        ytmp = at(used["t1"][0], "ytmp", [P, 2, T])
        mh = at(ya_start, "mh", [P, KT * T], F32R)
        r3 = Region(used["gt"][1])
        ml = r3.take("ml", [P, KT * T], F32R)
        ga = r3.take("ga", [P, 2, T])
        assert r3.next <= used["yah"][0] and r2.next <= used["uS"][0]
        r4 = Region(used["uS"][0])
        gb = r4.take("gb", [P, 2, T])
        sacc = r4.take("sacc", [P, T])
        mm_ = at(used["t1"][0], "mm", [P, 2, T])
        xT = at(used["yah"][0], "xT", [P, KT * T])
        o2 = at(used["ybh"][0], "o2", [P, KT * T])
        r5 = Region(arena)
        sqo = r5.take("sqo", [P, 2, T])
        pT = r5.take("pT", [P, 2, T])
        wple = r5.take("wple", [P, 2, 2 * P])
        yo = r5.take("yo", [P, 2, T])
        assert r5.next <= used["gt"][1]
        g3 = ga
        ytk = at(ya_start, "ytk", [P, 2, 3 * P])
        xt2 = at(used["hh"][0], "xt2", [P, 3, D])
        pt = at(used["xt2"][1], "pt", [P, 3, PLE])
        x1h = at(used["hh"][0], "x1h", [P, KT * T], F32R)
        x1l = at(used["hl"][0], "x1l", [P, KT * T], F32R)
        end = max(b for _, b in used.values())
        room = (nc.sbuf_usable_end if not callable(nc.sbuf_usable_end) else nc.sbuf_usable_end())
        assert base + 4 * end <= room, (base + 4 * end, room)
        assert used["S0n"][0] >= used["xw"][1] and used["S0n"][1] <= used["hT"][0]
        assert used["pt"][1] <= used["hl"][1] and used["la1"][1] <= used["gp"][1]

        acc = [ctx.enter_context(nc.psum_tensor(f"acc{i}", [P, 512], F32)) for i in range(2)]
        B01, B23, B45 = [ctx.enter_context(nc.psum_tensor(f"wide{i}", [P, 1024], F32)) for i in range(3)]
        B = [w[:, 512 * i:512 * (i + 1)] for w in (B01, B23, B45) for i in range(2)]

        sems = {}
        for name in """y_out0 y_out1 wple_in0 wple_in1 lo_ready x_in0 x_in1 x_in2 eout sout const_in rows_in map_in zeroed
            last_done rows_out cur_p_ready lw2_in s0_in par_done xw_ready xw_used cur_m_ready acc_free vbd_ready
            a_ready kf_ready sg_ready sgs_ready exp_ready api_ready kbd_ready bbd_ready tail_ready dpl_ready
            tails_ready xpk_ready end_ready send_ready lora2_ps s0_ps yal_ready pool_in utok_ev chunk_used x2_in
            xT_ready x1a x1b ytk_ready ple_ps hi_ready zsh_ready hT_ps x_stat hT_done hh_done dh_done last_ps lora_act
            s0t_ready ksq_ready decay_in kk_max kk_norm cum_ready cumx_ready ah_ready bh_ready z_ps zabd_ready vt_ps
            vs_ready bt_ps bt_ready y_ready ybd_ready x_ps x_ready kt_ps kt_ready tail_ps s_ready sd_ready endbd_ready
            sbd_ready ubd_ready end_ps o_ps o_ready send_ps dev_ready dsq_ready var_ps sd_done y_done yah_ready gsil_ready
            gsig_ready yb_ready gates_ready yb_done utok_ps sb_ready m_ready mh_ready so_ready xT_ps pT_ps pT_ready sacc_ready ssq_ps srt
            x1h_ready g3_ready yt_ps par_ready chain h_rows h_split hl_done kk_ps kk_rn rk_ready kkn_ready rh_ready rk_ps
            bv_ready score_ps akbd_ready arb_ready ark_ready t_ps t_ready m_ps rhs_ps rhs_ready u_ps u_ready
            s_ps xpb_ready mean_ps mixed pyb_ps ybl_ready mb_ready ml_ready o2_ready x1l_ready g3m yo_ready raw0 raw1
            raw2 raw3 dve_step waits""".split():
            sems[name] = ctx.enter_context(nc.semaphore(name))
        s = sems

        def cfs(name):
            a, b = CF[name]
            return cf[:, a:b]

        def cms(name):
            a, b = CM[name]
            return cm[:, a:b]

        ident, istk, ones2, mean2, meand = [cfs(n) for n in ("ident", "istk", "ones2", "mean2", "meand")]

        def half(q):
            return slice(HD * q, HD * q + HD)

        def grp(t):
            return t[:, :].rearrange("p (g c) -> p g c", g=G)

        def flat(t, g):
            return t[:, g].rearrange("p h c -> p (h c)")

        def tok(g):
            return slice(C * g, C * g + C)

        w_in_v = w_in[0].rearrange("(k p) n -> p k n", p=P)
        wa_v = w_branch[0, 0].rearrange("(k p) n -> p k n", p=P)
        wb_v = w_branch[0, 1].rearrange("(k p) n -> p k n", p=P)
        wo_v = w_out[0].rearrange("(k p) n -> p k n", p=P)
        wg_v = w_ple_gate[0].rearrange("(k p) n -> p k n", p=P)
        wple_v = w_ple[0].rearrange("(k p) n -> p k n", p=P)

        block = ctx.enter_context(nc.Block())

        @block.sync
        def _(sp):
            def load(view, k0, col, count, j, free=True):
                slot = j % SLOTS
                if free:
                    sp.wait_ge(s["lo_ready"], count + j - (SLOTS - 1))
                    sp.sem_inc(s["waits"], 1)
                sp.dma_start(wraw[:, slot, :].rearrange("p (k n) -> p k n", k=KC),
                             view[:, k0:k0 + KC, ds(col, P)]).then_inc(s[f"raw{slot}"], 16)

            def load_tiles(cols, count, free):
                for n, col in enumerate(cols):
                    for h in range(2):
                        j = 2 * n + h
                        load(w_in_v, KC * h, col, count, j, free=free or j >= SLOTS)

            sp.dma_start(xt[:, 0, :], x_prompt[0, 0:P, :]).then_inc(s["x_in0"], 16)
            sp.dma_start(cf[:, :], const_f).then_inc(s["const_in"], 16)
            row = 0
            for v in [mu_rkv[0].rearrange("a (q p) -> (a q) p", p=P)] + [
                    v[0].rearrange("(q p) -> q p", p=P) for v in (w0, a0, k_k, k_a, r_k, ln_w, ln_b)]:
                n = v.shape[0]
                sp.dma_start(rows[row:row + n, 0, :], v).then_inc(s["rows_in"], 16)
                row += n
            row = 0
            for v in (norm_pre[0].rearrange("(q p) -> q p", p=P), norm_post[0].rearrange("(q p) -> q p", p=P),
                      mu_lora[0].rearrange("a (q p) -> (a q) p", p=P)[0:32, :], pool_scale[0].rearrange("(q p) -> q p", p=P)):
                n = v.shape[0]
                sp.dma_start(rows[row:row + n, 1, :], v).then_inc(s["rows_in"], 16)
                row += n
            sp.dma_start(xt[:, 1, :], x_prompt[0, P:TP, :]).then_inc(s["x_in1"], 16)
            sp.dma_start(xt[0:NB * TB, 2, :], x_sample.rearrange("b t d -> (b t) d")).then_inc(s["x_in2"], 16)
            sp.dma_start(xt[NB * TB:NB * TB + NB, 2, :], state_shift[0]).then_inc(s["x_in2"], 16)
            load_tiles((COL_K, COL_R, COL_V, COL_G), 0, free=False)
            with sp.Fori(1, PAIRS) as q:
                load_tiles([q * P + c for c in (COL_K, COL_R, COL_V, COL_G, COL_U - P, COL_GP - P)],
                           q * CH_STEP + BASE_STEP, free=True)
            load_tiles((COL_GA, COL_GB, COL_GA + P, COL_GB + P, COL_U + 7 * P, COL_GP + 7 * P),
                       PAIRS * CH_STEP + BASE_STEP, free=True)
            load_tiles((COL_GA + 2 * P, COL_GB + 2 * P, COL_GA + 3 * P, COL_GB + 3 * P), BASE_EARLY, free=True)
            for b, view in enumerate((wa_v, wb_v)):
                for i in range(EARLY):
                    load(view, 0, i * P, BASE_EARLY + 2 * EARLY, EARLY * b + i)
            with sp.Fori(EARLY // 2, KT // 2) as n:
                for m in range(2):
                    for j, (view, k0, col) in enumerate(((w_in_v, 0, COL_GA), (w_in_v, KC, COL_GA), (w_in_v, 0, COL_GB),
                                                         (w_in_v, KC, COL_GB), (wa_v, 0, 0), (wb_v, 0, 0))):
                        load(view, k0, n * (2 * P) + (m * P + col), n * (2 * CH_MERGE) + BASE_MERGE, CH_MERGE * m + j)
            for view, start in ((wo_v, BASE_OUT), (wg_v, BASE_GATE)):
                with sp.Fori(0, KT // 2) as n:
                    for m in range(2):
                        for h in range(2):
                            load(view, KC * h, n * (2 * P) + m * P, n * 4 + start, 2 * m + h)

        @block.gpsimd
        def _(pool):
            gp_ = nc.gpsimd

            def wait_alone(name, value):
                pool.wait_ge(s[name], value)
                pool.sem_inc(s["waits"], 1)

            pool.wait_ge(s["x_in1"], 16)
            pool.dma_start(cm[:, :], const_m).then_inc(s["map_in"], 16)
            pool.dma_start(lw1[:, :, :], w1[0].rearrange("(k p) n -> p k n", p=P)).then_inc(s["map_in"], 16)
            pool.dma_start(la1[:, :, :], a1[0].rearrange("(k p) n -> p k n", p=P)).then_inc(s["map_in"], 16)
            gp_.memset(zsh[:, 0:1], 0.0).then_inc(s["zeroed"], 1)

            def pair_params(q):
                gp_.tensor_copy(cur_p[:, :], par[:, :].rearrange("p (n q) -> p n q", q=PAIRS)[:, :, ds(q, 1)]
                                .rearrange("p n q -> p (n q)")).then_inc(s["cur_p_ready"], 1)

            def pair_loads(q):
                pool.dma_start(lw2[:, :], w2[0][:, ds(q * P, P)]).then_inc(s["lw2_in"], 16)
                pool.dma_start(la2[:, :], a2[0][:, ds(q * P, P)]).then_inc(s["lw2_in"], 16)
                for h in range(2):
                    pool.dma_start(S0n[half(h), :, half(h)],
                                   state_wkv[0].rearrange("b h i j -> i b h j")[:, :, ds(q * 2 + h, 1), :]
                                   .rearrange("i b h j -> i b (h j)")).then_inc(s["s0_in"], 16)

            pool.wait_ge(s["par_done"], 4)
            pair_params(0)
            for j in range(SLOTS):
                pool.wait_ge(s["hi_ready"], j + 1)
                gp_.tensor_tensor(wl[:, j, :], wraw[:, j, :], wh[:, j, :].bitcast(F32), ALU.subtract).then_inc(s["lo_ready"], 1)
            pool.wait_ge(s["hT_ps"], 12)
            gp_.memset(S0n[:], 0.0).then_inc(s["zeroed"], 1)
            pool.wait_ge(s["zeroed"], 2)
            pair_loads(0)
            for c in (2, 3):
                pool.wait_ge(s["hh_done"], c + 1)
                gp_.tensor_tensor(hl[:, 4 * c * TS:4 * (c + 1) * TS], hT[:, 4 * c * TS:4 * (c + 1) * TS],
                                  hh[:, 4 * c * TS:4 * (c + 1) * TS].bitcast(F32), ALU.subtract).then_inc(s["hl_done"], 1)
            pool.wait_ge(s["last_done"], 2)
            for n in range(2):
                src = hlastT[:, P * n:P * (n + 1)]
                pool.dma_start(shift_prompt[0, 0].rearrange("(k p) -> k p", p=P)[8 * n:8 * n + 8, :],
                               src[0:8, :]).then_inc(s["rows_out"], 16)
                for k in range(8):
                    pool.dma_start(shift_sample[0, :, P * (8 * n + k):P * (8 * n + k + 1)],
                                   src[8 + NB * k:8 + NB * (k + 1), :]).then_inc(s["rows_out"], 16)
            pool.wait_ge(s["rows_out"], 16 * 18)
            pool.wait_ge(s["xw_ready"], 2 * KT)
            pool.wait_ge(s["xw_used"], 2 * KT)
            blocks = (vBD, aBD, bBD, kBD, YBD, ZaBD, EndBD)
            for t in blocks:
                gp_.memset(t[:], 0.0).then_inc(s["zeroed"], 1)
            pool.wait_ge(s["zeroed"], 2 + len(blocks))

            def mix(r):
                gp_.tensor_copy(cur_m[:, :], par[:, :].rearrange("p (n q) -> p n q", q=PAIRS)[:, :, ds(r, 1)]
                                .rearrange("p n q -> p (n q)")).then_inc(s["cur_m_ready"], 1)
                wait_alone("cur_m_ready", r + 1)
                wait_alone("acc_free", r * TILES_STEP + (ACC_STEP + TILES_STEP))
                for h in range(2):
                    gp_.tensor_copy(vBD[half(h), :, h, :], grp(vS)[half(h)]).then_inc(s["vbd_ready"], 1)
                wait_alone("vbd_ready", r * 2 + 2)
                wait_alone("a_ready", r + 1)
                gp_.tensor_scalar(kf[:, :], aS[:, :], cur_m[:, K_A:K_A + 1], cur_m[:, OM_KA:OM_KA + 1],
                                  ALU.mult, ALU.add).then_inc(s["kf_ready"], 1)
                wait_alone("kf_ready", r * 2 + 1)
                gp_.tensor_tensor(kf[:, :], kf[:, :], kS[:, :], ALU.mult).then_inc(s["kf_ready"], 1)
                wait_alone("sg_ready", r + 1)
                gp_.tensor_tensor(sg[:, :], sg[:, :], gS[:, :], ALU.mult).then_inc(s["sgs_ready"], 1)
                wait_alone("exp_ready", r * 3 + 3)
                gp_.tensor_tensor(aS[:, :], aS[:, :], pi[:, :], ALU.mult).then_inc(s["api_ready"], 1)
                wait_alone("api_ready", r + 1)
                for h in range(2):
                    gp_.tensor_tensor(kBD[half(h), :, h, :], grp(kf)[half(h)], grp(pi)[half(h)],
                                      ALU.mult).then_inc(s["kbd_ready"], 1)
                wait_alone("kbd_ready", r * 2 + 2)

            def mix_sample(r):
                wait_alone("bbd_ready", r * 2 + 2)
                pl = pd[:, TP:T].rearrange("p (b t) -> p b t", t=TB)[:, :, TB - 1:TB]
                for n, t in enumerate((bBD, kBD)):
                    gp_.tensor_tensor(tail4[:, n].rearrange("p h (b t) -> p h b t", t=TB),
                                      t[:, G - 1].rearrange("p h (b t) -> p h b t", t=TB),
                                      pl.unsqueeze(1).to_broadcast([P, 2, NB, TB]), ALU.mult).then_inc(s["tail_ready"], 1)
                gp_.tensor_tensor(dPL[:, :, :], istk.unsqueeze(1).to_broadcast([P, NB, C]),
                                  pl.to_broadcast([P, NB, C]), ALU.mult).then_inc(s["dpl_ready"], 1)

            def mix_out(r):
                wait_alone("tails_ready", r * 2 + 2)
                bm = cfs("batch").unsqueeze(2).to_broadcast([P, NB, C])
                gp_.tensor_tensor(xpK[:, :, :], tails[:, 1, :].unsqueeze(1).to_broadcast([P, NB, C]), bm,
                                  ALU.mult).then_inc(s["xpk_ready"], 1)
                wait_alone("end_ready", r + 1)
                for h in range(2):
                    pool.dma_start(wkv_prompt[0, 0][ds(r * 2 + h, 1)].rearrange("h i j -> (h i) j"),
                                   eo[half(h), half(h)]).then_inc(s["eout"], 16)
                wait_alone("send_ready", r + 1)
                for h in range(2):
                    pool.dma_start(wkv_sample[0].rearrange("b h i j -> i b h j")[:, :, ds(r * 2 + h, 1), :]
                                   .rearrange("i b h j -> i b (h j)"), so[half(h), :, :]).then_inc(s["sout"], 16)
                wait_alone("eout", r * 32 + 32)
                wait_alone("sout", r * 32 + 32)

            with pool.Fori(1, PAIRS) as q:
                r = q - 1
                wait_alone("acc_free", q * TILES_STEP + ACC_STEP)
                pair_params(q)
                mix(r)
                mix_sample(r)
                wait_alone("lora2_ps", q)
                wait_alone("s0_ps", q)
                pair_loads(q)
                mix_out(r)
            pool.wait_ge(s["acc_free"], PAIRS * TILES_STEP + ACC_STEP)
            mix(PAIRS - 1)
            mix_sample(PAIRS - 1)
            mix_out(PAIRS - 1)

            pool.wait_ge(s["y_done"], PAIRS)
            pool.dma_start(spt[:, :], state_pool[0].rearrange("b t c -> (b t) c")).then_inc(s["pool_in"], 16)
            gp_.memset(ue[:, :, 0:BUF], 0.0).then_inc(s["zeroed"], 1)
            pool.dma_start(pw[:, :, :], pool_w[0].rearrange("g (k p) n -> p (g k) n", p=P)).then_inc(s["map_in"], 16)
            pool.dma_start(pool_sample[0, :, 0:BUF - TB, :], state_pool[0, :, TB:BUF, :]).then_inc(s["rows_out"], 16)
            pool.wait_ge(s["yah_ready"], 1)
            gp_.tensor_tensor(yal[:, :], yf[:, :], yah[:, :].bitcast(F32), ALU.subtract).then_inc(s["yal_ready"], 1)
            pool.wait_ge(s["gsig_ready"], 1)
            gp_.tensor_tensor(gp[:, :, :].rearrange("p k t -> p (k t)"), gp[:, :, :].rearrange("p k t -> p (k t)"),
                              gsig[:, :], ALU.mult).then_inc(s["gsil_ready"], 1)
            pool.wait_ge(s["utok_ev"], 2)
            pool.dma_start(pool_prompt[0, 0], utok[0:BUF, :]).then_inc(s["rows_out"], 16)
            for b in range(NB):
                pool.dma_start(pool_sample[0, b, BUF - TB:BUF, :],
                               utok[BUF + TB * b:BUF + TB * (b + 1), :]).then_inc(s["rows_out"], 16)
            pool.wait_ge(s["rows_out"], 16 * (18 + 1 + 1 + NB))

            pool.wait_ge(s["chunk_used"], BASE_OUT)
            pool.dma_start(xt2[:, 0, :], x_prompt[0, 0:P, :]).then_inc(s["x2_in"], 16)
            pool.dma_start(xt2[:, 1, :], x_prompt[0, P:TP, :]).then_inc(s["x2_in"], 16)
            pool.dma_start(xt2[0:NB * TB, 2, :], x_sample.rearrange("b t d -> (b t) d")).then_inc(s["x2_in"], 16)
            pool.dma_start(pt[:, 0, :], p_prompt[0, 0, 0:P, :]).then_inc(s["x2_in"], 16)
            pool.dma_start(pt[:, 1, :], p_prompt[0, 0, P:TP, :]).then_inc(s["x2_in"], 16)
            pool.dma_start(pt[0:NB * TB, 2, :], p_sample[0].rearrange("b t d -> (b t) d")).then_inc(s["x2_in"], 16)
            for m in range(2):
                pool.dma_start(wple[:, m, :].rearrange("p (k n) -> p k n", k=2),
                               wple_v[:, :, m * P:(m + 1) * P]).then_inc(s[f"wple_in{m}"], 16)
            for k in range(KT):
                pool.wait_ge(s["xT_ready"], k + 1)
                pool.wait_ge(s["x1a"], k + 1)
                gp_.tensor_tensor(xT[:, T * k:T * (k + 1)], xT[:, T * k:T * (k + 1)], o2[:, T * k:T * (k + 1)],
                                  ALU.add).then_inc(s["x1b"], 1)

            def store(n, m):
                wait_alone("ytk_ready", n * 4 + 2 * m + 2)
                col = n * (2 * P) + m * P
                pool.dma_start(y_prompt[0].rearrange("(a p) d -> p a d", p=P)[:, :, ds(col, P)],
                               ytk[:, m, 0:2 * P].rearrange("p (a n) -> p a n", a=2)).then_inc(s[f"y_out{m}"], 16)
                pool.dma_start(y_sample.rearrange("b t d -> (b t) d")[:, ds(col, P)],
                               ytk[0:NB * TB, m, 2 * P:3 * P]).then_inc(s[f"y_out{m}"], 16)

            with pool.Fori(0, KT // 2 - 1) as n:
                for m in range(2):
                    wait_alone("ple_ps", n * 2 + m + 1)
                    pool.dma_start(wple[:, m, :].rearrange("p (k n) -> p k n", k=2),
                                   wple_v[:, :, ds(n * (2 * P) + (m + 2) * P, P)]).then_inc(s[f"wple_in{m}"], 16)
                    store(n, m)
            for m in range(2):
                store(KT // 2 - 1, m)
            pool.wait_ge(s["y_out0"], 16 * KT)
            pool.wait_ge(s["y_out1"], 16 * KT)

        @block.scalar
        def _(act):
            A = nc.scalar

            def split_hi(count, j, rounds):
                slot = j % SLOTS
                act.wait_ge(s[f"raw{slot}"], rounds * 16 + 16)
                if not (isinstance(count, int) and count + j < SLOTS):
                    act.wait_ge(s["chunk_used"], count + j - (SLOTS - 1))
                A.copy(wh[:, slot, :], wraw[:, slot, :]).then_inc(s["hi_ready"], 1)

            def ahead(count, rounds, j):
                jj = j + AHEAD
                split_hi(count, jj, rounds + jj // SLOTS)

            def evac_mixed(mu, bank, used_chunks, last):
                act.wait_ge(s["chunk_used"], used_chunks)
                act.wait_ge(s["acc_free"], last)
                act.wait_ge(s["cur_p_ready"], mu[1])
                m = cur_p[:, mu[0]:mu[0] + 1]
                A.mul(zsh[:, 1:TP], bank[:, 0:TP - 1], m)
                zb = zsh[:, TP:T].rearrange("p (b t) -> p b t", t=TB)
                A.mul(zb[:, :, 1:TB], bank[:, TP:T].rearrange("p (b t) -> p b t", t=TB)[:, :, 0:TB - 1], m)
                A.mul(zb[:, :, 0], bank[:, T:TS], m).then_inc(s["zsh_ready"], 1)

            act.wait_ge(s["const_in"], 16)
            for t in range(3):
                n = P if t < 2 else NB * TB
                act.wait_ge(s[f"x_in{t}"], 16 if t < 2 else 32)
                A.activation(hT[0:n, 0:D], xt[0:n, t, :], ACT.Square, accum_out=stat[0:n, t:t + 1]).then_inc(s["x_stat"], 1)
                act.wait_ge(s["x_stat"], 2 * t + 1)
                A.activation(stat[0:n, t:t + 1], stat[0:n, t:t + 1], ACT.Sqrt, scale=1.0 / D,
                             bias=cfs("eps")[0:n, 0:1]).then_inc(s["x_stat"], 1)
            for j in range(SLOTS):
                split_hi(0, j, 0)
            for c in range(4):
                act.wait_ge(s["hT_done"], 8 + 2 * (c + 1))
                A.copy(hh[:, 4 * c * TS:4 * (c + 1) * TS], hT[:, 4 * c * TS:4 * (c + 1) * TS]).then_inc(s["hh_done"], 1)
            act.wait_ge(s["dh_done"], 4)
            act.wait_ge(s["last_ps"], 2)
            A.copy(hlastT[:, 0:P], B[4][0:72, 0:P]).then_inc(s["last_done"], 1)
            A.copy(hlastT[:, P:2 * P], B[5][0:72, 0:P]).then_inc(s["last_done"], 1)

            def tile_out(q, n):
                if n < 3 and not isinstance(q, int):
                    evac_mixed(((MU_K, MU_R, MU_V)[n], q + 1), acc[n % 2], q * CH_STEP + (BASE_STEP + 2 * n + 2),
                               q * TILES_STEP + (ACC_STEP + n))

            for j in range(CH_FIRST):
                if j + AHEAD >= SLOTS:
                    ahead(0, 0, j)
                if j % 2 == 1 and j < 7:
                    n = j // 2
                    act.wait_ge(s["chunk_used"], 2 * n + 2)
                    if n:
                        act.wait_ge(s["acc_free"], n)
                    act.wait_ge(s["cur_p_ready"], 1)
                    act.wait_ge(s["zeroed"], 1)
                    m = cur_p[:, (MU_K, MU_R, MU_V)[n]:(MU_K, MU_R, MU_V)[n] + 1]
                    bank = acc[n % 2]
                    A.mul(zsh[:, 1:TP], bank[:, 0:TP - 1], m)
                    zb = zsh[:, TP:T].rearrange("p (b t) -> p b t", t=TB)
                    A.mul(zb[:, :, 1:TB], bank[:, TP:T].rearrange("p (b t) -> p b t", t=TB)[:, :, 0:TB - 1], m)
                    A.mul(zb[:, :, 0], bank[:, T:TS], m).then_inc(s["zsh_ready"], 1)
            act.wait_ge(s["xw_used"], 2 * KT)
            A.activation(t1[:, :], B[0][0:RANK, 0:T], ACT.Tanh).then_inc(s["lora_act"], 1)
            A.copy(la[:, :], B[1][0:RANK, 0:T]).then_inc(s["lora_act"], 1)

            def mix(r, q):
                def go(j):
                    ahead(q * CH_STEP + BASE_STEP, q * (CH_STEP // SLOTS) + BASE_STEP // SLOTS, j)

                def out(n):
                    tile_out(q, n)

                go(0)
                act.wait_ge(s["s0_ps"], r + 1)
                A.copy(S0T[:, :, :].rearrange("p b c -> p (b c)"), B45[:, :]).then_inc(s["s0t_ready"], 1)
                act.wait_ge(s["cur_m_ready"], r + 1)
                A.activation(sq[:, :], kS[:, :], ACT.Square, scale=cur_m[:, K_K:K_K + 1]).then_inc(s["ksq_ready"], 1)
                act.wait_ge(s["lora2_ps"], r + 1)
                A.activation(pm[:, :], B[0][:, 0:T], ACT.Sigmoid, bias=cur_m[:, W0:W0 + 1]).then_inc(s["decay_in"], 1)
                A.activation(aS[:, :], B[1][:, 0:T], ACT.Sigmoid, bias=cur_m[:, A0:A0 + 1]).then_inc(s["a_ready"], 1)
                A.activation(sg[:, :], gS[:, :], ACT.Sigmoid).then_inc(s["sg_ready"], 1)
                act.wait_ge(s["kk_max"], r + 1)
                A.activation(rn[:, :], rn[:, :], ACT.Sqrt).then_inc(s["kk_norm"], 1)
                act.wait_ge(s["cum_ready"], r + 1)
                A.activation(pi[:, :], cl[:, :], ACT.Exp, scale=DECAY).then_inc(s["exp_ready"], 1)
                A.activation(pd[:, :], cl[:, :], ACT.Exp, scale=-DECAY).then_inc(s["exp_ready"], 1)
                act.wait_ge(s["cumx_ready"], r + 1)
                A.activation(pm[:, :], pm[:, :], ACT.Exp, scale=-DECAY).then_inc(s["exp_ready"], 1)
                go(1)
                act.wait_ge(s["vt_ps"], r + 1)
                A.copy(VtBD[:, :, :, :].rearrange("p g h c -> p (g h c)"), B45[:, 0:2 * T])
                for h in range(2):
                    A.copy(Vs[half(h)], B45[half(h), 0:2 * T].rearrange("p (g h c) -> p g h c", g=G, h=2)[:, :, h, :]
                           ).then_inc(s["vs_ready"], 1)
                act.wait_ge(s["ah_ready"], r + 1)
                for h in range(2):
                    A.copy(aBD[half(h), :, h, :], ar[half(h), 0, :].rearrange("p (g c) -> p g c", g=G))
                act.wait_ge(s["bh_ready"], r + 1)
                for h in range(2):
                    A.copy(bBD[half(h), :, h, :], grp(bU)[half(h)]).then_inc(s["bbd_ready"], 1)
                go(2)
                out(0)
                act.wait_ge(s["z_ps"], r + 1)
                A.copy(Zs[:, :, :].rearrange("p a c -> p (a c)"), B[5][:, 0:2 * C])
                for h in range(2):
                    A.copy(ZaBD[half(h), h, :], B[5][half(h), 0:C]).then_inc(s["zabd_ready"], 1)
                go(3)
                act.wait_ge(s["bt_ps"], r + 1)
                A.copy(BtBD[:, :, :, :].rearrange("p g h c -> p (g h c)"), B45[:, 0:2 * T]).then_inc(s["bt_ready"], 1)

                def ybd(n):
                    gs = G if n <= SMALL else GP
                    act.wait_ge(s["y_ready"], r * (LEVELS + 1) + n + 1)
                    for h in range(2):
                        A.copy(YBD[half(h), 0:gs, h, :], Y[half(h), 0:gs]).then_inc(s["ybd_ready"], 1)

                def xbd(n):
                    gs = G if n < SMALL else GP
                    act.wait_ge(s["x_ps"], r * LEVELS + n + 1)
                    A.copy(XBD[:, 0:gs].rearrange("p g h c -> p (g h c)"), B45[:, 0:2 * C * gs]).then_inc(s["x_ready"], 1)

                ybd(0)
                xbd(0)
                act.wait_ge(s["kt_ps"], r + 1)
                A.copy(KtBD[:, :, :, :].rearrange("p g h c -> p (g h c)"), B23[:, 0:2 * T]).then_inc(s["kt_ready"], 1)
                go(4)
                out(1)
                for n in range(1, LEVELS):
                    ybd(n)
                    xbd(n)
                    if n > 1:
                        go(3 + n)
                    if n == 3:
                        out(2)
                ybd(LEVELS)
                act.wait_ge(s["tail_ps"], r + 1)
                for h in range(2):
                    A.copy(tails[half(h)], B[5][half(h), 0:4 * C].rearrange("p (n h c) -> p n h c", n=2, h=2)[:, :, h, :]
                           ).then_inc(s["tails_ready"], 1)
                for g in range(GP):
                    if g:
                        act.wait_ge(s["s_ready"], r * GP + g)
                        A.mul(Sd[:, :], Ss[:, g - 1, :], pd[:, C * g + C - 1:C * g + C]).then_inc(s["sd_ready"], 1)
                    if g in (1, 3):
                        go(8 + g // 2)
                act.wait_ge(s["u_ready"], r * GP + GP)
                for h in range(2):
                    A.copy(UBD[half(h), :, h, :], Us[half(h)]).then_inc(s["ubd_ready"], 1)
                act.wait_ge(s["s_ready"], r * GP + GP)
                for h in range(2):
                    A.copy(SBD[half(h), 0:GP - 1, h, :], Ss[half(h), 0:GP - 1, :]).then_inc(s["sbd_ready"], 1)
                for h in range(2):
                    A.copy(EndBD[half(h), h, :], Ss[half(h), GP - 1, :]).then_inc(s["endbd_ready"], 1)
                go(10)
                act.wait_ge(s["o_ps"], r + 1)
                A.copy(O_s[:, :], B[4][:, 0:T]).then_inc(s["o_ready"], 1)
                act.wait_ge(s["end_ps"], r + 1)
                A.copy(eo[:, :], B[0][:, 0:P]).then_inc(s["end_ready"], 1)
                act.wait_ge(s["send_ps"], r + 1)
                A.copy(so[:, :, :].rearrange("p b c -> p (b c)"), B[3][:, :]).then_inc(s["send_ready"], 1)
                act.wait_ge(s["dev_ready"], r + 1)
                A.activation(dsq[:, :], dO[:, :], ACT.Square).then_inc(s["dsq_ready"], 1)
                go(11)
                act.wait_ge(s["var_ps"], r + 1)
                A.activation(sd[:, :], B[2][:, 0:T], ACT.Sqrt, bias=cfs("eps")[:, 1:2]).then_inc(s["sd_done"], 1)

            with act.Fori(1, PAIRS) as q:
                mix(q - 1, q)
            mix(PAIRS - 1, PAIRS)

            def early(j):
                ahead(BASE_EARLY, BASE_EARLY // SLOTS, j)

            early(0)
            act.wait_ge(s["y_done"], PAIRS)
            A.copy(yah[:, :], yf[:, :]).then_inc(s["yah_ready"], 1)
            act.wait_ge(s["acc_free"], ACC_ALL)
            early(1)
            for t in (kS, rS, vS, gS):
                A.activation(t[:, :], t[:, :], ACT.Sigmoid).then_inc(s["sb_ready"], 1)
            act.wait_ge(s["eout"], 32 * PAIRS)
            act.wait_ge(s["sout"], 32 * PAIRS)
            A.activation(gsig[:, :], gp[:, :, :].rearrange("p k t -> p (k t)"), ACT.Sigmoid).then_inc(s["gsig_ready"], 1)
            for j in range(2, 10):
                if j % 2 == 0:
                    g = j // 2 - 1
                    act.wait_ge(s["chunk_used"], BASE_EARLY + j)
                    A.activation(gt[:, g, :], acc[g % 2][:, 0:T], ACT.Sigmoid).then_inc(s["gates_ready"], 1)
                early(j)
                if j == 3:
                    act.wait_ge(s["utok_ps"], 4)
                    for n in range(2):
                        A.copy(utok[:, 512 * n:512 * (n + 1)], B[4 + n][0:NB * TB + BUF, :]).then_inc(s["utok_ev"], 1)

            def high_y(m):
                act.wait_ge(s["yb_ready"], m + 1)
                A.copy(ybh[:, m * T:(m + 1) * T], ytmp[:, m % 2, :]).then_inc(s["yb_done"], 1)

            for m in range(4):
                high_y(m)
            early(10)
            for m in range(4, 8):
                high_y(m)
            for j in range(11, 16):
                early(j)
                if j >= 13:
                    i = j - 13
                    act.wait_ge(s["m_ready"], i + 1)
                    A.copy(mh[:, T * i:T * (i + 1)], mm_[:, i % 2, :]).then_inc(s["mh_ready"], 1)
            act.wait_ge(s["m_ready"], EARLY)
            A.copy(mh[:, T * 3:T * 4], mm_[:, 1, :]).then_inc(s["mh_ready"], 1)

            with act.Fori(EARLY // 2, KT // 2) as n:
                for m in range(2):
                    i = n * 2 + m
                    bank = [acc[0], acc[1]] if m == 0 else [B[2], B[3]]
                    for j in range(CH_MERGE):
                        ahead(n * (2 * CH_MERGE) + BASE_MERGE, n * (2 * CH_MERGE // SLOTS) + BASE_MERGE // SLOTS,
                              CH_MERGE * m + j)
                        if j == 2:
                            act.wait_ge(s["chunk_used"], i * CH_MERGE + BASE_MERGE + 2)
                            A.activation(ga[:, m, :], bank[0][:, 0:T], ACT.Sigmoid)
                        if j == 4:
                            act.wait_ge(s["chunk_used"], i * CH_MERGE + BASE_MERGE + 4)
                            A.activation(gb[:, m, :], bank[1][:, 0:T], ACT.Sigmoid).then_inc(s["sb_ready"], 1)
                    act.wait_ge(s["m_ready"], i + 1)
                    A.copy(mh[:, ds(n * (2 * T) + m * T, T)], mm_[:, m, :]).then_inc(s["mh_ready"], 1)

            def square_tile(n, m):
                i = n * 2 + m
                for h in range(2):
                    ahead(n * 4 + BASE_OUT, n + BASE_OUT // SLOTS, 2 * m + h)
                act.wait_ge(s["chunk_used"], i * 2 + (BASE_OUT + 2))
                A.activation(sqo[:, m, :], acc[m][:, 0:T], ACT.Square).then_inc(s["so_ready"], 1)

            for m in range(2):
                square_tile(0, m)
            for k in range(KT):
                act.wait_ge(s["xT_ps"], k + 1)
                A.copy(xT[:, T * k:T * (k + 1)], B[k % 4][:, 0:T]).then_inc(s["xT_ready"], 1)
            for k in range(2):
                act.wait_ge(s["pT_ps"], k + 1)
                A.copy(pT[:, k, :], B[4 + k][:, 0:T]).then_inc(s["pT_ready"], 1)
            with act.Fori(1, KT // 2) as n:
                for m in range(2):
                    act.wait_ge(s["sacc_ready"], n * 2 + m - 1)
                    square_tile(n, m)
            act.wait_ge(s["ssq_ps"], 1)
            A.activation(sacc[:, :], B[5][:, 0:T], ACT.Sqrt, bias=cfs("eps")[:, 0:1]).then_inc(s["srt"], 1)
            for k in range(KT):
                act.wait_ge(s["x1b"], k + 1)
                A.copy(x1h[:, T * k:T * (k + 1)], xT[:, T * k:T * (k + 1)]).then_inc(s["x1h_ready"], 1)

            def gate_tile(n, m, last=False):
                i = n * 2 + m
                for h in range(2):
                    if not last or 2 * m + h + AHEAD < 4:
                        ahead(n * 4 + BASE_GATE, n + BASE_GATE // SLOTS, 2 * m + h)
                act.wait_ge(s["chunk_used"], i * 2 + (BASE_GATE + 2))
                A.activation(g3[:, m, :], acc[m][:, 0:T], ACT.Sigmoid).then_inc(s["g3_ready"], 1)

            def token_tile(i, m, stored=None):
                act.wait_ge(s["yt_ps"], i + 1)
                if stored is not None:
                    act.wait_ge(s[f"y_out{m}"], stored)
                A.copy(ytk[:, m, 0:2 * P], B[2 + m][:, 0:2 * P]).then_inc(s["ytk_ready"], 1)
                A.copy(ytk[0:NB * TB, m, 2 * P:3 * P], B[2 + m][0:NB * TB, 2 * P:3 * P]).then_inc(s["ytk_ready"], 1)

            gate_tile(0, 0)
            gate_tile(0, 1)
            token_tile(0, 0)
            gate_tile(1, 0)
            token_tile(1, 1)
            gate_tile(1, 1)
            token_tile(2, 0, 32)
            with act.Fori(2, KT // 2 - 1) as n:
                gate_tile(n, 0)
                token_tile(n * 2 - 1, 1, n * 32 - 32)
                gate_tile(n, 1)
                token_tile(n * 2, 0, n * 32)
            n = KT // 2 - 1
            gate_tile(n, 0, last=True)
            token_tile(n * 2 - 1, 1, n * 32 - 32)
            gate_tile(n, 1, last=True)
            token_tile(n * 2, 0, n * 32)
            token_tile(n * 2 + 1, 1, n * 32)

        @block.vector
        def _(dve):
            V = nc.vector

            def split_lo(count, j):
                slot = j % SLOTS
                dve.wait_ge(s["hi_ready"], count + j + 1)
                V.tensor_tensor(wl[:, slot, :], wraw[:, slot, :], wh[:, slot, :].bitcast(F32), ALU.subtract
                                ).then_inc(s["lo_ready"], 1)

            def ahead(count, j):
                split_lo(count, j + AHEAD)

            def tile_out(q, n):
                if isinstance(q, int) and q == 0:
                    used_chunks = 2 * n + 2
                else:
                    used_chunks = q * CH_STEP + (BASE_STEP + 2 * n + 2)
                dve.wait_ge(s["chunk_used"], used_chunks)
                bank = acc[n % 2][:, 0:T]
                if n < 3 and not (isinstance(q, int) and q == PAIRS):
                    dve.wait_ge(s["zsh_ready"], q * 3 + n + 1)
                    V.scalar_tensor_tensor((kS, rS, vS)[n][:, :], bank, cur_p[:, (OM_K, OM_R, OM_V)[n]:(OM_K, OM_R, OM_V)[n] + 1],
                                           zsh[:, :], ALU.mult, ALU.add).then_inc(s["acc_free"], 1)
                elif n < 4:
                    V.tensor_copy((kS, rS, vS, gS)[n][:, :], bank).then_inc(s["acc_free"], 1)
                else:
                    t = (uS, gp)[n - 4][:, :, :].rearrange("p k t -> p (k t)")
                    where = slice(T * (q - 1), T * q) if isinstance(q, int) else ds(q * T - T, T)
                    V.tensor_copy(t[:, where], bank).then_inc(s["acc_free"], 1)

            dve.wait_ge(s["par_ready"], 2)
            V.tensor_copy(par[:, 0:NROW * PAIRS], B[4][:, 0:NROW * PAIRS]).then_inc(s["par_done"], 1)
            V.tensor_copy(par2[:, :], B[5][:, 0:NPAR2]).then_inc(s["par_done"], 1)
            dve.wait_ge(s["par_done"], 2)
            V.tensor_scalar(par[:, OM_R * PAIRS:(OM_V + 1) * PAIRS], par[:, 0:3 * PAIRS], -1.0, 1.0,
                            ALU.mult, ALU.add).then_inc(s["par_done"], 1)
            V.tensor_scalar(par[:, OM_KA * PAIRS:(OM_KA + 1) * PAIRS], par[:, K_A * PAIRS:(K_A + 1) * PAIRS], -1.0, 1.0,
                            ALU.mult, ALU.add).then_inc(s["par_done"], 1)
            hTv = hT[:, :].rearrange("p (k t) -> p k t", t=TS)
            hhv = hh[:, :].rearrange("p (k t) -> p k t", t=TS)
            hlv = hl[:, :].rearrange("p (k t) -> p k t", t=TS)

            def h_rows(t):
                n = P if t < 2 else NB * TB
                if t == 2:
                    dve.wait_ge(s["hT_ps"], 4)
                dve.wait_ge(s["x_stat"], 2 * t + 2)
                V.reciprocal(stat[0:n, t:t + 1], stat[0:n, t:t + 1]).then_inc(s["chain"], 1)
                dve.wait_ge(s["chain"], t + 1)
                V.tensor_scalar(ht[0:n, t % 2, :], xt[0:n, t, :], stat[0:n, t:t + 1], None, ALU.mult).then_inc(s["h_rows"], 1)
                if t == 2:
                    V.tensor_copy(ht[n:n + NB, 0, :], xt[n:n + NB, 2, :]).then_inc(s["h_rows"], 1)

            def h_columns(t):
                for c in range(4):
                    dve.wait_ge(s["hT_ps"], 4 * t + c + 1)
                    n = P if t < 2 else NB * TB
                    src = B[c][:, :].rearrange("p (k t) -> p k t", t=P)
                    V.tensor_tensor(hTv[:, 4 * c:4 * c + 4, P * t:P * t + n], src[:, :, 0:n],
                                    par2[:, NPRE + 4 * c:NPRE + 4 * c + 4].unsqueeze(2).to_broadcast([P, 4, n]),
                                    ALU.mult).then_inc(s["hT_done"], 1)
                    if t == 2:
                        V.tensor_copy(hTv[:, 4 * c:4 * c + 4, T:TS], src[:, :, n:n + NB]).then_inc(s["hT_done"], 1)

            h_rows(0)
            h_rows(1)
            dve.wait_ge(s["par_done"], 4)
            dve.wait_ge(s["x_stat"], 6)
            h_columns(0)
            h_rows(2)
            h_columns(1)
            h_columns(2)
            for c in range(2):
                dve.wait_ge(s["hh_done"], c + 1)
                V.tensor_tensor(hl[:, 4 * c * TS:4 * (c + 1) * TS], hT[:, 4 * c * TS:4 * (c + 1) * TS],
                                hh[:, 4 * c * TS:4 * (c + 1) * TS].bitcast(F32), ALU.subtract).then_inc(s["h_split"], 1)
            dve.wait_ge(s["lo_ready"], SLOTS)
            dve.wait_ge(s["hT_done"], 16)
            for n in range(2):
                V.tensor_copy(hlast[:, 72 * n:72 * n + 8], hTv[:, 8 * n:8 * n + 8, TP - 1]).then_inc(s["dh_done"], 1)
                V.tensor_copy(hlast[:, 72 * n + 8:72 * n + 72].rearrange("p (k b) -> p k b", b=NB),
                              hTv[:, 8 * n:8 * n + 8, TP + TB - 1:T:TB]).then_inc(s["dh_done"], 1)
            dhv = dh[:, :].rearrange("p (k t) -> p k t", t=T)
            V.tensor_scalar(dhv[:, :, 0:1], hTv[:, :, 0:1], -1.0, None, ALU.mult).then_inc(s["dh_done"], 1)
            V.tensor_tensor(dhv[:, :, 1:TP], hTv[:, :, 0:TP - 1], hTv[:, :, 1:TP], ALU.subtract).then_inc(s["dh_done"], 1)
            for b in range(NB):
                a = TP + TB * b
                V.tensor_tensor(dhv[:, :, a + 1:a + TB], hTv[:, :, a:a + TB - 1], hTv[:, :, a + 1:a + TB],
                                ALU.subtract).then_inc(s["dh_done"], 1)
            V.tensor_tensor(dhv[:, :, TP:T:TB], hTv[:, :, T:TS], hTv[:, :, TP:T:TB], ALU.subtract).then_inc(s["dh_done"], 1)
            dve.wait_ge(s["dh_done"], 4 + NB + 3)
            dve.wait_ge(s["map_in"], 48)
            for j in range(CH_FIRST):
                if j + AHEAD >= SLOTS:
                    ahead(0, j)
                for k in MAP_TILES[j]:
                    for m, mu in enumerate((MUW, MUA)):
                        n = 2 * k + m
                        if n >= 4:
                            dve.wait_ge(s["xw_used"], n - 3)
                        V.scalar_tensor_tensor(xw[:, n % 4, :], dhv[:, k, :], par2[:, mu + k:mu + k + 1], hTv[:, k, 0:T],
                                               ALU.mult, ALU.add).then_inc(s["xw_ready"], 1)
                if j % 2 == 1:
                    tile_out(0, j // 2)

            def mix(r, q):
                def go(j):
                    ahead(q * CH_STEP + BASE_STEP, j)

                def out(n):
                    tile_out(q, n)

                go(0)
                dve.wait_ge(s["kk_ps"], r + 1)
                V.tensor_scalar(rn[:, :], B[2][:, 0:T], 1e-24, None, ALU.max).then_inc(s["kk_max"], 1)
                dve.wait_ge(s["decay_in"], r + 1)
                V.tensor_tensor_scan(cl[:, :], cfs("segment"), pm[:, :], 0.0, ALU.mult, ALU.add).then_inc(s["cum_ready"], 1)
                dve.wait_ge(s["cum_ready"], r + 1)
                V.tensor_tensor(pm[:, :], cl[:, :], pm[:, :], ALU.subtract).then_inc(s["cumx_ready"], 1)
                dve.wait_ge(s["kk_norm"], r + 1)
                V.reciprocal(rn[:, :], rn[:, :]).then_inc(s["kk_rn"], 1)
                dve.wait_ge(s["cur_m_ready"], r + 1)
                dve.wait_ge(s["kf_ready"], r * 2 + 2)
                V.scalar_tensor_tensor(sq[:, :], rS[:, :], cur_m[:, R_K:R_K + 1], kf[:, :], ALU.mult, ALU.mult
                                       ).then_inc(s["rk_ready"], 1)
                dve.wait_ge(s["kk_rn"], r + 1)
                V.scalar_tensor_tensor(kkn[:, :], kS[:, :], cur_m[:, K_K:K_K + 1], rn[:, :], ALU.mult, ALU.mult
                                       ).then_inc(s["kkn_ready"], 1)
                dve.wait_ge(s["kkn_ready"], r + 1)
                dve.wait_ge(s["exp_ready"], r * 3 + 3)
                V.scalar_tensor_tensor(ar[:, 0, :], kkn[:, :], -1.0, pm[:, :], ALU.mult, ALU.mult).then_inc(s["ah_ready"], 1)
                dve.wait_ge(s["api_ready"], r + 1)
                V.tensor_tensor(bU[:, :], kkn[:, :], aS[:, :], ALU.mult).then_inc(s["bh_ready"], 1)
                V.tensor_tensor(ar[:, 1, :], rS[:, :], pd[:, :], ALU.mult).then_inc(s["rh_ready"], 1)
                dve.wait_ge(s["rk_ps"], r + 1)
                V.tensor_tensor(bv[:, :], B[3][:, 0:T], vS[:, :], ALU.mult).then_inc(s["bv_ready"], 1)
                go(1)
                go(2)
                out(0)
                bd = [P, G, 2, C]
                sb, sk = [w[:, 0:2 * T].rearrange("p (g a c) -> p g a c", g=G, a=2) for w in (B01, B23)]
                dve.wait_ge(s["score_ps"], r * 3 + 1)
                V.tensor_tensor(Tm[:, :, :], sb[:, :, 0, :], cms("pairs").rearrange("p (g c) -> p g c", g=G), ALU.mult
                                ).then_inc(s["dve_step"], 1)
                dve.wait_ge(s["dve_step"], r * 4 + 1)
                V.tensor_tensor(Y[:, :, :], Tm[:, :, :], istk.unsqueeze(1).to_broadcast([P, G, C]), ALU.add).then_inc(s["y_ready"], 1)
                dve.wait_ge(s["score_ps"], r * 3 + 2)
                V.tensor_tensor(ABD[:, :, :, :], B[4][:, 0:T].rearrange("p (g c) -> p g c", g=G).unsqueeze(2).to_broadcast(bd),
                                cms("lower").rearrange("p (g h c) -> p g h c", g=G, h=2), ALU.mult)
                V.tensor_tensor(ARB[:, :, :], sb[:, :, 1, :], cms("incl").rearrange("p (g c) -> p g c", g=G), ALU.mult
                                ).then_inc(s["arb_ready"], 1)
                dve.wait_ge(s["score_ps"], r * 3 + 3)
                V.tensor_tensor(AKBD[:, :, :, :], sk[:, :, 0, :].unsqueeze(2).to_broadcast(bd),
                                cms("strict").rearrange("p (g h c) -> p g h c", g=G, h=2), ALU.mult).then_inc(s["akbd_ready"], 1)
                V.tensor_tensor(ARK[:, :, :], sk[:, :, 1, :], cms("incl").rearrange("p (g c) -> p g c", g=G), ALU.mult
                                ).then_inc(s["ark_ready"], 1)
                go(3)
                lv = CM["level"][0]
                for n in range(LEVELS):
                    w = T if n < SMALL else TP
                    dve.wait_ge(s["t_ps"], r * LEVELS + n + 1)
                    V.tensor_tensor(Tm[:, :, :].rearrange("p g c -> p (g c)")[:, 0:w], B[0][:, 0:w],
                                    cm[:, lv + n * T:lv + n * T + w], ALU.mult).then_inc(s["t_ready"], 1)
                    if n:
                        go(3 + n)
                    if n == 1:
                        out(1)
                    dve.wait_ge(s["m_ps"], r * LEVELS + n + 1)
                    dve.wait_ge(s["ybd_ready"], r * (2 * LEVELS + 2) + 2 * n + 2)
                    Yf = Y[:, :, :].rearrange("p g c -> p (g c)")[:, 0:w]
                    V.tensor_tensor(Yf, B[1][:, 0:w], Yf, ALU.add).then_inc(s["y_ready"], 1)
                    if n == 3:
                        out(2)
                for g in range(GP):
                    dve.wait_ge(s["rhs_ps"], r * GP + g + 1)
                    w = 2 * C if g == 0 else C
                    V.tensor_copy(RHS[:, :, :].rearrange("p a c -> p (a c)")[:, 0:w], B[2][:, 0:w]).then_inc(s["rhs_ready"], 1)
                    dve.wait_ge(s["u_ps"], r * GP + g + 1)
                    if g == 0:
                        V.tensor_copy(Us[:, 0:G:G - 1, :], B[3][:, 0:2 * C].rearrange("p (a c) -> p a c", a=2)).then_inc(s["u_ready"], 1)
                    else:
                        V.tensor_copy(Us[:, g, :], B[3][:, 0:C]).then_inc(s["u_ready"], 1)
                    dve.wait_ge(s["s_ps"], r * GP + g + 1)
                    decay = pd[:, C * g + C - 1:C * g + C]
                    if g == 0:
                        V.tensor_scalar(Ss[:, 0, :], B[0][:, 0:C], decay, None, ALU.mult).then_inc(s["s_ready"], 1)
                    else:
                        dve.wait_ge(s["sd_ready"], r * (GP - 1) + g)
                        V.scalar_tensor_tensor(Ss[:, g, :], B[0][:, 0:C], decay, Sd[:, :], ALU.mult, ALU.add).then_inc(s["s_ready"], 1)
                    if g in (1, 3):
                        go(8 + g // 2)
                    if g == 1:
                        out(3)
                dve.wait_ge(s["tails_ready"], r * 2 + 2)
                V.tensor_tensor(xpB[:, :, :], tails[:, 0, :].unsqueeze(1).to_broadcast([P, NB, C]),
                                cfs("batch").unsqueeze(2).to_broadcast([P, NB, C]), ALU.mult).then_inc(s["xpb_ready"], 1)
                go(10)
                out(4)
                dve.wait_ge(s["mean_ps"], r + 1)
                V.tensor_tensor(dO[:, :], O_s[:, :], B[5][:, 0:T], ALU.subtract).then_inc(s["dev_ready"], 1)
                go(11)
                dve.wait_ge(s["sd_done"], r + 1)
                V.reciprocal(sd[:, :], sd[:, :]).then_inc(s["dve_step"], 1)
                dve.wait_ge(s["dve_step"], r * 4 + 2)
                V.scalar_tensor_tensor(dO[:, :], dO[:, :], cur_m[:, LN_W:LN_W + 1], sd[:, :], ALU.mult, ALU.mult).then_inc(s["dve_step"], 1)
                dve.wait_ge(s["dve_step"], r * 4 + 3)
                V.scalar_tensor_tensor(dO[:, :], dO[:, :], cur_m[:, LN_B:LN_B + 1], bv[:, :], ALU.add, ALU.add).then_inc(s["dve_step"], 1)
                dve.wait_ge(s["dve_step"], r * 4 + 4)
                dve.wait_ge(s["sgs_ready"], r + 1)
                V.tensor_tensor(yf[:, ds(r * T, T)], dO[:, :], sg[:, :], ALU.mult).then_inc(s["y_done"], 1)
                out(5)

            with dve.Fori(1, PAIRS) as q:
                mix(q - 1, q)
            mix(PAIRS - 1, PAIRS)

            def early(*js):
                for j in js:
                    ahead(BASE_EARLY, j)

            E = EXT
            count = cfs("count").rearrange("p (g t) -> p g t", t=16)
            steps = 3

            def window(g):
                nonlocal steps
                w = WINDOWS[g]
                u = uS[:, 2 * g:2 * g + 2, :]
                samples = ue[:, :, BUF + TP:E].rearrange("p k (b t) -> p k b t", b=NB)
                V.tensor_copy(ue[:, :, BUF:BUF + TP], u[:, :, 0:TP])
                V.tensor_copy(samples[:, :, :, BUF:BUF + TB], u[:, :, TP:T].rearrange("p k (b t) -> p k b t", b=NB))
                a = NB * BUF * (2 * g % 4)
                V.tensor_copy(samples[:, :, :, 0:BUF], B[g // 2][:, a:a + 2 * NB * BUF]
                              .rearrange("p (k b t) -> p k b t", k=2, b=NB)).then_inc(s["chain"], 1)
                src = ue
                for n in range(g + 1):
                    steps += 1
                    dve.wait_ge(s["chain"], steps)
                    dst, h = (win_a, win_b)[n % 2], 2 ** n
                    V.tensor_tensor(dst[:, :, 2 * h - 1:E], src[:, :, 2 * h - 1:E], src[:, :, h - 1:E - h], ALU.add
                                    ).then_inc(s["chain"], 1)
                    src = dst
                steps += 1
                dve.wait_ge(s["chain"], steps)
                V.tensor_tensor(head[:, :, :], src[:, :, BUF:BUF + 16],
                                count[:, g].unsqueeze(1).to_broadcast([P, 2, 16]), ALU.mult).then_inc(s["chain"], 1)
                steps += 1
                dve.wait_ge(s["chain"], steps)
                V.tensor_tensor(u[:, :, 0:16], head[:, :, :], u[:, :, 0:16], ALU.subtract).then_inc(s["mixed"], 1)
                V.scalar_tensor_tensor(u[:, :, 16:TP], src[:, :, BUF + 16:BUF + TP], 1.0 / w, u[:, :, 16:TP],
                                       ALU.mult, ALU.subtract).then_inc(s["mixed"], 1)
                for k in range(2):
                    us = u[:, k, TP:T].rearrange("p (b t) -> p b t", b=NB)
                    V.scalar_tensor_tensor(us, src[:, k, BUF + TP:E].rearrange("p (b t) -> p b t", b=NB)[:, :, BUF:BUF + TB],
                                           1.0 / w, us, ALU.mult, ALU.subtract).then_inc(s["mixed"], 1)

            def gated(m):
                dve.wait_ge(s["pyb_ps"], m + 1)
                if m >= 2:
                    dve.wait_ge(s["ybl_ready"], m - 1)
                V.scalar_tensor_tensor(ytmp[:, m % 2, :], B[2 + m % 2][:, 0:T], par2[:, PSC + m:PSC + m + 1], gp[:, m, :],
                                       ALU.mult, ALU.mult).then_inc(s["yb_ready"], 1)
                dve.wait_ge(s["yb_done"], m + 1)
                V.tensor_tensor(ybl[:, m * T:(m + 1) * T], ytmp[:, m % 2, :], ybh[:, m * T:(m + 1) * T].bitcast(F32),
                                ALU.subtract).then_inc(s["ybl_ready"], 1)

            early(0, 1)
            dve.wait_ge(s["zeroed"], 10)
            dve.wait_ge(s["utok_ps"], 4)
            window(0)
            early(2, 3)
            window(1)
            early(4, 5)
            window(2)
            early(6, 7)
            window(3)
            early(8, 9)
            dve.wait_ge(s["gsil_ready"], 1)
            for m in range(4):
                gated(m)
            early(10)
            for m in range(4, 8):
                gated(m)
            early(11, 12)
            dve.wait_ge(s["rows_out"], 16 * (18 + 1 + 1 + NB))
            gates = ((kS[:, :], rS[:, :]), (vS[:, :], gS[:, :]), (gt[:, 0, :], gt[:, 1, :]), (gt[:, 2, :], gt[:, 3, :]))
            dve.wait_ge(s["sb_ready"], 4)
            dve.wait_ge(s["gates_ready"], 4)

            def early_merge(i):
                dve.wait_ge(s["chunk_used"], BASE_EARLY + 2 * EARLY + EARLY + i + 1)
                sa, sb_ = gates[i]
                V.tensor_tensor(sa, sa, (acc[0], acc[1], B[4], B[5])[i][:, 0:T], ALU.mult)
                V.tensor_tensor(sb_, sb_, B[i][:, 0:T], ALU.mult).then_inc(s["mb_ready"], 1)
                dve.wait_ge(s["mb_ready"], i + 1)
                V.tensor_tensor(mm_[:, i % 2, :], sa, sb_, ALU.add).then_inc(s["m_ready"], 1)
                dve.wait_ge(s["mh_ready"], i + 1)
                V.tensor_tensor(ml[:, T * i:T * (i + 1)], mm_[:, i % 2, :], mh[:, T * i:T * (i + 1)].bitcast(F32),
                                ALU.subtract).then_inc(s["ml_ready"], 1)

            for i in range(3):
                early(13 + i)
                early_merge(i)
            early_merge(3)

            with dve.Fori(EARLY // 2, KT // 2) as n:
                for m in range(2):
                    i = n * 2 + m
                    banks = (B[0], B[1]) if m == 0 else (B[4], B[5])
                    for j in range(CH_MERGE):
                        ahead(n * (2 * CH_MERGE) + BASE_MERGE, CH_MERGE * m + j)
                    dve.wait_ge(s["chunk_used"], i * CH_MERGE + (BASE_MERGE + 6))
                    dve.wait_ge(s["sb_ready"], i + 1)
                    V.tensor_tensor(ga[:, m, :], ga[:, m, :], banks[0][:, 0:T], ALU.mult)
                    V.tensor_tensor(gb[:, m, :], gb[:, m, :], banks[1][:, 0:T], ALU.mult).then_inc(s["mb_ready"], 1)
                    dve.wait_ge(s["mb_ready"], i + 1)
                    V.tensor_tensor(mm_[:, m, :], ga[:, m, :], gb[:, m, :], ALU.add).then_inc(s["m_ready"], 1)
                    dve.wait_ge(s["mh_ready"], i + 1)
                    V.tensor_tensor(ml[:, ds(n * (2 * T) + m * T, T)], mm_[:, m, :],
                                    mh[:, ds(n * (2 * T) + m * T, T)].bitcast(F32), ALU.subtract).then_inc(s["ml_ready"], 1)

            def out_tile(n, m, first=False):
                i = n * 2 + m
                for h in range(2):
                    ahead(n * 4 + BASE_OUT, 2 * m + h)
                dve.wait_ge(s["so_ready"], i + 1)
                V.tensor_tensor(o2[:, ds(n * (2 * T) + m * T, T)], acc[m][:, 0:T],
                                par2[:, ds(n * 2 + (NPOST + m), 1)].to_broadcast([P, T]), ALU.mult).then_inc(s["o2_ready"], 1)
                if first:
                    V.tensor_copy(sacc[:, :], sqo[:, m, :]).then_inc(s["sacc_ready"], 1)
                else:
                    dve.wait_ge(s["sacc_ready"], i)
                    V.tensor_tensor(sacc[:, :], sacc[:, :], sqo[:, m, :], ALU.add).then_inc(s["sacc_ready"], 1)

            out_tile(0, 0, first=True)
            out_tile(0, 1)
            with dve.Fori(1, KT // 2) as n:
                for m in range(2):
                    out_tile(n, m)
            dve.wait_ge(s["srt"], 1)
            V.reciprocal(sacc[:, :], sacc[:, :]).then_inc(s["chain"], 1)
            dve.wait_ge(s["chain"], steps + 1)
            dve.wait_ge(s["o2_ready"], KT)

            def lower_part(k):
                dve.wait_ge(s["x1h_ready"], k + 1)
                V.tensor_tensor(x1l[:, T * k:T * (k + 1)], xT[:, T * k:T * (k + 1)],
                                x1h[:, T * k:T * (k + 1)].bitcast(F32), ALU.subtract).then_inc(s["x1l_ready"], 1)

            for k in range(KT):
                V.tensor_tensor(o2[:, T * k:T * (k + 1)], o2[:, T * k:T * (k + 1)], sacc[:, :], ALU.mult).then_inc(s["x1a"], 1)
                if k >= 3:
                    lower_part(k - 3)
            for k in range(KT - 3, KT):
                lower_part(k)

            def gate_tile(n, m, last=False):
                i = n * 2 + m
                for h in range(2):
                    if not last or 2 * m + h + AHEAD < 4:
                        ahead(n * 4 + BASE_GATE, 2 * m + h)
                dve.wait_ge(s["g3_ready"], i + 1)
                dve.wait_ge(s["ple_ps"], i + 1)
                V.tensor_tensor(g3[:, m, :], g3[:, m, :], B[m][:, 0:T], ALU.mult).then_inc(s["g3m"], 1)
                dve.wait_ge(s["g3m"], i + 1)
                V.tensor_tensor(yo[:, m, :], g3[:, m, :], xT[:, ds(n * (2 * T) + m * T, T)], ALU.add).then_inc(s["yo_ready"], 1)

            with dve.Fori(0, KT // 2 - 1) as n:
                for m in range(2):
                    gate_tile(n, m)
            for m in range(2):
                gate_tile(KT // 2 - 1, m, last=True)

        @block.tensor
        def _(pe):
            M = nc.tensor

            def passes(out, slot, k, hi, lo, width, first, last):
                wcol = slice(P * k, P * (k + 1))
                M.matmul(out[:, 0:width], wh[:, slot, wcol], hi, start=first, stop=False)
                M.matmul(out[:, 0:width], wh[:, slot, wcol], lo, start=False, stop=False)
                return M.matmul(out[:, 0:width], wl[:, slot, wcol], hi, start=False, stop=last)

            def chunk(count, j, out, hi, lo, pitch, width, k0, first, last, part=None):
                slot = j % SLOTS
                ks = range(KC) if part is None else part
                for k in ks:
                    if k == 0:
                        pe.wait_ge(s["lo_ready"], count + j + 1)
                    a = (k0 + k) * pitch
                    mm = passes(out, slot, k, hi[:, a:a + width], lo[:, a:a + width], width,
                                first and k == 0, last and k == KC - 1)
                    if k == KC - 1:
                        mm.then_inc(s["chunk_used"], 1)

            def transpose(out, in_):
                rows = in_.shape[0]
                return M.transpose(out, in_, ident[0:rows, 0:rows])

            pe.wait_ge(s["const_in"], 16)
            pe.wait_ge(s["rows_in"], 12 * 16)
            transpose(B[4][:, 0:NROW * PAIRS], rows[0:NROW * PAIRS, 0, :]).then_inc(s["par_ready"], 1)
            transpose(B[5][:, 0:NPAR2], rows[0:NPAR2, 1, :]).then_inc(s["par_ready"], 1)
            for t in range(3):
                n = P if t < 2 else NB * TB + NB
                pe.wait_ge(s["h_rows"], (1, 2, 4)[t])
                for c in range(4):
                    if t:
                        pe.wait_ge(s["hT_done"], 4 * (t - 1) + c + 1)
                    for k in range(4):
                        col = P * (4 * c + k)
                        last = transpose(B[c][:, P * k:P * k + n], ht[0:n, t % 2, col:col + P])
                    last.then_inc(s["hT_ps"], 1)

            class Stream:

                def __init__(self, q):
                    self.q, self.at = q, 0

                def advance(self, n):
                    q = self.q
                    first = isinstance(q, int) and q == 0
                    for _ in range(n):
                        tile, kt = self.at // KT, self.at % KT
                        if kt == 0 and not (first and tile < 2):
                            pe.wait_ge(s["acc_free"], tile - 1 if first else q * TILES_STEP + (ACC_STEP + tile - 1))
                        width = TS if tile < 3 and not (isinstance(q, int) and q == PAIRS) else T
                        chunk(0 if first else q * CH_STEP + BASE_STEP, 2 * tile + kt // KC, acc[tile % 2], hh, hl, TS,
                              width, KC * (kt // KC), kt // KC == 0, kt // KC == 1, part=[kt % KC])
                        self.at += 1

            first = Stream(0)
            for c in range(4):
                if c < 2:
                    pe.wait_ge(s["h_split"], c + 1)
                else:
                    pe.wait_ge(s["hl_done"], c - 1)
                first.advance(4)
            pe.wait_ge(s["par_done"], 4)
            pe.wait_ge(s["dh_done"], 4)
            transpose(B[4][0:72, 0:P], hlast[:, 0:72]).then_inc(s["last_ps"], 1)
            transpose(B[5][0:72, 0:P], hlast[:, 72:144]).then_inc(s["last_ps"], 1)
            pe.wait_ge(s["map_in"], 48)
            for j in range(1, CH_FIRST):
                if j > 1:
                    first.advance(KC)
                for n in [2 * k + m for k in MAP_TILES[j] for m in range(2)]:
                    k = n // 2
                    pe.wait_ge(s["xw_ready"], n + 1)
                    M.matmul(B[n % 2][0:RANK, 0:T], (lw1, la1)[n % 2][:, k, :], xw[:, n % 4, :],
                             start=k == 0, stop=k == KT - 1).then_inc(s["xw_used"], 1)

            ADV = [10, 6, 4, 6, 4, 3, 2, 2, 2, 2, 2, 1, 5, 4]

            def mix(r, q):
                st = Stream(q)
                pe.wait_ge(s["s0_in"], r * 32 + 32)
                pe.wait_ge(s["last_done"], 2)
                for b in range(NB):
                    last = transpose(B45[:, P * b:P * (b + 1)], S0n[:, b, :])
                last.then_inc(s["s0_ps"], 1)
                pe.wait_ge(s["lw2_in"], r * 32 + 32)
                pe.wait_ge(s["lora_act"], 2)
                M.matmul(B[0][:, 0:T], lw2[:, :], t1[:, :], start=True, stop=True)
                M.matmul(B[1][:, 0:T], la2[:, :], la[:, :], start=True, stop=True).then_inc(s["lora2_ps"], 1)
                st.advance(ADV[0])
                pe.wait_ge(s["ksq_ready"], r + 1)
                M.matmul(B[2][:, 0:T], ones2, sq[:, :], start=True, stop=True).then_inc(s["kk_ps"], 1)
                st.advance(ADV[1])
                pe.wait_ge(s["s0t_ready"], r + 1)
                pe.wait_ge(s["vbd_ready"], r * 2 + 2)
                for g in range(G):
                    last = transpose(B45[:, P * g:P * (g + 1)], flat(vBD, g))
                last.then_inc(s["vt_ps"], 1)
                st.advance(ADV[2])
                pe.wait_ge(s["rk_ready"], r + 1)
                M.matmul(B[3][:, 0:T], ones2, sq[:, :], start=True, stop=True).then_inc(s["rk_ps"], 1)
                st.advance(ADV[3])
                pe.wait_ge(s["vs_ready"], r * 2 + 2)
                pe.wait_ge(s["rh_ready"], r + 1)
                z = B[5][:, 0:2 * C].rearrange("p (a c) -> p a c", a=2)
                for b in range(NB):
                    last = M.matmul(z[:, :, TB * b:TB * (b + 1)], S0T[:, b, :], ar[:, :, TP + TB * b:TP + TB * (b + 1)],
                                    start=True, stop=True)
                last.then_inc(s["z_ps"], 1)
                pe.wait_ge(s["bbd_ready"], r * 2 + 2)
                pe.wait_ge(s["kbd_ready"], r * 2 + 2)
                for g in range(G):
                    last = M.matmul(B01[:, P * g:P * (g + 1)].rearrange("p (a c) -> p a c", a=2), flat(bBD, g),
                                    ar[:, :, tok(g)], start=True, stop=True)
                last.then_inc(s["score_ps"], 1)
                for g in range(G):
                    last = M.matmul(B[4][:, tok(g)], flat(aBD, g), bU[:, tok(g)], start=True, stop=True)
                last.then_inc(s["score_ps"], 1)
                pe.wait_ge(s["bv_ready"], r + 1)
                for g in range(G):
                    last = M.matmul(B23[:, P * g:P * (g + 1)].rearrange("p (a c) -> p a c", a=2), flat(kBD, g),
                                    ar[:, :, tok(g)], start=True, stop=True)
                last.then_inc(s["score_ps"], 1)
                st.advance(ADV[4])
                pe.wait_ge(s["arb_ready"], r + 1)
                pe.wait_ge(s["zabd_ready"], r * 2 + 2)
                for g in range(G):
                    last = transpose(B45[:, P * g:P * (g + 1)], flat(bBD, g))
                last.then_inc(s["bt_ps"], 1)
                st.advance(ADV[5])
                pe.wait_ge(s["akbd_ready"], r + 1)
                pe.wait_ge(s["arb_ready"], r + 1)
                pe.wait_ge(s["ark_ready"], r + 1)
                for g in range(G):
                    last = transpose(B23[:, P * g:P * (g + 1)], flat(kBD, g))
                last.then_inc(s["kt_ps"], 1)

                def products(n):
                    pe.wait_ge(s["y_ready"], r * (LEVELS + 1) + n + 1)
                    for g in range(G if n < SMALL else GP):
                        last = M.matmul(B[0][:, tok(g)], flat(ABD, g), Y[:, g, :], start=True, stop=True)
                    last.then_inc(s["t_ps"], 1)

                def inverse_transpose(n):
                    pe.wait_ge(s["ybd_ready"], r * (2 * LEVELS + 2) + 2 * n + 2)
                    if n == 0:
                        pe.wait_ge(s["bt_ready"], r + 1)
                    for g in range(G if n < SMALL else GP):
                        last = transpose(B45[:, P * g:P * (g + 1)], flat(YBD, g))
                    last.then_inc(s["x_ps"], 1)

                def update(n):
                    pe.wait_ge(s["t_ready"], r * LEVELS + n + 1)
                    pe.wait_ge(s["x_ready"], r * LEVELS + n + 1)
                    for g in range(G if n < SMALL else GP):
                        last = M.matmul(B[1][:, tok(g)], flat(XBD, g), Tm[:, g, :], start=True, stop=True)
                    last.then_inc(s["m_ps"], 1)

                for n in range(LEVELS):
                    products(n)
                    st.advance(ADV[6])
                    inverse_transpose(n)
                    st.advance(ADV[7])
                    update(n)
                    st.advance(ADV[8])
                pe.wait_ge(s["tail_ready"], r * 2 + 2)
                pe.wait_ge(s["x_ready"], r * LEVELS + LEVELS)
                for n in range(2):
                    last = transpose(B[5][:, P * n:P * (n + 1)], tail4[:, n].rearrange("p h c -> p (h c)"))
                last.then_inc(s["tail_ps"], 1)
                pe.wait_ge(s["kt_ready"], r + 1)
                for g in range(GP):
                    M.matmul(B[2][:, 0:C], flat(AKBD, g), Vs[:, g, :], start=True, stop=g == 0)
                    if g == 0:
                        M.matmul(B[2][:, C:2 * C], flat(AKBD, G - 1), Vs[:, G - 1, :], start=True, stop=False)
                        last = M.matmul(B[2][:, C:2 * C], ZaBD[:, :, :].rearrange("p h c -> p (h c)"), istk, start=False, stop=True)
                    else:
                        pe.wait_ge(s["s_ready"], r * GP + g)
                        last = M.matmul(B[2][:, 0:C], flat(aBD, g), Ss[:, g - 1, :], start=False, stop=True)
                    last.then_inc(s["rhs_ps"], 1)
                    st.advance(ADV[9])
                    pe.wait_ge(s["ybd_ready"], r * (2 * LEVELS + 2) + 2 * LEVELS + 2)
                    pe.wait_ge(s["rhs_ready"], r * GP + g + 1)
                    last = M.matmul(B[3][:, 0:C], flat(YBD, g), RHS[:, 0, :], start=True, stop=True)
                    if g == 0:
                        last = M.matmul(B[3][:, C:2 * C], flat(YBD, G - 1), RHS[:, 1, :], start=True, stop=True)
                    last.then_inc(s["u_ps"], 1)
                    st.advance(ADV[10])
                    M.matmul(B[0][:, 0:C], flat(KtBD, g), Vs[:, g, :], start=True, stop=False)
                    pe.wait_ge(s["u_ready"], r * GP + g + 1)
                    M.matmul(B[0][:, 0:C], flat(BtBD, g), Us[:, g, :], start=False, stop=True).then_inc(s["s_ps"], 1)
                    st.advance(ADV[11] if g < GP - 1 else ADV[13])
                pe.wait_ge(s["sbd_ready"], r * 2 + 2)
                pe.wait_ge(s["ubd_ready"], r * 2 + 2)
                for g in range(G):
                    o = B[4][:, tok(g)]
                    M.matmul(o, flat(VtBD, g), ARK[:, g, :], start=True, stop=False)
                    if g == G - 1:
                        M.matmul(o, ident, Zs[:, 1, :], start=False, stop=False)
                    elif g:
                        M.matmul(o, flat(SBD, g - 1), ar[:, 1, tok(g)], start=False, stop=False)
                    last = M.matmul(o, flat(UBD, g), ARB[:, g, :], start=False, stop=True)
                last.then_inc(s["o_ps"], 1)
                pe.wait_ge(s["endbd_ready"], r * 2 + 2)
                transpose(B[0][:, 0:P], EndBD[:, :, :].rearrange("p h c -> p (h c)")).then_inc(s["end_ps"], 1)
                for name in ("xpb_ready", "xpk_ready", "dpl_ready"):
                    pe.wait_ge(s[name], r + 1)
                M.matmul(B[3][:, :], flat(UBD, G - 1), xpB[:, :, :].rearrange("p b c -> p (b c)"), start=True, stop=False)
                M.matmul(B[3][:, :], flat(VtBD, G - 1), xpK[:, :, :].rearrange("p b c -> p (b c)"), start=False, stop=False)
                for b in range(NB):
                    last = M.matmul(B[3][:, C * b:C * (b + 1)], S0T[:, b, :], dPL[:, b, :], start=False, stop=b == NB - 1)
                last.then_inc(s["send_ps"], 1)
                pe.wait_ge(s["o_ready"], r + 1)
                pe.wait_ge(s["tails_ready"], r * 2 + 2)
                M.matmul(B[5][:, 0:T], mean2, O_s[:, :], start=True, stop=True).then_inc(s["mean_ps"], 1)
                st.advance(ADV[12])
                pe.wait_ge(s["dsq_ready"], r + 1)
                M.matmul(B[2][:, 0:T], mean2, dsq[:, :], start=True, stop=True).then_inc(s["var_ps"], 1)
                st.advance(TILES_STEP * KT - st.at)

            with pe.Fori(1, PAIRS) as q:
                mix(q - 1, q)
            mix(PAIRS - 1, PAIRS)

            pe.wait_ge(s["acc_free"], ACC_ALL)
            for k in range(8):
                last = transpose(B[4 + k // 4][0:NB * TB + BUF, P * (k % 4):P * (k % 4 + 1)], uS[:, k, TP - BUF:T])
                if k % 4 == 3:
                    last.then_inc(s["utok_ps"], 1)

            def early_gate(g, h):
                if g >= 2:
                    pe.wait_ge(s["gates_ready"], g - 1)
                chunk(BASE_EARLY, 2 * g + h, acc[g % 2], hh, hl, TS, T, KC * h, h == 0, h == 1)

            def early_branch(b, i):
                bank = B[i] if b else (acc[0], acc[1], B[4], B[5])[i]
                hi, lo = ((yah, yal), (ybh, ybl))[b]
                chunk(BASE_EARLY + 2 * EARLY, EARLY * b + i, bank, hi, lo, T, T, 0, True, True)

            def pool_map(m):
                pe.wait_ge(s["mixed"], 4 * (m // 2) + 4)
                if m >= 2:
                    pe.wait_ge(s["yb_ready"], m - 1)
                for k in range(2):
                    last = M.matmul(B[2 + m % 2][:, 0:T], pw[:, m // 2 * 2 + k, P * (m % 2):P * (m % 2) + P],
                                    uS[:, m // 2 * 2 + k, :], start=k == 0, stop=k == 1)
                last.then_inc(s["pyb_ps"], 1)

            early_gate(0, 0)
            pe.wait_ge(s["pool_in"], 16)
            for k in range(8):
                w = NB * BUF
                last = transpose(B[k // 4][:, w * (k % 4):w * (k % 4 + 1)], spt[:, P * k:P * (k + 1)])
                if k % 4 == 3:
                    last.then_inc(s["utok_ps"], 1)
            early_gate(0, 1)
            for g in range(1, 4):
                for h in range(2):
                    early_gate(g, h)
            pe.wait_ge(s["yal_ready"], 1)
            pe.wait_ge(s["gates_ready"], 3)
            early_branch(0, 0)
            pe.wait_ge(s["map_in"], 64)
            for m in range(4):
                pool_map(m)
            pe.wait_ge(s["gates_ready"], 4)
            early_branch(0, 1)
            for m in range(4, 8):
                pool_map(m)
            pe.wait_ge(s["utok_ev"], 2)
            early_branch(0, 2)
            early_branch(0, 3)
            pe.wait_ge(s["ybl_ready"], 8)
            for i in range(EARLY):
                early_branch(1, i)

            def merge_tile(n, m):
                banks = (acc[0], acc[1], B[0], B[1]) if m == 0 else (B[2], B[3], B[4], B[5])
                count = n * (2 * CH_MERGE) + BASE_MERGE
                pe.wait_ge(s["m_ready"], n * 2 + m - 1)
                for g in range(2):
                    for h in range(2):
                        chunk(count, CH_MERGE * m + 2 * g + h, banks[g], hh, hl, TS, T, KC * h, h == 0, h == 1)
                chunk(count, CH_MERGE * m + 4, banks[2], yah, yal, T, T, 0, True, True)
                chunk(count, CH_MERGE * m + 5, banks[3], ybh, ybl, T, T, 0, True, True)

            with pe.Fori(EARLY // 2, KT // 2) as n:
                for m in range(2):
                    merge_tile(n, m)

            pe.wait_ge(s["ml_ready"], KT)

            def out_tile(n, m, free):
                if free:
                    pe.wait_ge(s["o2_ready"], n * 2 + m - 1)
                for h in range(2):
                    chunk(n * 4 + BASE_OUT, 2 * m + h, acc[m], mh, ml, T, T, KC * h, h == 0, h == 1)

            for m in range(2):
                out_tile(0, m, False)
            sizes = (P, P, NB * TB)
            pe.wait_ge(s["x2_in"], 96)
            for k in range(KT):
                if k >= 4:
                    pe.wait_ge(s["xT_ready"], k - 3)
                for t in range(3):
                    last = transpose(B[k % 4][:, P * t:P * t + sizes[t]], xt2[0:sizes[t], t, P * k:P * (k + 1)])
                last.then_inc(s["xT_ps"], 1)
            pe.wait_ge(s["x2_in"], 96)
            for k in range(2):
                for t in range(3):
                    last = transpose(B[4 + k][:, P * t:P * t + sizes[t]], pt[0:sizes[t], t, P * k:P * (k + 1)])
                last.then_inc(s["pT_ps"], 1)
            with pe.Fori(1, KT // 2) as n:
                for m in range(2):
                    out_tile(n, m, True)
            pe.wait_ge(s["sacc_ready"], KT)
            pe.wait_ge(s["pT_ready"], 2)
            M.matmul(B[5][:, 0:T], meand, sacc[:, :], start=True, stop=True).then_inc(s["ssq_ps"], 1)

            def gate_tile(n, m, pace=False):
                if pace:
                    for h in range(2):
                        for k in range(KC):
                            pe.wait_ge(s["x1l_ready"], KC * h + k + 1)
                            chunk(n * 4 + BASE_GATE, 2 * m + h, acc[m], x1h, x1l, T, T, KC * h, h == 0, h == 1, part=[k])
                else:
                    for h in range(2):
                        chunk(n * 4 + BASE_GATE, 2 * m + h, acc[m], x1h, x1l, T, T, KC * h, h == 0, h == 1)
                pe.wait_ge(s[f"wple_in{m}"], n * 16 + 16)
                for k in range(2):
                    last = M.matmul(B[m][:, 0:T], wple[:, m, P * k:P * (k + 1)], pT[:, k, :], start=k == 0, stop=k == 1)
                last.then_inc(s["ple_ps"], 1)

            def tokens(i, m, free):
                pe.wait_ge(s["yo_ready"], i + 1)
                if free is not None:
                    pe.wait_ge(s["ytk_ready"], free)
                for t in range(3):
                    last = transpose(B[2 + m][0:sizes[t], P * t:P * (t + 1)], yo[:, m, P * t:P * t + sizes[t]])
                last.then_inc(s["yt_ps"], 1)

            pe.wait_ge(s["o2_ready"], KT)
            gate_tile(0, 0, pace=True)
            gate_tile(0, 1)
            tokens(0, 0, None)
            pe.wait_ge(s["yo_ready"], 1)
            gate_tile(1, 0)
            tokens(1, 1, None)
            gate_tile(1, 1)
            tokens(2, 0, 2)
            with pe.Fori(2, KT // 2) as n:
                gate_tile(n, 0)
                tokens(n * 2 - 1, 1, n * 4 - 4)
                gate_tile(n, 1)
                tokens(n * 2, 0, n * 4 - 2)
            tokens(KT - 1, 1, 2 * KT - 4)


OUTS = [((1, TP, D), "float32"), ((NB, TB, D), "float32"), ((1, 1, 16, HD, HD), "float32"), ((1, 1, D), "float32"),
        ((1, 1, BUF, R), "float32"), ((1, NB, 16, HD, HD), "float32"), ((1, NB, D), "float32"), ((1, NB, BUF, R), "float32")]
INS = ["x_prompt", "x_sample", "state_wkv", "state_shift", "state_pool", "p_prompt", "p_sample", "norm_pre", "norm_post",
       "w_in", "mu_rkv", "mu_lora", "w0", "w1", "w2", "a0", "a1", "a2", "k_k", "k_a", "r_k", "ln_w", "ln_b", "pool_w",
       "pool_scale", "w_branch", "w_out", "w_ple", "w_ple_gate"]


def kernel(**inputs):
    import ml_dtypes
    from concourse import bacc
    from concourse.bass_utils import run_bass_kernel_spmd

    nc = bacc.Bacc("TRN2", target_bir_lowering=False, num_devices=1)
    const_f, const_m = shape_constants()
    arrays = {f"in_{n}": np.ascontiguousarray(inputs[n]) for n in INS}
    arrays["in_const_f"] = const_f
    arrays["in_const_m"] = const_m.astype(ml_dtypes.bfloat16)
    args = [nc.dram_tensor(n, a.shape, mybir.dt.from_np(a.dtype), kind="ExternalInput").ap() for n, a in arrays.items()]
    for i, (shape, dtype) in enumerate(OUTS):
        args.append(nc.dram_tensor(f"out_{i}", shape, mybir.dt.from_np(np.dtype(dtype)), kind="ExternalOutput").ap())
    build(nc, *args)
    r = run_bass_kernel_spmd(nc, [arrays], core_ids=[0])
    return tuple(r.results[0][f"out_{i}"] for i in range(len(OUTS)))
```

```python
from contextlib import ExitStack

import numpy as np
import concourse.bass as bass
from concourse import mybir

F32 = mybir.dt.float32
F32R = mybir.dt.float32r
BF16 = mybir.dt.bfloat16
ALU = mybir.AluOpType
ACT = mybir.ActivationFunctionType
ds = bass.ds

P = 128
D = 2048
KT = D // P
R = 1024
PAIRS = R // P
HD = 64
TP = 256
NB = 8
TB = 8
T = TP + NB * TB
TS = T + NB
C = 64
G = T // C
GP = TP // C
RANK = 96
PLE = 256
EMB = 8
BUF = 15
WINDOWS = (2, 4, 8, 16)
PGROUP = R // len(WINDOWS)
DECAY = 0.606531
RMS_EPS = 1e-6
GN_EPS = 64e-5
ROUNDS = 2
LEVELS = 4
SMALL = 1

MAP_TILES = [(), (), (0, 1, 2), (3, 4, 5), (6, 7, 8), (9, 10, 11), (12, 13), (14, 15)]
KC = 8
SLOTS = 4
AHEAD = 3
CH_FIRST = 8
CH_STEP = 12
CH_MERGE = 6
BASE_STEP = CH_FIRST - CH_STEP
BASE_EARLY = BASE_STEP + CH_STEP * (PAIRS + 1)
EARLY = 4
BASE_MERGE = BASE_EARLY + 4 * EARLY - CH_MERGE * EARLY
BASE_OUT = BASE_MERGE + CH_MERGE * KT
TILES_STEP = 6
ACC_STEP = 4 - TILES_STEP
ACC_ALL = ACC_STEP + TILES_STEP * (PAIRS + 1)
BASE_GATE = BASE_OUT + 2 * KT
CHUNKS = BASE_GATE + 2 * KT

COL_R, COL_K, COL_V, COL_G = 0, R, 2 * R, 3 * R
COL_U, COL_GP, COL_GA, COL_GB = 4 * R, 5 * R, 6 * R, 6 * R + D

MU_R, MU_K, MU_V, W0, A0, K_K, K_A, R_K, LN_W, LN_B, OM_R, OM_K, OM_V, OM_KA = range(14)
NPAR, NROW = 14, 10
NPRE, NPOST, MUW, MUA, PSC = 0, 16, 32, 48, 64
NPAR2 = 72

EXT = BUF + TP + NB * (BUF + TB)

CF = {}
CM = {}


def _columns(table, *widths):
    at = 0
    for name, width in widths:
        table[name] = (at, at + width)
        at += width
    return at


N_CF = _columns(CF, ("ident", P), ("istk", HD), ("ones2", P), ("mean2", P), ("meand", P), ("segment", T),
                ("batch", NB), ("eps", 2), ("count", 4 * 16))
N_CM = _columns(CM, ("quads", T), ("incl", T), ("strict", 2 * T), ("lower", 2 * T), ("level", LEVELS * T))


def shape_constants():
    f = np.zeros((P, N_CF), np.float32)
    p = np.arange(P)
    head, row = p // HD, p % HD

    def put(table, arr, name, value):
        a, b = table[name]
        arr[:, a:b] = value.reshape(P, b - a)

    put(CF, f, "ident", np.eye(P))
    put(CF, f, "istk", (row[:, None] == np.arange(HD)[None]))
    same = head[:, None] == head[None]
    put(CF, f, "ones2", same * 1.0)
    put(CF, f, "mean2", same / HD)
    put(CF, f, "meand", np.full((P, P), 1.0 / D))
    tok = np.arange(T)
    first = np.where(tok < TP, tok % C == 0, tok % TB == 0)
    put(CF, f, "segment", np.broadcast_to(1.0 - first, (P, T)))
    put(CF, f, "batch", (row // TB)[:, None] == np.arange(NB)[None])
    put(CF, f, "eps", np.broadcast_to(np.array([RMS_EPS, GN_EPS]), (P, 2)))
    put(CF, f, "count", np.broadcast_to(np.array([[1.0 / min(t + 1, w) for t in range(16)] for w in WINDOWS]), (P, 4, 16)))

    m = np.zeros((P, N_CM), np.float32)
    s, t = row[:, None, None], np.arange(C)[None, None, :]
    g = np.arange(G)[None, :, None]
    seq = (g < GP) | (s // TB == t // TB)
    put(CM, m, "incl", (s <= t) & seq)

    def level(b):
        inside = (s // (2 * b) == t // (2 * b)) & ((s // b) % 2 == 0) & ((t // b) % 2 == 1)
        return inside & ((g < GP) | (2 * b <= TB))

    put(CM, m, "quads", (s // 4 == t // 4) & (s < t) & seq)
    a = CM["level"][0]
    for n in range(LEVELS):
        m[:, a + n * T:a + (n + 1) * T] = level(2 ** (n + 2)).reshape(P, T)

    def diagonal(x):
        x = np.broadcast_to(x, (P, G, C))[:, :, None, :] & (head[:, None, None, None] == np.arange(2)[None, None, :, None])
        return x

    put(CM, m, "strict", diagonal((s < t) & seq))
    put(CM, m, "lower", diagonal((s > t) & seq))
    return f, m


def build(nc, x_prompt, x_sample, state_wkv, state_shift, state_pool, p_prompt, p_sample, norm_pre, norm_post,
          w_in, mu_rkv, mu_lora, w0, w1, w2, a0, a1, a2, k_k, k_a, r_k, ln_w, ln_b, pool_w, pool_scale,
          w_branch, w_out, w_ple, w_ple_gate, const_f, const_m,
          y_prompt, y_sample, wkv_prompt, shift_prompt, pool_prompt, wkv_sample, shift_sample, pool_sample):
    with ExitStack() as ctx:
        base = (nc.sbuf_base + 31) // 32 * 32
        used = {}

        def at(word, name, shape, dt=F32):
            size = int(np.prod(shape[1:])) * (2 if dt == BF16 else 4)
            used[name] = (word, word + (size + 3) // 4)
            return nc.alloc_sbuf_tensor_at(name, list(shape), dt, offset=base + 4 * word)

        class Region:
            def __init__(self, start):
                self.next = start

            def take(self, name, shape, dt=F32):
                t = at(self.next, name, shape, dt)
                self.next = (used[name][1] + 7) // 8 * 8
                return t

        fixed = Region(0)
        cf = fixed.take("cf", [P, N_CF])
        cm = fixed.take("cm", [P, N_CM], BF16)
        par = fixed.take("par", [P, NPAR * PAIRS])
        par2 = fixed.take("par2", [P, NPAR2])
        hh = fixed.take("hh", [P, KT * TS], F32R)
        hl = fixed.take("hl", [P, KT * TS], F32R)
        wraw = fixed.take("wraw", [P, SLOTS, KC * P])
        wh = fixed.take("wh", [P, SLOTS, KC * P], F32R)
        wl = fixed.take("wl", [P, SLOTS, KC * P], F32R)
        ya_start = fixed.next
        yf = fixed.take("yf", [P, PAIRS * T])
        gp = fixed.take("gp", [P, 8, T])
        t1 = fixed.take("t1", [RANK, T])
        la = fixed.take("la", [RANK, T])
        arena = fixed.next

        r1 = Region(arena)
        zsh = r1.take("zsh", [P, T])
        kS = r1.take("kS", [P, T])
        rS = r1.take("rS", [P, T])
        vS = r1.take("vS", [P, T])
        gS = r1.take("gS", [P, T])
        cur_p = r1.take("cur_p", [P, NPAR])
        cur_m = r1.take("cur_m", [P, NPAR])
        lw2 = r1.take("lw2", [RANK, P])
        la2 = r1.take("la2", [RANK, P])
        start_overlay = r1.next
        r0 = Region(start_overlay)
        xt = r0.take("xt", [P, 3, D])
        dh = at(used["xt"][0], "dh", [P, KT * T])
        ht = r0.take("ht", [P, 2, D])
        xw = at(used["ht"][0], "xw", [P, 4, T])
        hT = r0.take("hT", [P, KT * TS])
        rows = r0.take("rows", [P, 2, P])
        stat = r0.take("stat", [P, 4])
        hlast = r0.take("hlast", [P, 2 * 72])
        hlastT = r0.take("hlastT", [72, 2 * P])
        lw1 = at(ya_start, "lw1", [P, KT, RANK])
        la1 = at(used["lw1"][1], "la1", [P, KT, RANK])
        aBD = r1.take("aBD", [P, G, 2, C])
        bBD = r1.take("bBD", [P, G, 2, C])
        kBD = r1.take("kBD", [P, G, 2, C])
        vBD = r1.take("vBD", [P, G, 2, C])
        ABD = r1.take("ABD", [P, G, 2, C])
        AKBD = r1.take("AKBD", [P, G, 2, C])
        YBD = r1.take("YBD", [P, G, 2, C])
        BtBD = r1.take("BtBD", [P, G, 2, C])
        KtBD = r1.take("KtBD", [P, G, 2, C])
        VtBD = r1.take("VtBD", [P, G, 2, C])
        ZaBD = r1.take("ZaBD", [P, 2, C])
        EndBD = r1.take("EndBD", [P, 2, C])
        S0T = r1.take("S0T", [P, NB, P])
        S0n = r1.take("S0n", [P, NB, P])
        UBD, SBD, XBD = bBD, kBD, vBD
        sq = r1.take("sq", [P, T])
        pm = r1.take("pm", [P, T])
        aS = r1.take("aS", [P, T])
        sg = r1.take("sg", [P, T])
        cl = r1.take("cl", [P, T])
        rn = r1.take("rn", [P, T])
        pd = r1.take("pd", [P, T])
        pi = r1.take("pi", [P, T])
        kf = r1.take("kf", [P, T])
        bv = r1.take("bv", [P, T])
        kkn = r1.take("kkn", [P, T])
        bU = r1.take("bU", [P, T])
        ar = r1.take("ar", [P, 2, T])
        Y = r1.take("Y", [P, G, C])
        Tm = r1.take("Tm", [P, G, C])
        ARB = r1.take("ARB", [P, G, C])
        ARK = r1.take("ARK", [P, G, C])
        Vs = r1.take("Vs", [P, G, C])
        Us = r1.take("Us", [P, G, C])
        Ss = r1.take("Ss", [P, G, C])
        Sd = r1.take("Sd", [P, C])
        RHS = r1.take("RHS", [P, 2, C])
        Zs = r1.take("Zs", [P, 2, C])
        tail4 = r1.take("tail4", [P, 2, 2, C])
        tails = r1.take("tails", [P, 2, C])
        xpB = at(used["sq"][0], "xpB", [P, NB, C])
        xpK = r1.take("xpK", [P, NB, C])
        so = r1.take("so", [P, NB, C])
        zr = at(used["Y"][0], "zr", [P, NB, 2 * TB + C])
        S0D = at(used["S0T"][0], "S0D", [P, NB, C])
        assert used["zr"][1] <= used["Tm"][1]
        eo = r1.take("eo", [P, P])
        O_s, dO, dsq, sd = cl, pd, pi, kf
        uS = r1.take("uS", [P, 8, T])
        r2 = Region(used["gS"][1])
        gt = r2.take("gt", [P, 4, T])
        ue = r2.take("ue", [P, 2, EXT])
        win_a = r2.take("win_a", [P, 2, EXT])
        win_b = r2.take("win_b", [P, 2, EXT])
        spt = r2.take("spt", [NB * BUF, R])
        utok = at(used["spt"][0], "utok", [NB * TB + BUF, R])
        pw = r2.take("pw", [P, 8, PGROUP])
        head = r2.take("head", [P, 2, 16])
        yah = r2.take("yah", [P, PAIRS * T], F32R)
        yal = r2.take("yal", [P, PAIRS * T], F32R)
        ybh = r2.take("ybh", [P, 8 * T], F32R)
        ybl = r2.take("ybl", [P, 8 * T], F32R)
        gsig = at(used["ybl"][0], "gsig", [P, 8 * T])
        ue1 = at(used["ybh"][0], "ue1", [P, 2, EXT])
        ue2 = at((used["ue1"][1] + 7) // 8 * 8, "ue2", [P, 2, EXT])
        assert used["ue2"][1] <= used["ybh"][1]
        ues = (ue, ue1, ue2, ue)
        ytmp = at(used["t1"][0], "ytmp", [P, 2, T])
        mh = at(ya_start, "mh", [P, KT * T], F32R)
        r3 = Region(used["gt"][1])
        ml = r3.take("ml", [P, KT * T], F32R)
        ga = r3.take("ga", [P, 2, T])
        assert r3.next <= used["yah"][0] and r2.next <= used["uS"][0]
        r4 = Region(used["uS"][0])
        gb = r4.take("gb", [P, 2, T])
        sacc = r4.take("sacc", [P, T])
        mm_ = at(used["t1"][0], "mm", [P, 2, T])
        xT = at(used["yah"][0], "xT", [P, KT * T])
        o2 = at(used["ybh"][0], "o2", [P, KT * T])
        r5 = Region(arena)
        sqo = r5.take("sqo", [P, 2, T])
        pT = r5.take("pT", [P, 2, T])
        wple = r5.take("wple", [P, 2, 2 * P])
        yo = r5.take("yo", [P, 2, T])
        emb = at(used["ml"][0], "emb", [P, EMB, T])
        wple0 = r4.take("wple0", [P, EMB - 2, 2 * P])
        assert r5.next <= used["gt"][1]
        g3 = ga
        ytk = at(ya_start, "ytk", [P, 2, 3 * P])
        xt2 = at(used["hh"][0], "xt2", [P, 3, D])
        pt = at(used["xt2"][1], "pt", [P, 3, PLE])
        x1h = at(used["hh"][0], "x1h", [P, KT * T], F32R)
        x1l = at(used["hl"][0], "x1l", [P, KT * T], F32R)
        end = max(b for _, b in used.values())
        room = (nc.sbuf_usable_end if not callable(nc.sbuf_usable_end) else nc.sbuf_usable_end())
        assert base + 4 * end <= room, (base + 4 * end, room)
        assert used["S0n"][0] >= used["xw"][1] and used["S0n"][1] <= used["hT"][0]
        assert used["pt"][1] <= used["hl"][1] and used["la1"][1] <= used["gp"][1]

        acc = [ctx.enter_context(nc.psum_tensor(f"acc{i}", [P, 512], F32)) for i in range(2)]
        B01, B23, B45 = [ctx.enter_context(nc.psum_tensor(f"wide{i}", [P, 1024], F32)) for i in range(3)]
        B = [w[:, 512 * i:512 * (i + 1)] for w in (B01, B23, B45) for i in range(2)]

        sems = {}
        for name in """y_out0 y_out1 wple_in0 wple_in1 lo_ready x_in0 x_in1 x_in2 eout sout const_in rows_in map_in filled
            last_done rows_out cur_p_ready lw2_in s0_in par_done xw_ready xw_used cur_m_ready acc_free vbd_ready
            a_ready kf_ready sg_ready sgs_ready exp_ready api_ready kbd_ready bbd_ready tail_ready dpl_ready
            tails_ready xpk_ready end_ready send_ready lora2_ps s0_ps yal_ready pool_in utok_ev chunk_used x2_in
            xT_ready x1a x1b ytk_ready ple_ps hi_ready zsh_ready hT_ps x_stat hT_done hh_done dh_done last_ps act_start
            s0t_ready ksq_ready decay_in kk_max kk_norm cum_ready cumx_ready ah_ready bh_ready z_ps zabd_ready vt_ps
            vs_ready bt_ps y_ready ybd_ready x_ps x_ready kt_ps tail_ps s_ready sd_ready endbd_ready
            sbd_ready ubd_ready end_ps o_ps o_ready send_ps dev_ready dsq_ready var_ps sd_done y_done yah_ready gsil_ready
            gsig_ready yb_ready gates_ready yb_done utok_ps sb_ready m_ready mh_ready so_ready xT_ps pT_ps emb_done sacc_ready ssq_ps srt
            x1h_ready g3_ready yt_ps par_ready chain h_rows h_split hl_done kk_ps kk_rn rk_ready kkn_ready rh_ready rk_ps
            bv_ready score_ps ark_ready t_ps t_ready m_ps rhs_ps rhs_ready u_ps u_ready
            s_ps xpb_ready mean_ps mixed pyb_ps ybl_ready mb_ready ml_ready o2_ready x1l_ready g3m yo_ready raw0 raw1
            raw2 raw3 dve_step waits""".split():
            sems[name] = ctx.enter_context(nc.semaphore(name))
        s = sems

        def cfs(name):
            a, b = CF[name]
            return cf[:, a:b]

        def cms(name):
            a, b = CM[name]
            return cm[:, a:b]

        ident, istk, ones2, mean2, meand = [cfs(n) for n in ("ident", "istk", "ones2", "mean2", "meand")]

        def half(q):
            return slice(HD * q, HD * q + HD)

        def grp(t):
            return t[:, :].rearrange("p (g c) -> p g c", g=G)

        def flat(t, g):
            return t[:, g].rearrange("p h c -> p (h c)")

        def tok(g):
            return slice(C * g, C * g + C)

        w_in_v = w_in[0].rearrange("(k p) n -> p k n", p=P)
        wa_v = w_branch[0, 0].rearrange("(k p) n -> p k n", p=P)
        wb_v = w_branch[0, 1].rearrange("(k p) n -> p k n", p=P)
        wo_v = w_out[0].rearrange("(k p) n -> p k n", p=P)
        wg_v = w_ple_gate[0].rearrange("(k p) n -> p k n", p=P)
        wple_v = w_ple[0].rearrange("(k p) n -> p k n", p=P)

        block = ctx.enter_context(nc.Block())

        @block.sync
        def _(sp):
            def load(view, k0, col, count, j, free=True):
                slot = j % SLOTS
                if free:
                    sp.wait_ge(s["lo_ready"], count + j - (SLOTS - 1))
                    sp.sem_inc(s["waits"], 1)
                sp.dma_start(wraw[:, slot, :].rearrange("p (k n) -> p k n", k=KC),
                             view[:, k0:k0 + KC, ds(col, P)]).then_inc(s[f"raw{slot}"], 16)

            def load_tiles(cols, count, free):
                for n, col in enumerate(cols):
                    for h in range(2):
                        j = 2 * n + h
                        load(w_in_v, KC * h, col, count, j, free=free or j >= SLOTS)

            sp.dma_start(xt[:, 0, :], x_prompt[0, 0:P, :]).then_inc(s["x_in0"], 16)
            sp.dma_start(cf[:, :], const_f).then_inc(s["const_in"], 16)
            row = 0
            for v in [mu_rkv[0].rearrange("a (q p) -> (a q) p", p=P)] + [
                    v[0].rearrange("(q p) -> q p", p=P) for v in (w0, a0, k_k, k_a, r_k, ln_w, ln_b)]:
                n = v.shape[0]
                sp.dma_start(rows[row:row + n, 0, :], v).then_inc(s["rows_in"], 16)
                row += n
            row = 0
            for v in (norm_pre[0].rearrange("(q p) -> q p", p=P), norm_post[0].rearrange("(q p) -> q p", p=P),
                      mu_lora[0].rearrange("a (q p) -> (a q) p", p=P)[0:32, :], pool_scale[0].rearrange("(q p) -> q p", p=P)):
                n = v.shape[0]
                sp.dma_start(rows[row:row + n, 1, :], v).then_inc(s["rows_in"], 16)
                row += n
            sp.dma_start(xt[:, 1, :], x_prompt[0, P:TP, :]).then_inc(s["x_in1"], 16)
            sp.dma_start(xt[0:NB * TB, 2, :], x_sample.rearrange("b t d -> (b t) d")).then_inc(s["x_in2"], 16)
            sp.dma_start(xt[NB * TB:NB * TB + NB, 2, :], state_shift[0]).then_inc(s["x_in2"], 16)
            load_tiles((COL_K, COL_R, COL_V, COL_G), 0, free=False)
            with sp.Fori(1, PAIRS) as q:
                load_tiles([q * P + c for c in (COL_K, COL_R, COL_V, COL_G, COL_U - P, COL_GP - P)],
                           q * CH_STEP + BASE_STEP, free=True)
            load_tiles((COL_GA, COL_GB, COL_GA + P, COL_GB + P, COL_U + 7 * P, COL_GP + 7 * P),
                       PAIRS * CH_STEP + BASE_STEP, free=True)
            load_tiles((COL_GA + 2 * P, COL_GB + 2 * P, COL_GA + 3 * P, COL_GB + 3 * P), BASE_EARLY, free=True)
            for b, view in enumerate((wa_v, wb_v)):
                for i in range(EARLY):
                    load(view, 0, i * P, BASE_EARLY + 2 * EARLY, EARLY * b + i)
            with sp.Fori(EARLY // 2, KT // 2) as n:
                for m in range(2):
                    for j, (view, k0, col) in enumerate(((w_in_v, 0, COL_GA), (w_in_v, KC, COL_GA), (w_in_v, 0, COL_GB),
                                                         (w_in_v, KC, COL_GB), (wa_v, 0, 0), (wb_v, 0, 0))):
                        load(view, k0, n * (2 * P) + (m * P + col), n * (2 * CH_MERGE) + BASE_MERGE, CH_MERGE * m + j)
            for view, start in ((wo_v, BASE_OUT), (wg_v, BASE_GATE)):
                with sp.Fori(0, KT // 2) as n:
                    for m in range(2):
                        for h in range(2):
                            load(view, KC * h, n * (2 * P) + m * P, n * 4 + start, 2 * m + h)

        @block.gpsimd
        def _(pool):
            gp_ = nc.gpsimd

            def wait_alone(name, value):
                pool.wait_ge(s[name], value)
                pool.sem_inc(s["waits"], 1)

            pool.wait_ge(s["x_in1"], 16)
            pool.dma_start(cm[:, :], const_m).then_inc(s["map_in"], 16)
            pool.dma_start(lw1[:, :, :], w1[0].rearrange("(k p) n -> p k n", p=P)).then_inc(s["map_in"], 16)
            pool.dma_start(la1[:, :, :], a1[0].rearrange("(k p) n -> p k n", p=P)).then_inc(s["map_in"], 16)
            gp_.memset(zsh[:, 0:1], 0.0).then_inc(s["filled"], 1)

            def pair_params(q):
                gp_.tensor_copy(cur_p[:, :], par[:, :].rearrange("p (n q) -> p n q", q=PAIRS)[:, :, ds(q, 1)]
                                .rearrange("p n q -> p (n q)")).then_inc(s["cur_p_ready"], 1)

            def pair_loads(q):
                pool.dma_start(lw2[:, :], w2[0][:, ds(q * P, P)]).then_inc(s["lw2_in"], 16)
                pool.dma_start(la2[:, :], a2[0][:, ds(q * P, P)]).then_inc(s["lw2_in"], 16)
                for h in range(2):
                    pool.dma_start(S0n[half(h), :, half(h)],
                                   state_wkv[0].rearrange("b h i j -> i b h j")[:, :, ds(q * 2 + h, 1), :]
                                   .rearrange("i b h j -> i b (h j)")).then_inc(s["s0_in"], 16)

            pool.wait_ge(s["par_done"], 4)
            pair_params(0)
            for j in range(SLOTS):
                pool.wait_ge(s["hi_ready"], j + 1)
                gp_.tensor_tensor(wl[:, j, :], wraw[:, j, :], wh[:, j, :].bitcast(F32), ALU.subtract).then_inc(s["lo_ready"], 1)
            pool.wait_ge(s["hT_ps"], 12)
            gp_.memset(S0n[:], 0.0).then_inc(s["filled"], 1)
            pool.wait_ge(s["hh_done"], 4)
            gp_.tensor_tensor(hl[:, 12 * TS:16 * TS], hT[:, 12 * TS:16 * TS], hh[:, 12 * TS:16 * TS].bitcast(F32),
                              ALU.subtract).then_inc(s["hl_done"], 1)
            pool.wait_ge(s["filled"], 2)
            pair_loads(0)
            pool.wait_ge(s["last_done"], 2)
            for n in range(2):
                src = hlastT[:, P * n:P * (n + 1)]
                pool.dma_start(shift_prompt[0, 0].rearrange("(k p) -> k p", p=P)[8 * n:8 * n + 8, :],
                               src[0:8, :]).then_inc(s["rows_out"], 16)
                for k in range(8):
                    pool.dma_start(shift_sample[0, :, P * (8 * n + k):P * (8 * n + k + 1)],
                                   src[8 + NB * k:8 + NB * (k + 1), :]).then_inc(s["rows_out"], 16)
            pool.wait_ge(s["rows_out"], 16 * 18)
            pool.wait_ge(s["xw_ready"], 2 * KT)
            pool.wait_ge(s["xw_used"], 2 * KT)
            blocks = (vBD, aBD, bBD, kBD, YBD, ZaBD, EndBD)
            for t in blocks:
                gp_.memset(t[:], 0.0).then_inc(s["filled"], 1)
            pool.wait_ge(s["filled"], 2 + len(blocks))

            def mix(r):
                gp_.tensor_copy(cur_m[:, :], par[:, :].rearrange("p (n q) -> p n q", q=PAIRS)[:, :, ds(r, 1)]
                                .rearrange("p n q -> p (n q)")).then_inc(s["cur_m_ready"], 1)
                wait_alone("cur_m_ready", r + 1)
                wait_alone("acc_free", r * TILES_STEP + (ACC_STEP + TILES_STEP))
                for h in range(2):
                    gp_.tensor_copy(vBD[half(h), :, h, :], grp(vS)[half(h)]).then_inc(s["vbd_ready"], 1)
                wait_alone("vbd_ready", r * 2 + 2)
                wait_alone("a_ready", r + 1)
                gp_.tensor_scalar(kf[:, :], aS[:, :], cur_m[:, K_A:K_A + 1], cur_m[:, OM_KA:OM_KA + 1],
                                  ALU.mult, ALU.add).then_inc(s["kf_ready"], 1)
                wait_alone("kf_ready", r * 2 + 1)
                gp_.tensor_tensor(kf[:, :], kf[:, :], kS[:, :], ALU.mult).then_inc(s["kf_ready"], 1)
                wait_alone("sg_ready", r + 1)
                gp_.tensor_tensor(sg[:, :], sg[:, :], gS[:, :], ALU.mult).then_inc(s["sgs_ready"], 1)
                wait_alone("exp_ready", r * 3 + 3)
                gp_.tensor_tensor(aS[:, :], aS[:, :], pi[:, :], ALU.mult).then_inc(s["api_ready"], 1)
                wait_alone("api_ready", r + 1)
                pl = pd[:, TP:T].rearrange("p (b t) -> p b t", t=TB)[:, :, TB - 1:TB]
                gp_.tensor_tensor(zr[:, :, 2 * TB:2 * TB + C], istk.unsqueeze(1).to_broadcast([P, NB, C]),
                                  pl.to_broadcast([P, NB, C]), ALU.mult).then_inc(s["dpl_ready"], 1)
                wait_alone("dpl_ready", r + 1)
                for h in range(2):
                    gp_.tensor_tensor(kBD[half(h), :, h, :], grp(kf)[half(h)], grp(pi)[half(h)],
                                      ALU.mult).then_inc(s["kbd_ready"], 1)
                wait_alone("kbd_ready", r * 2 + 2)

            def mix_sample(r):
                wait_alone("bbd_ready", r * 2 + 2)
                pl = pd[:, TP:T].rearrange("p (b t) -> p b t", t=TB)[:, :, TB - 1:TB]
                for n, t in enumerate((bBD, kBD)):
                    gp_.tensor_tensor(tail4[:, n].rearrange("p h (b t) -> p h b t", t=TB),
                                      t[:, G - 1].rearrange("p h (b t) -> p h b t", t=TB),
                                      pl.unsqueeze(1).to_broadcast([P, 2, NB, TB]), ALU.mult).then_inc(s["tail_ready"], 1)

            def mix_out(r):
                wait_alone("tails_ready", r * 2 + 2)
                bm = cfs("batch").unsqueeze(2).to_broadcast([P, NB, C])
                gp_.tensor_tensor(xpK[:, :, :], tails[:, 1, :].unsqueeze(1).to_broadcast([P, NB, C]), bm,
                                  ALU.mult).then_inc(s["xpk_ready"], 1)
                wait_alone("end_ready", r + 1)
                for h in range(2):
                    pool.dma_start(wkv_prompt[0, 0][ds(r * 2 + h, 1)].rearrange("h i j -> (h i) j"),
                                   eo[half(h), half(h)]).then_inc(s["eout"], 16)
                wait_alone("send_ready", r + 1)
                for h in range(2):
                    pool.dma_start(wkv_sample[0].rearrange("b h i j -> i b h j")[:, :, ds(r * 2 + h, 1), :]
                                   .rearrange("i b h j -> i b (h j)"), so[half(h), :, :]).then_inc(s["sout"], 16)
                wait_alone("eout", r * 32 + 32)
                wait_alone("sout", r * 32 + 32)

            with pool.Fori(1, PAIRS) as q:
                r = q - 1
                wait_alone("acc_free", q * TILES_STEP + ACC_STEP)
                pair_params(q)
                mix(r)
                mix_sample(r)
                wait_alone("lora2_ps", q)
                wait_alone("s0_ps", q)
                pair_loads(q)
                mix_out(r)
            pool.wait_ge(s["acc_free"], PAIRS * TILES_STEP + ACC_STEP)
            mix(PAIRS - 1)
            mix_sample(PAIRS - 1)
            mix_out(PAIRS - 1)

            pool.wait_ge(s["y_done"], PAIRS)
            pool.dma_start(spt[:, :], state_pool[0].rearrange("b t c -> (b t) c")).then_inc(s["pool_in"], 16)
            for t in ues[0:3]:
                gp_.memset(t[:, :, 0:BUF], 0.0).then_inc(s["filled"], 1)

            def halo_tokens(g):
                u = uS[:, 2 * g:2 * g + 2, :]
                gp_.tensor_copy(ues[g][:, :, BUF:BUF + TP], u[:, :, 0:TP]).then_inc(s["filled"], 1)
                gp_.tensor_copy(ues[g][:, :, BUF + TP:EXT].rearrange("p k (b t) -> p k b t", b=NB)[:, :, :, BUF:BUF + TB],
                                u[:, :, TP:T].rearrange("p k (b t) -> p k b t", b=NB)).then_inc(s["filled"], 1)

            for g in range(3):
                halo_tokens(g)
            pool.dma_start(pw[:, :, :], pool_w[0].rearrange("g (k p) n -> p (g k) n", p=P)).then_inc(s["map_in"], 16)
            pool.dma_start(pool_sample[0, :, 0:BUF - TB, :], state_pool[0, :, TB:BUF, :]).then_inc(s["rows_out"], 16)
            pool.wait_ge(s["mixed"], 4)
            halo_tokens(3)
            pool.wait_ge(s["yah_ready"], 1)
            gp_.tensor_tensor(yal[:, :], yf[:, :], yah[:, :].bitcast(F32), ALU.subtract).then_inc(s["yal_ready"], 1)
            pool.wait_ge(s["gsig_ready"], 1)
            gp_.tensor_tensor(gp[:, :, :].rearrange("p k t -> p (k t)"), gp[:, :, :].rearrange("p k t -> p (k t)"),
                              gsig[:, :], ALU.mult).then_inc(s["gsil_ready"], 1)
            pool.wait_ge(s["utok_ev"], 2)
            pool.dma_start(pool_prompt[0, 0], utok[0:BUF, :]).then_inc(s["rows_out"], 16)
            for b in range(NB):
                pool.dma_start(pool_sample[0, b, BUF - TB:BUF, :],
                               utok[BUF + TB * b:BUF + TB * (b + 1), :]).then_inc(s["rows_out"], 16)
            for m in range(8):
                pool.wait_ge(s["yb_done"], m + 1)
                gp_.tensor_tensor(ybl[:, m * T:(m + 1) * T], ytmp[:, m % 2, :], ybh[:, m * T:(m + 1) * T].bitcast(F32),
                                  ALU.subtract).then_inc(s["ybl_ready"], 1)
            pool.wait_ge(s["rows_out"], 16 * (18 + 1 + 1 + NB))

            pool.wait_ge(s["chunk_used"], BASE_OUT)
            pool.dma_start(xt2[:, 0, :], x_prompt[0, 0:P, :]).then_inc(s["x2_in"], 16)
            pool.dma_start(xt2[:, 1, :], x_prompt[0, P:TP, :]).then_inc(s["x2_in"], 16)
            pool.dma_start(xt2[0:NB * TB, 2, :], x_sample.rearrange("b t d -> (b t) d")).then_inc(s["x2_in"], 16)
            pool.dma_start(pt[:, 0, :], p_prompt[0, 0, 0:P, :]).then_inc(s["x2_in"], 16)
            pool.dma_start(pt[:, 1, :], p_prompt[0, 0, P:TP, :]).then_inc(s["x2_in"], 16)
            pool.dma_start(pt[0:NB * TB, 2, :], p_sample[0].rearrange("b t d -> (b t) d")).then_inc(s["x2_in"], 16)
            for m in range(EMB):
                to = wple[:, m, :] if m < 2 else wple0[:, m - 2, :]
                pool.dma_start(to.rearrange("p (k n) -> p k n", k=2),
                               wple_v[:, :, m * P:(m + 1) * P]).then_inc(s["map_in"], 16)
            for k in range(KT):
                pool.wait_ge(s["xT_ready"], k + 1)
                pool.wait_ge(s["x1a"], k + 1)
                gp_.tensor_tensor(xT[:, T * k:T * (k + 1)], xT[:, T * k:T * (k + 1)], o2[:, T * k:T * (k + 1)],
                                  ALU.add).then_inc(s["x1b"], 1)

            def store(n, m):
                wait_alone("ytk_ready", n * 4 + 2 * m + 2)
                col = n * (2 * P) + m * P
                pool.dma_start(y_prompt[0].rearrange("(a p) d -> p a d", p=P)[:, :, ds(col, P)],
                               ytk[:, m, 0:2 * P].rearrange("p (a n) -> p a n", a=2)).then_inc(s[f"y_out{m}"], 16)
                pool.dma_start(y_sample.rearrange("b t d -> (b t) d")[:, ds(col, P)],
                               ytk[0:NB * TB, m, 2 * P:3 * P]).then_inc(s[f"y_out{m}"], 16)

            pool.wait_ge(s["ple_ps"], 2)
            for m in range(2):
                pool.dma_start(wple[:, m, :].rearrange("p (k n) -> p k n", k=2),
                               wple_v[:, :, (EMB + m) * P:(EMB + m + 1) * P]).then_inc(s[f"wple_in{m}"], 16)
            with pool.Fori(0, EMB // 2) as n:
                for m in range(2):
                    store(n, m)
            with pool.Fori(EMB // 2, KT // 2 - 1) as n:
                for m in range(2):
                    wait_alone("ple_ps", n * 2 + m + 1)
                    pool.dma_start(wple[:, m, :].rearrange("p (k n) -> p k n", k=2),
                                   wple_v[:, :, ds(n * (2 * P) + (m + 2) * P, P)]).then_inc(s[f"wple_in{m}"], 16)
                    store(n, m)
            for m in range(2):
                store(KT // 2 - 1, m)
            pool.wait_ge(s["y_out0"], 16 * KT)
            pool.wait_ge(s["y_out1"], 16 * KT)

        @block.scalar
        def _(act):
            A = nc.scalar

            def split_hi(count, j, rounds):
                slot = j % SLOTS
                act.wait_ge(s[f"raw{slot}"], rounds * 16 + 16)
                if not (isinstance(count, int) and count + j < SLOTS):
                    act.wait_ge(s["chunk_used"], count + j - (SLOTS - 1))
                A.copy(wh[:, slot, :], wraw[:, slot, :]).then_inc(s["hi_ready"], 1)

            def ahead(count, rounds, j):
                jj = j + AHEAD
                split_hi(count, jj, rounds + jj // SLOTS)

            def evac_mixed(mu, bank, used_chunks, last):
                act.wait_ge(s["chunk_used"], used_chunks)
                act.wait_ge(s["acc_free"], last)
                act.wait_ge(s["cur_p_ready"], mu[1])
                m = cur_p[:, mu[0]:mu[0] + 1]
                A.mul(zsh[:, 1:TP], bank[:, 0:TP - 1], m)
                zb = zsh[:, TP:T].rearrange("p (b t) -> p b t", t=TB)
                A.mul(zb[:, :, 1:TB], bank[:, TP:T].rearrange("p (b t) -> p b t", t=TB)[:, :, 0:TB - 1], m)
                A.mul(zb[:, :, 0], bank[:, T:TS], m).then_inc(s["zsh_ready"], 1)

            act.wait_ge(s["const_in"], 16)
            for t in range(3):
                n = P if t < 2 else NB * TB
                act.wait_ge(s[f"x_in{t}"], 16 if t < 2 else 32)
                A.activation(hT[0:n, KT * TS - D:KT * TS], xt[0:n, t, :], ACT.Square, accum_out=stat[0:n, t:t + 1]).then_inc(s["x_stat"], 1)
                act.wait_ge(s["x_stat"], 2 * t + 1)
                A.activation(stat[0:n, t:t + 1], stat[0:n, t:t + 1], ACT.Sqrt, scale=1.0 / D,
                             bias=cfs("eps")[0:n, 0:1]).then_inc(s["x_stat"], 1)
            for j in range(SLOTS):
                split_hi(0, j, 0)
            act.wait_ge(s["hT_ps"], 4)
            A.copy(ht[NB * TB:NB * TB + NB, 0, :], xt[NB * TB:NB * TB + NB, 2, :]).then_inc(s["act_start"], 1)
            for c in range(4):
                act.wait_ge(s["hT_done"], 8 + 2 * (c + 1))
                A.copy(hh[:, 4 * c * TS:4 * (c + 1) * TS], hT[:, 4 * c * TS:4 * (c + 1) * TS]).then_inc(s["hh_done"], 1)
            act.wait_ge(s["dh_done"], 4)
            act.wait_ge(s["last_ps"], 2)
            A.copy(hlastT[:, 0:P], B[4][0:72, 0:P]).then_inc(s["last_done"], 1)
            A.copy(hlastT[:, P:2 * P], B[5][0:72, 0:P]).then_inc(s["last_done"], 1)

            def tile_out(q, n):
                if n < 3 and not isinstance(q, int):
                    evac_mixed(((MU_K, MU_R, MU_V)[n], q + 1), acc[n % 2], q * CH_STEP + (BASE_STEP + 2 * n + 2),
                               q * TILES_STEP + (ACC_STEP + n))

            for j in range(CH_FIRST):
                if j + AHEAD >= SLOTS:
                    ahead(0, 0, j)
                if j % 2 == 1 and j < 7:
                    n = j // 2
                    act.wait_ge(s["chunk_used"], 2 * n + 2)
                    if n:
                        act.wait_ge(s["acc_free"], n)
                    act.wait_ge(s["cur_p_ready"], 1)
                    act.wait_ge(s["filled"], 1)
                    m = cur_p[:, (MU_K, MU_R, MU_V)[n]:(MU_K, MU_R, MU_V)[n] + 1]
                    bank = acc[n % 2]
                    A.mul(zsh[:, 1:TP], bank[:, 0:TP - 1], m)
                    zb = zsh[:, TP:T].rearrange("p (b t) -> p b t", t=TB)
                    A.mul(zb[:, :, 1:TB], bank[:, TP:T].rearrange("p (b t) -> p b t", t=TB)[:, :, 0:TB - 1], m)
                    A.mul(zb[:, :, 0], bank[:, T:TS], m).then_inc(s["zsh_ready"], 1)
            act.wait_ge(s["xw_used"], 2 * KT)
            A.activation(t1[:, :], B[0][0:RANK, 0:T], ACT.Tanh).then_inc(s["act_start"], 1)
            A.copy(la[:, :], B[1][0:RANK, 0:T]).then_inc(s["act_start"], 1)

            def mix(r, q):
                def go(j):
                    ahead(q * CH_STEP + BASE_STEP, q * (CH_STEP // SLOTS) + BASE_STEP // SLOTS, j)

                def out(n):
                    tile_out(q, n)

                go(0)
                act.wait_ge(s["cur_m_ready"], r + 1)
                A.activation(sq[:, :], kS[:, :], ACT.Square, scale=cur_m[:, K_K:K_K + 1]).then_inc(s["ksq_ready"], 1)
                act.wait_ge(s["s0_ps"], r + 1)
                A.copy(S0T[:, :, :].rearrange("p b c -> p (b c)"), B45[:, :]).then_inc(s["s0t_ready"], 1)
                act.wait_ge(s["lora2_ps"], r + 1)
                A.activation(pm[:, :], B[0][:, 0:T], ACT.Sigmoid, bias=cur_m[:, W0:W0 + 1]).then_inc(s["decay_in"], 1)
                A.activation(aS[:, :], B[1][:, 0:T], ACT.Sigmoid, bias=cur_m[:, A0:A0 + 1]).then_inc(s["a_ready"], 1)
                A.activation(sg[:, :], gS[:, :], ACT.Sigmoid).then_inc(s["sg_ready"], 1)
                act.wait_ge(s["kk_max"], r + 1)
                A.activation(rn[:, :], rn[:, :], ACT.Sqrt).then_inc(s["kk_norm"], 1)
                act.wait_ge(s["cum_ready"], r + 1)
                A.activation(pi[:, :], cl[:, :], ACT.Exp, scale=DECAY).then_inc(s["exp_ready"], 1)
                A.activation(pd[:, :], cl[:, :], ACT.Exp, scale=-DECAY).then_inc(s["exp_ready"], 1)
                act.wait_ge(s["cumx_ready"], r + 1)
                A.activation(pm[:, :], pm[:, :], ACT.Exp, scale=-DECAY).then_inc(s["exp_ready"], 1)
                go(1)
                act.wait_ge(s["vt_ps"], r + 1)
                A.copy(VtBD[:, :, :, :].rearrange("p g h c -> p (g h c)"), B45[:, 0:2 * T])
                for h in range(2):
                    A.copy(Vs[half(h)], B45[half(h), 0:2 * T].rearrange("p (g h c) -> p g h c", g=G, h=2)[:, :, h, :]
                           ).then_inc(s["vs_ready"], 1)
                act.wait_ge(s["ah_ready"], r + 1)
                for h in range(2):
                    A.copy(aBD[half(h), :, h, :], ar[half(h), 0, :].rearrange("p (g c) -> p g c", g=G))
                act.wait_ge(s["bh_ready"], r + 1)
                for h in range(2):
                    A.copy(bBD[half(h), :, h, :], grp(bU)[half(h)]).then_inc(s["bbd_ready"], 1)
                go(2)
                out(0)
                act.wait_ge(s["z_ps"], r + 1)
                zp = B45.rearrange("p (b n) -> p b n", b=NB)
                A.copy(Zs[:, 1, :].rearrange("p (b t) -> p b t", t=TB), zp[:, :, TB:2 * TB])
                A.copy(S0D[:, :, :], zp[:, :, 2 * TB:2 * TB + C]).then_inc(s["s0t_ready"], 1)
                for h in range(2):
                    A.copy(ZaBD[half(h), h, :].rearrange("p (b t) -> p b t", t=TB), zp[half(h), :, 0:TB]
                           ).then_inc(s["zabd_ready"], 1)
                go(3)
                act.wait_ge(s["bt_ps"], r + 1)
                A.copy(BtBD[:, :, :, :].rearrange("p g h c -> p (g h c)"), B45[:, 0:2 * T])

                def ybd(n):
                    gs = G if n <= SMALL else GP
                    act.wait_ge(s["y_ready"], r * (LEVELS + ROUNDS + 1) + (ROUNDS + n + 1))
                    for h in range(2):
                        A.copy(YBD[half(h), 0:gs, h, :], Y[half(h), 0:gs]).then_inc(s["ybd_ready"], 1)

                def xbd(n):
                    gs = G if n < SMALL else GP
                    act.wait_ge(s["x_ps"], r * LEVELS + n + 1)
                    A.copy(XBD[:, 0:gs].rearrange("p g h c -> p (g h c)"), B45[:, 0:2 * C * gs]).then_inc(s["x_ready"], 1)

                act.wait_ge(s["kt_ps"], r + 1)
                A.copy(KtBD[:, :, :, :].rearrange("p g h c -> p (g h c)"), B23[:, 0:2 * T])
                go(4)
                out(1)
                for n in range(LEVELS):
                    ybd(n)
                    xbd(n)
                    if n:
                        go(4 + n)
                    if n == 2:
                        out(2)
                ybd(LEVELS)
                act.wait_ge(s["tail_ps"], r + 1)
                for h in range(2):
                    A.copy(tails[half(h)], B[5][half(h), 0:4 * C].rearrange("p (n h c) -> p n h c", n=2, h=2)[:, :, h, :]
                           ).then_inc(s["tails_ready"], 1)
                for g in range(GP):
                    if g:
                        act.wait_ge(s["s_ready"], r * GP + g)
                        A.mul(Sd[:, :], Ss[:, g - 1, :], pd[:, C * g + C - 1:C * g + C]).then_inc(s["sd_ready"], 1)
                    if g in (1, 3):
                        go(8 + g // 2)
                act.wait_ge(s["u_ready"], r * GP + GP)
                for h in range(2):
                    A.copy(UBD[half(h), :, h, :], Us[half(h)]).then_inc(s["ubd_ready"], 1)
                act.wait_ge(s["s_ready"], r * GP + GP)
                for h in range(2):
                    A.copy(SBD[half(h), 0:GP - 1, h, :], Ss[half(h), 0:GP - 1, :]).then_inc(s["sbd_ready"], 1)
                for h in range(2):
                    A.copy(EndBD[half(h), h, :], Ss[half(h), GP - 1, :]).then_inc(s["endbd_ready"], 1)
                go(10)
                act.wait_ge(s["o_ps"], r + 1)
                A.copy(O_s[:, :], B[4][:, 0:T]).then_inc(s["o_ready"], 1)
                act.wait_ge(s["end_ps"], r + 1)
                A.copy(eo[:, :], B[0][:, 0:P]).then_inc(s["end_ready"], 1)
                act.wait_ge(s["dev_ready"], r + 1)
                A.activation(dsq[:, :], dO[:, :], ACT.Square).then_inc(s["dsq_ready"], 1)
                go(11)
                act.wait_ge(s["var_ps"], r + 1)
                A.activation(sd[:, :], B[2][:, 0:T], ACT.Sqrt, bias=cfs("eps")[:, 1:2]).then_inc(s["sd_done"], 1)

            with act.Fori(1, PAIRS) as q:
                mix(q - 1, q)
            mix(PAIRS - 1, PAIRS)

            def early(j):
                ahead(BASE_EARLY, BASE_EARLY // SLOTS, j)

            def high_y(m):
                act.wait_ge(s["yb_ready"], m + 1)
                A.copy(ybh[:, m * T:(m + 1) * T], ytmp[:, m % 2, :]).then_inc(s["yb_done"], 1)

            early(0)
            act.wait_ge(s["y_done"], PAIRS)
            A.copy(yah[:, :], yf[:, :]).then_inc(s["yah_ready"], 1)
            act.wait_ge(s["acc_free"], ACC_ALL)
            early(1)
            for t in (kS, rS, vS, gS):
                A.activation(t[:, :], t[:, :], ACT.Sigmoid).then_inc(s["sb_ready"], 1)
            act.wait_ge(s["eout"], 32 * PAIRS)
            act.wait_ge(s["sout"], 32 * PAIRS)
            A.activation(gsig[:, :], gp[:, :, :].rearrange("p k t -> p (k t)"), ACT.Sigmoid).then_inc(s["gsig_ready"], 1)
            for j in range(2, 10):
                if j % 2 == 0:
                    g = j // 2 - 1
                    act.wait_ge(s["chunk_used"], BASE_EARLY + j)
                    A.activation(gt[:, g, :], acc[g % 2][:, 0:T], ACT.Sigmoid).then_inc(s["gates_ready"], 1)
                early(j)
                if j == 3:
                    act.wait_ge(s["utok_ps"], 4)
                    for n in range(2):
                        A.copy(utok[:, 512 * n:512 * (n + 1)], B[4 + n][0:NB * TB + BUF, :]).then_inc(s["utok_ev"], 1)

            early(10)
            for m in range(4):
                high_y(m)
            early(11)
            for m in range(4, 8):
                high_y(m)
            early(12)
            for i in range(EARLY):
                if i != 2:
                    early(13 + (i + 1) // 2)
                act.wait_ge(s["m_ready"], i + 1)
                A.copy(mh[:, T * i:T * (i + 1)], mm_[:, i % 2, :]).then_inc(s["mh_ready"], 1)

            with act.Fori(EARLY // 2, KT // 2) as n:
                for m in range(2):
                    i = n * 2 + m
                    bank = [acc[0], acc[1]] if m == 0 else [B[2], B[3]]
                    for j in range(CH_MERGE):
                        ahead(n * (2 * CH_MERGE) + BASE_MERGE, n * (2 * CH_MERGE // SLOTS) + BASE_MERGE // SLOTS,
                              CH_MERGE * m + j)
                        if j == 2:
                            act.wait_ge(s["chunk_used"], i * CH_MERGE + BASE_MERGE + 2)
                            A.activation(ga[:, m, :], bank[0][:, 0:T], ACT.Sigmoid)
                        if j == 4:
                            act.wait_ge(s["chunk_used"], i * CH_MERGE + BASE_MERGE + 4)
                            A.activation(gb[:, m, :], bank[1][:, 0:T], ACT.Sigmoid).then_inc(s["sb_ready"], 1)
                    act.wait_ge(s["m_ready"], i + 1)
                    A.copy(mh[:, ds(n * (2 * T) + m * T, T)], mm_[:, m, :]).then_inc(s["mh_ready"], 1)

            def square_tile(n, m):
                i = n * 2 + m
                for h in range(2):
                    ahead(n * 4 + BASE_OUT, n + BASE_OUT // SLOTS, 2 * m + h)
                act.wait_ge(s["chunk_used"], i * 2 + (BASE_OUT + 2))
                A.activation(sqo[:, m, :], acc[m][:, 0:T], ACT.Square).then_inc(s["so_ready"], 1)

            for m in range(2):
                square_tile(0, m)
            for k in range(KT):
                act.wait_ge(s["xT_ps"], k + 1)
                A.copy(xT[:, T * k:T * (k + 1)], B[k % 4][:, 0:T]).then_inc(s["xT_ready"], 1)
            for k in range(2):
                act.wait_ge(s["pT_ps"], k + 1)
                A.copy(pT[:, k, :], B[4 + k][:, 0:T]).then_inc(s["xT_ready"], 1)
            with act.Fori(1, KT // 2) as n:
                for m in range(2):
                    act.wait_ge(s["sacc_ready"], n * 2 + m - 1)
                    square_tile(n, m)
            act.wait_ge(s["sacc_ready"], KT)
            A.activation(sqo[:, 0, 0:1], cfs("eps")[:, 0:1], ACT.Sqrt)
            act.wait_ge(s["ssq_ps"], 1)
            A.activation(sacc[:, :], B[5][:, 0:T], ACT.Sqrt, bias=cfs("eps")[:, 0:1]).then_inc(s["srt"], 1)
            for k in range(KT):
                if k < EMB:
                    act.wait_ge(s["ple_ps"], k + 1)
                    A.copy(emb[:, k, :], B[k % 4][:, 0:T]).then_inc(s["emb_done"], 1)
                act.wait_ge(s["x1b"], k + 1)
                A.copy(x1h[:, T * k:T * (k + 1)], xT[:, T * k:T * (k + 1)]).then_inc(s["x1h_ready"], 1)

            def gate_tile(n, m, last=False):
                i = n * 2 + m
                for h in range(2):
                    if not last or 2 * m + h + AHEAD < 4:
                        ahead(n * 4 + BASE_GATE, n + BASE_GATE // SLOTS, 2 * m + h)
                act.wait_ge(s["chunk_used"], i * 2 + (BASE_GATE + 2))
                A.activation(g3[:, m, :], acc[m][:, 0:T], ACT.Sigmoid).then_inc(s["g3_ready"], 1)

            def token_tile(i, m, stored=None):
                act.wait_ge(s["yt_ps"], i + 1)
                if stored is not None:
                    act.wait_ge(s[f"y_out{m}"], stored)
                A.copy(ytk[:, m, 0:2 * P], B[2 + m][:, 0:2 * P]).then_inc(s["ytk_ready"], 1)
                A.copy(ytk[0:NB * TB, m, 2 * P:3 * P], B[2 + m][0:NB * TB, 2 * P:3 * P]).then_inc(s["ytk_ready"], 1)

            gate_tile(0, 0)
            gate_tile(0, 1)
            token_tile(0, 0)
            gate_tile(1, 0)
            token_tile(1, 1)
            gate_tile(1, 1)
            token_tile(2, 0, 32)
            with act.Fori(2, KT // 2 - 1) as n:
                gate_tile(n, 0)
                token_tile(n * 2 - 1, 1, n * 32 - 32)
                gate_tile(n, 1)
                token_tile(n * 2, 0, n * 32)
            n = KT // 2 - 1
            gate_tile(n, 0, last=True)
            token_tile(n * 2 - 1, 1, n * 32 - 32)
            gate_tile(n, 1, last=True)
            token_tile(n * 2, 0, n * 32)
            token_tile(n * 2 + 1, 1, n * 32)

        @block.vector
        def _(dve):
            V = nc.vector

            def split_lo(count, j):
                slot = j % SLOTS
                dve.wait_ge(s["hi_ready"], count + j + 1)
                V.tensor_tensor(wl[:, slot, :], wraw[:, slot, :], wh[:, slot, :].bitcast(F32), ALU.subtract
                                ).then_inc(s["lo_ready"], 1)

            def ahead(count, j):
                split_lo(count, j + AHEAD)

            def tile_out(q, n):
                if isinstance(q, int) and q == 0:
                    used_chunks = 2 * n + 2
                else:
                    used_chunks = q * CH_STEP + (BASE_STEP + 2 * n + 2)
                dve.wait_ge(s["chunk_used"], used_chunks)
                bank = acc[n % 2][:, 0:T]
                if n < 3 and not (isinstance(q, int) and q == PAIRS):
                    dve.wait_ge(s["zsh_ready"], q * 3 + n + 1)
                    V.scalar_tensor_tensor((kS, rS, vS)[n][:, :], bank, cur_p[:, (OM_K, OM_R, OM_V)[n]:(OM_K, OM_R, OM_V)[n] + 1],
                                           zsh[:, :], ALU.mult, ALU.add).then_inc(s["acc_free"], 1)
                elif n < 4:
                    V.tensor_copy((kS, rS, vS, gS)[n][:, :], bank).then_inc(s["acc_free"], 1)
                else:
                    t = (uS, gp)[n - 4][:, :, :].rearrange("p k t -> p (k t)")
                    where = slice(T * (q - 1), T * q) if isinstance(q, int) else ds(q * T - T, T)
                    V.tensor_copy(t[:, where], bank).then_inc(s["acc_free"], 1)

            dve.wait_ge(s["par_ready"], 2)
            V.tensor_copy(par[:, 0:NROW * PAIRS], B[4][:, 0:NROW * PAIRS]).then_inc(s["par_done"], 1)
            V.tensor_copy(par2[:, :], B[5][:, 0:NPAR2]).then_inc(s["par_done"], 1)
            dve.wait_ge(s["par_done"], 2)
            V.tensor_scalar(par[:, OM_R * PAIRS:(OM_V + 1) * PAIRS], par[:, 0:3 * PAIRS], -1.0, 1.0,
                            ALU.mult, ALU.add).then_inc(s["par_done"], 1)
            V.tensor_scalar(par[:, OM_KA * PAIRS:(OM_KA + 1) * PAIRS], par[:, K_A * PAIRS:(K_A + 1) * PAIRS], -1.0, 1.0,
                            ALU.mult, ALU.add).then_inc(s["par_done"], 1)
            hTv = hT[:, :].rearrange("p (k t) -> p k t", t=TS)
            hhv = hh[:, :].rearrange("p (k t) -> p k t", t=TS)
            hlv = hl[:, :].rearrange("p (k t) -> p k t", t=TS)

            def h_rows(t):
                n = P if t < 2 else NB * TB
                if t == 2:
                    dve.wait_ge(s["hT_ps"], 4)
                dve.wait_ge(s["x_stat"], 2 * t + 2)
                V.reciprocal(stat[0:n, t:t + 1], stat[0:n, t:t + 1]).then_inc(s["chain"], 1)
                dve.wait_ge(s["chain"], t + 1)
                V.tensor_scalar(ht[0:n, t % 2, :], xt[0:n, t, :], stat[0:n, t:t + 1], None, ALU.mult).then_inc(s["h_rows"], 1)

            def h_columns(t, cs=range(4)):
                for c in cs:
                    dve.wait_ge(s["hT_ps"], 4 * t + c + 1)
                    n = P if t < 2 else NB * TB
                    src = B[c][:, :].rearrange("p (k t) -> p k t", t=P)
                    V.tensor_tensor(hTv[:, 4 * c:4 * c + 4, P * t:P * t + n], src[:, :, 0:n],
                                    par2[:, NPRE + 4 * c:NPRE + 4 * c + 4].unsqueeze(2).to_broadcast([P, 4, n]),
                                    ALU.mult).then_inc(s["hT_done"], 1)
                    if t == 2:
                        V.tensor_copy(hTv[:, 4 * c:4 * c + 4, T:TS], src[:, :, n:n + NB]).then_inc(s["hT_done"], 1)

            h_rows(0)
            dve.wait_ge(s["par_done"], 4)
            h_columns(0, (0, 1))
            h_rows(1)
            dve.wait_ge(s["x_stat"], 6)
            h_columns(0, (2, 3))
            h_rows(2)
            h_columns(1)
            h_columns(2)
            for c in range(3):
                dve.wait_ge(s["hh_done"], c + 1)
                V.tensor_tensor(hl[:, 4 * c * TS:4 * (c + 1) * TS], hT[:, 4 * c * TS:4 * (c + 1) * TS],
                                hh[:, 4 * c * TS:4 * (c + 1) * TS].bitcast(F32), ALU.subtract).then_inc(s["h_split"], 1)
            dve.wait_ge(s["lo_ready"], SLOTS)
            dve.wait_ge(s["hT_done"], 16)
            for n in range(2):
                V.tensor_copy(hlast[:, 72 * n:72 * n + 8], hTv[:, 8 * n:8 * n + 8, TP - 1]).then_inc(s["dh_done"], 1)
                V.tensor_copy(hlast[:, 72 * n + 8:72 * n + 72].rearrange("p (k b) -> p k b", b=NB),
                              hTv[:, 8 * n:8 * n + 8, TP + TB - 1:T:TB]).then_inc(s["dh_done"], 1)
            dhv = dh[:, :].rearrange("p (k t) -> p k t", t=T)
            V.tensor_scalar(dhv[:, :, 0:1], hTv[:, :, 0:1], -1.0, None, ALU.mult).then_inc(s["dh_done"], 1)
            V.tensor_tensor(dhv[:, :, 1:TP], hTv[:, :, 0:TP - 1], hTv[:, :, 1:TP], ALU.subtract).then_inc(s["dh_done"], 1)
            for b in range(NB):
                a = TP + TB * b
                V.tensor_tensor(dhv[:, :, a + 1:a + TB], hTv[:, :, a:a + TB - 1], hTv[:, :, a + 1:a + TB],
                                ALU.subtract).then_inc(s["dh_done"], 1)
            V.tensor_tensor(dhv[:, :, TP:T:TB], hTv[:, :, T:TS], hTv[:, :, TP:T:TB], ALU.subtract).then_inc(s["dh_done"], 1)
            dve.wait_ge(s["dh_done"], 4 + NB + 3)
            dve.wait_ge(s["map_in"], 48)
            for j in range(CH_FIRST):
                if j + AHEAD >= SLOTS:
                    ahead(0, j)
                for k in MAP_TILES[j]:
                    for m, mu in enumerate((MUW, MUA)):
                        n = 2 * k + m
                        if n >= 4:
                            dve.wait_ge(s["xw_used"], n - 3)
                        V.scalar_tensor_tensor(xw[:, n % 4, :], dhv[:, k, :], par2[:, mu + k:mu + k + 1], hTv[:, k, 0:T],
                                               ALU.mult, ALU.add).then_inc(s["xw_ready"], 1)
                if j % 2 == 1:
                    tile_out(0, j // 2)

            def mix(r, q):
                def go(j):
                    ahead(q * CH_STEP + BASE_STEP, j)

                def out(n):
                    tile_out(q, n)

                go(0)
                dve.wait_ge(s["kk_ps"], r + 1)
                V.tensor_scalar(rn[:, :], B[2][:, 0:T], 1e-24, None, ALU.max).then_inc(s["kk_max"], 1)
                dve.wait_ge(s["decay_in"], r + 1)
                V.tensor_tensor_scan(cl[:, :], cfs("segment"), pm[:, :], 0.0, ALU.mult, ALU.add).then_inc(s["cum_ready"], 1)
                dve.wait_ge(s["cum_ready"], r + 1)
                V.tensor_tensor(pm[:, :], cl[:, :], pm[:, :], ALU.subtract).then_inc(s["cumx_ready"], 1)
                dve.wait_ge(s["kk_norm"], r + 1)
                V.reciprocal(rn[:, :], rn[:, :]).then_inc(s["kk_rn"], 1)
                dve.wait_ge(s["cur_m_ready"], r + 1)
                dve.wait_ge(s["kf_ready"], r * 2 + 2)
                V.scalar_tensor_tensor(sq[:, :], rS[:, :], cur_m[:, R_K:R_K + 1], kf[:, :], ALU.mult, ALU.mult
                                       ).then_inc(s["rk_ready"], 1)
                dve.wait_ge(s["kk_rn"], r + 1)
                V.scalar_tensor_tensor(kkn[:, :], kS[:, :], cur_m[:, K_K:K_K + 1], rn[:, :], ALU.mult, ALU.mult
                                       ).then_inc(s["kkn_ready"], 1)
                dve.wait_ge(s["kkn_ready"], r + 1)
                dve.wait_ge(s["exp_ready"], r * 3 + 3)
                V.scalar_tensor_tensor(ar[:, 0, :], kkn[:, :], -1.0, pm[:, :], ALU.mult, ALU.mult).then_inc(s["ah_ready"], 1)
                dve.wait_ge(s["api_ready"], r + 1)
                V.tensor_tensor(bU[:, :], kkn[:, :], aS[:, :], ALU.mult).then_inc(s["bh_ready"], 1)
                V.tensor_tensor(ar[:, 1, :], rS[:, :], pd[:, :], ALU.mult).then_inc(s["rh_ready"], 1)
                dve.wait_ge(s["ah_ready"], r + 1)
                dve.wait_ge(s["rh_ready"], r * 2 + 1)
                V.tensor_copy(zr[:, :, 0:2 * TB].rearrange("p b (a t) -> p b a t", a=2),
                              ar[:, :, TP:T].rearrange("p a (b t) -> p b a t", t=TB)).then_inc(s["rh_ready"], 1)
                dve.wait_ge(s["rk_ps"], r + 1)
                V.tensor_tensor(bv[:, :], B[3][:, 0:T], vS[:, :], ALU.mult).then_inc(s["bv_ready"], 1)
                go(1)
                go(2)
                out(0)
                bd = [P, G, 2, C]
                sb, sk = [w[:, 0:2 * T].rearrange("p (g a c) -> p g a c", g=G, a=2) for w in (B01, B23)]
                dve.wait_ge(s["score_ps"], r * 3 + 1)
                V.tensor_tensor(Tm[:, :, :], sb[:, :, 0, :], cms("quads").rearrange("p (g c) -> p g c", g=G), ALU.mult
                                ).then_inc(s["dve_step"], 1)
                dve.wait_ge(s["dve_step"], r * 6 + 1)
                V.tensor_tensor(Y[:, :, :], Tm[:, :, :], istk.unsqueeze(1).to_broadcast([P, G, C]), ALU.add).then_inc(s["y_ready"], 1)
                V.tensor_tensor(ARB[:, :, :], sb[:, :, 1, :], cms("incl").rearrange("p (g c) -> p g c", g=G), ALU.mult)
                dve.wait_ge(s["score_ps"], r * 3 + 2)
                V.tensor_tensor(AKBD[:, :, :, :], sk[:, :, 0, :].unsqueeze(2).to_broadcast(bd),
                                cms("strict").rearrange("p (g h c) -> p g h c", g=G, h=2), ALU.mult)
                dve.wait_ge(s["score_ps"], r * 3 + 3)
                V.tensor_tensor(ABD[:, :, :, :], B[4][:, 0:T].rearrange("p (g c) -> p g c", g=G).unsqueeze(2).to_broadcast(bd),
                                cms("lower").rearrange("p (g h c) -> p g h c", g=G, h=2), ALU.mult)
                V.tensor_tensor(ARK[:, :, :], sk[:, :, 1, :], cms("incl").rearrange("p (g c) -> p g c", g=G), ALU.mult
                                ).then_inc(s["ark_ready"], 1)
                for i in range(ROUNDS):
                    dve.wait_ge(s["t_ps"], r * (LEVELS + ROUNDS) + i + 1)
                    V.tensor_tensor(Tm[:, :, :].rearrange("p g c -> p (g c)"), B[0][:, 0:T], cms("quads"), ALU.mult
                                    ).then_inc(s["dve_step"], 1)
                    dve.wait_ge(s["dve_step"], r * 6 + (i + 2))
                    V.tensor_tensor(Y[:, :, :], Tm[:, :, :], istk.unsqueeze(1).to_broadcast([P, G, C]), ALU.add
                                    ).then_inc(s["y_ready"], 1)
                    if i == 0:
                        go(3)
                lv = CM["level"][0]
                for n in range(LEVELS):
                    w = T if n < SMALL else TP
                    dve.wait_ge(s["t_ps"], r * (LEVELS + ROUNDS) + (ROUNDS + n + 1))
                    V.tensor_tensor(Tm[:, :, :].rearrange("p g c -> p (g c)")[:, 0:w], B[0][:, 0:w],
                                    cm[:, lv + n * T:lv + n * T + w], ALU.mult).then_inc(s["t_ready"], 1)
                    if n == 0:
                        out(1)
                    dve.wait_ge(s["m_ps"], r * LEVELS + n + 1)
                    dve.wait_ge(s["ybd_ready"], r * (2 * LEVELS + 2) + 2 * n + 2)
                    Yf = Y[:, :, :].rearrange("p g c -> p (g c)")[:, 0:w]
                    V.tensor_tensor(Yf, B[1][:, 0:w], Yf, ALU.add).then_inc(s["y_ready"], 1)
                    go(4 + n)
                    if n == 2:
                        out(2)
                for g in range(GP):
                    dve.wait_ge(s["rhs_ps"], r * GP + g + 1)
                    w = 2 * C if g == 0 else C
                    V.tensor_copy(RHS[:, :, :].rearrange("p a c -> p (a c)")[:, 0:w], B[2][:, 0:w]).then_inc(s["rhs_ready"], 1)
                    dve.wait_ge(s["u_ps"], r * GP + g + 1)
                    if g == 0:
                        V.tensor_copy(Us[:, 0:G:G - 1, :], B[3][:, 0:2 * C].rearrange("p (a c) -> p a c", a=2)).then_inc(s["u_ready"], 1)
                    else:
                        V.tensor_copy(Us[:, g, :], B[3][:, 0:C]).then_inc(s["u_ready"], 1)
                    dve.wait_ge(s["s_ps"], r * GP + g + 1)
                    decay = pd[:, C * g + C - 1:C * g + C]
                    if g == 0:
                        V.tensor_scalar(Ss[:, 0, :], B[0][:, 0:C], decay, None, ALU.mult).then_inc(s["s_ready"], 1)
                    else:
                        dve.wait_ge(s["sd_ready"], r * (GP - 1) + g)
                        V.scalar_tensor_tensor(Ss[:, g, :], B[0][:, 0:C], decay, Sd[:, :], ALU.mult, ALU.add).then_inc(s["s_ready"], 1)
                    if g in (1, 3):
                        go(8 + g // 2)
                    if g == 2:
                        out(3)
                dve.wait_ge(s["tails_ready"], r * 2 + 2)
                V.tensor_tensor(xpB[:, :, :], tails[:, 0, :].unsqueeze(1).to_broadcast([P, NB, C]),
                                cfs("batch").unsqueeze(2).to_broadcast([P, NB, C]), ALU.mult).then_inc(s["xpb_ready"], 1)
                go(10)
                out(4)
                dve.wait_ge(s["mean_ps"], r + 1)
                V.tensor_tensor(dO[:, :], O_s[:, :], B[5][:, 0:T], ALU.subtract).then_inc(s["dev_ready"], 1)
                dve.wait_ge(s["send_ps"], r + 1)
                dve.wait_ge(s["s0t_ready"], r * 2 + 2)
                V.tensor_tensor(so[:, :, :].rearrange("p b c -> p (b c)"), B[3][:, :],
                                S0D[:, :, :].rearrange("p b c -> p (b c)"), ALU.add).then_inc(s["send_ready"], 1)
                go(11)
                dve.wait_ge(s["sd_done"], r + 1)
                V.reciprocal(sd[:, :], sd[:, :]).then_inc(s["dve_step"], 1)
                dve.wait_ge(s["dve_step"], r * 6 + 4)
                V.scalar_tensor_tensor(dO[:, :], dO[:, :], cur_m[:, LN_W:LN_W + 1], sd[:, :], ALU.mult, ALU.mult).then_inc(s["dve_step"], 1)
                dve.wait_ge(s["dve_step"], r * 6 + 5)
                V.scalar_tensor_tensor(dO[:, :], dO[:, :], cur_m[:, LN_B:LN_B + 1], bv[:, :], ALU.add, ALU.add).then_inc(s["dve_step"], 1)
                dve.wait_ge(s["dve_step"], r * 6 + 6)
                dve.wait_ge(s["sgs_ready"], r + 1)
                V.tensor_tensor(yf[:, ds(r * T, T)], dO[:, :], sg[:, :], ALU.mult).then_inc(s["y_done"], 1)
                out(5)

            with dve.Fori(1, PAIRS) as q:
                mix(q - 1, q)
            mix(PAIRS - 1, PAIRS)

            def early(*js):
                for j in js:
                    ahead(BASE_EARLY, j)

            E = EXT
            count = cfs("count").rearrange("p (g t) -> p g t", t=16)
            steps = 3

            def window(g):
                nonlocal steps
                w = WINDOWS[g]
                u = uS[:, 2 * g:2 * g + 2, :]
                samples = ues[g][:, :, BUF + TP:E].rearrange("p k (b t) -> p k b t", b=NB)
                dve.wait_ge(s["filled"], 12 + 2 * g + 2)
                a = NB * BUF * (2 * g % 4)
                V.tensor_copy(samples[:, :, :, 0:BUF], B[g // 2][:, a:a + 2 * NB * BUF]
                              .rearrange("p (k b t) -> p k b t", k=2, b=NB)).then_inc(s["chain"], 1)
                src = ues[g]
                for n in range(g + 1):
                    steps += 1
                    dve.wait_ge(s["chain"], steps)
                    dst, h = (win_a, win_b)[n % 2], 2 ** n
                    V.tensor_tensor(dst[:, :, 2 * h - 1:E], src[:, :, 2 * h - 1:E], src[:, :, h - 1:E - h], ALU.add
                                    ).then_inc(s["chain"], 1)
                    src = dst
                steps += 1
                dve.wait_ge(s["chain"], steps)
                V.tensor_tensor(head[:, :, :], src[:, :, BUF:BUF + 16],
                                count[:, g].unsqueeze(1).to_broadcast([P, 2, 16]), ALU.mult).then_inc(s["chain"], 1)
                steps += 1
                dve.wait_ge(s["chain"], steps)
                V.tensor_tensor(u[:, :, 0:16], head[:, :, :], u[:, :, 0:16], ALU.subtract).then_inc(s["mixed"], 1)
                V.scalar_tensor_tensor(u[:, :, 16:TP], src[:, :, BUF + 16:BUF + TP], 1.0 / w, u[:, :, 16:TP],
                                       ALU.mult, ALU.subtract).then_inc(s["mixed"], 1)
                for k in range(2):
                    us = u[:, k, TP:T].rearrange("p (b t) -> p b t", b=NB)
                    V.scalar_tensor_tensor(us, src[:, k, BUF + TP:E].rearrange("p (b t) -> p b t", b=NB)[:, :, BUF:BUF + TB],
                                           1.0 / w, us, ALU.mult, ALU.subtract).then_inc(s["mixed"], 1)

            def gated(m):
                dve.wait_ge(s["pyb_ps"], m + 1)
                if m >= 2:
                    dve.wait_ge(s["ybl_ready"], m - 1)
                V.scalar_tensor_tensor(ytmp[:, m % 2, :], B[2 + m % 2][:, 0:T], par2[:, PSC + m:PSC + m + 1], gp[:, m, :],
                                       ALU.mult, ALU.mult).then_inc(s["yb_ready"], 1)

            early(0, 1)
            dve.wait_ge(s["utok_ps"], 4)
            window(0)
            early(2, 3)
            window(1)
            early(4, 5)
            window(2)
            early(6, 7)
            window(3)
            early(8, 9)
            dve.wait_ge(s["gsil_ready"], 1)
            gated(0)
            gated(1)
            early(10)
            gated(2)
            gated(3)
            early(11)
            for m in range(4, 8):
                gated(m)
            early(12)
            dve.wait_ge(s["rows_out"], 16 * (18 + 1 + 1 + NB))
            gates = ((kS[:, :], rS[:, :]), (vS[:, :], gS[:, :]), (gt[:, 0, :], gt[:, 1, :]), (gt[:, 2, :], gt[:, 3, :]))
            dve.wait_ge(s["sb_ready"], 4)
            dve.wait_ge(s["gates_ready"], 4)

            def early_merge(i):
                dve.wait_ge(s["chunk_used"], BASE_EARLY + 2 * EARLY + EARLY + i + 1)
                sa, sb_ = gates[i]
                V.tensor_tensor(sa, sa, (acc[0], acc[1], B[4], B[5])[i][:, 0:T], ALU.mult)
                V.tensor_tensor(sb_, sb_, B[i][:, 0:T], ALU.mult).then_inc(s["mb_ready"], 1)
                dve.wait_ge(s["mb_ready"], i + 1)
                V.tensor_tensor(mm_[:, i % 2, :], sa, sb_, ALU.add).then_inc(s["m_ready"], 1)
                dve.wait_ge(s["mh_ready"], i + 1)
                V.tensor_tensor(ml[:, T * i:T * (i + 1)], mm_[:, i % 2, :], mh[:, T * i:T * (i + 1)].bitcast(F32),
                                ALU.subtract).then_inc(s["ml_ready"], 1)

            early(13)
            early_merge(0)
            early(14)
            early_merge(1)
            early_merge(2)
            early(15)
            early_merge(3)

            with dve.Fori(EARLY // 2, KT // 2) as n:
                for m in range(2):
                    i = n * 2 + m
                    banks = (B[0], B[1]) if m == 0 else (B[4], B[5])
                    for j in range(CH_MERGE):
                        ahead(n * (2 * CH_MERGE) + BASE_MERGE, CH_MERGE * m + j)
                    dve.wait_ge(s["chunk_used"], i * CH_MERGE + (BASE_MERGE + 6))
                    dve.wait_ge(s["sb_ready"], i + 1)
                    V.tensor_tensor(ga[:, m, :], ga[:, m, :], banks[0][:, 0:T], ALU.mult)
                    V.tensor_tensor(gb[:, m, :], gb[:, m, :], banks[1][:, 0:T], ALU.mult).then_inc(s["mb_ready"], 1)
                    dve.wait_ge(s["mb_ready"], i + 1)
                    V.tensor_tensor(mm_[:, m, :], ga[:, m, :], gb[:, m, :], ALU.add).then_inc(s["m_ready"], 1)
                    dve.wait_ge(s["mh_ready"], i + 1)
                    V.tensor_tensor(ml[:, ds(n * (2 * T) + m * T, T)], mm_[:, m, :],
                                    mh[:, ds(n * (2 * T) + m * T, T)].bitcast(F32), ALU.subtract).then_inc(s["ml_ready"], 1)

            def out_tile(n, m, first=False):
                i = n * 2 + m
                for h in range(2):
                    ahead(n * 4 + BASE_OUT, 2 * m + h)
                dve.wait_ge(s["so_ready"], i + 1)
                V.tensor_tensor(o2[:, ds(n * (2 * T) + m * T, T)], acc[m][:, 0:T],
                                par2[:, ds(n * 2 + (NPOST + m), 1)].to_broadcast([P, T]), ALU.mult).then_inc(s["o2_ready"], 1)
                if first:
                    V.tensor_copy(sacc[:, :], sqo[:, m, :]).then_inc(s["sacc_ready"], 1)
                else:
                    dve.wait_ge(s["sacc_ready"], i)
                    V.tensor_tensor(sacc[:, :], sacc[:, :], sqo[:, m, :], ALU.add).then_inc(s["sacc_ready"], 1)

            out_tile(0, 0, first=True)
            out_tile(0, 1)
            with dve.Fori(1, KT // 2) as n:
                for m in range(2):
                    out_tile(n, m)
            dve.wait_ge(s["srt"], 1)
            V.reciprocal(sacc[:, :], sacc[:, :]).then_inc(s["chain"], 1)
            dve.wait_ge(s["chain"], steps + 1)
            dve.wait_ge(s["o2_ready"], KT)

            def lower_part(k):
                dve.wait_ge(s["x1h_ready"], k + 1)
                V.tensor_tensor(x1l[:, T * k:T * (k + 1)], xT[:, T * k:T * (k + 1)],
                                x1h[:, T * k:T * (k + 1)].bitcast(F32), ALU.subtract).then_inc(s["x1l_ready"], 1)

            for k in range(KT):
                V.tensor_tensor(o2[:, T * k:T * (k + 1)], o2[:, T * k:T * (k + 1)], sacc[:, :], ALU.mult).then_inc(s["x1a"], 1)
                if k >= 3:
                    lower_part(k - 3)
            for k in range(KT - 3, KT):
                lower_part(k)

            def gate_tile(n, m, early=False, last=False):
                i = n * 2 + m
                for h in range(2):
                    if not last or 2 * m + h + AHEAD < 4:
                        ahead(n * 4 + BASE_GATE, 2 * m + h)
                dve.wait_ge(s["g3_ready"], i + 1)
                if early:
                    e = emb[:, :, :].rearrange("p k t -> p (k t)")[:, ds(n * (2 * T) + m * T, T)]
                else:
                    dve.wait_ge(s["ple_ps"], i + 1)
                    e = B[m][:, 0:T]
                V.tensor_tensor(g3[:, m, :], g3[:, m, :], e, ALU.mult).then_inc(s["g3m"], 1)
                dve.wait_ge(s["g3m"], i + 1)
                V.tensor_tensor(yo[:, m, :], g3[:, m, :], xT[:, ds(n * (2 * T) + m * T, T)], ALU.add).then_inc(s["yo_ready"], 1)

            dve.wait_ge(s["emb_done"], EMB)
            with dve.Fori(0, EMB // 2) as n:
                for m in range(2):
                    gate_tile(n, m, early=True)
            with dve.Fori(EMB // 2, KT // 2 - 1) as n:
                for m in range(2):
                    gate_tile(n, m)
            for m in range(2):
                gate_tile(KT // 2 - 1, m, last=True)

        @block.tensor
        def _(pe):
            M = nc.tensor

            def passes(out, slot, k, hi, lo, width, first, last):
                wcol = slice(P * k, P * (k + 1))
                M.matmul(out[:, 0:width], wh[:, slot, wcol], hi, start=first, stop=False)
                M.matmul(out[:, 0:width], wh[:, slot, wcol], lo, start=False, stop=False)
                return M.matmul(out[:, 0:width], wl[:, slot, wcol], hi, start=False, stop=last)

            def chunk(count, j, out, hi, lo, pitch, width, k0, first, last, part=None):
                slot = j % SLOTS
                ks = range(KC) if part is None else part
                for k in ks:
                    if k == 0:
                        pe.wait_ge(s["lo_ready"], count + j + 1)
                    a = (k0 + k) * pitch
                    mm = passes(out, slot, k, hi[:, a:a + width], lo[:, a:a + width], width,
                                first and k == 0, last and k == KC - 1)
                    if k == KC - 1:
                        mm.then_inc(s["chunk_used"], 1)

            def transpose(out, in_):
                rows = in_.shape[0]
                return M.transpose(out, in_, ident[0:rows, 0:rows])

            pe.wait_ge(s["const_in"], 16)
            pe.wait_ge(s["rows_in"], 12 * 16)
            transpose(B[4][:, 0:NROW * PAIRS], rows[0:NROW * PAIRS, 0, :]).then_inc(s["par_ready"], 1)
            transpose(B[5][:, 0:NPAR2], rows[0:NPAR2, 1, :]).then_inc(s["par_ready"], 1)
            for t in range(3):
                n = P if t < 2 else NB * TB + NB
                pe.wait_ge(s["h_rows"], t + 1)
                if t == 2:
                    pe.wait_ge(s["act_start"], 1)
                for c in range(4):
                    if t:
                        pe.wait_ge(s["hT_done"], 4 * (t - 1) + c + 1)
                    for k in range(4):
                        col = P * (4 * c + k)
                        last = transpose(B[c][:, P * k:P * k + n], ht[0:n, t % 2, col:col + P])
                    last.then_inc(s["hT_ps"], 1)

            class Stream:

                def __init__(self, q):
                    self.q, self.at = q, 0

                def advance(self, n):
                    q = self.q
                    first = isinstance(q, int) and q == 0
                    for _ in range(n):
                        tile, kt = self.at // KT, self.at % KT
                        if kt == 0 and not (first and tile < 2):
                            pe.wait_ge(s["acc_free"], tile - 1 if first else q * TILES_STEP + (ACC_STEP + tile - 1))
                        width = TS if tile < 3 and not (isinstance(q, int) and q == PAIRS) else T
                        chunk(0 if first else q * CH_STEP + BASE_STEP, 2 * tile + kt // KC, acc[tile % 2], hh, hl, TS,
                              width, KC * (kt // KC), kt // KC == 0, kt // KC == 1, part=[kt % KC])
                        self.at += 1

            first = Stream(0)
            for c in range(4):
                if c < 3:
                    pe.wait_ge(s["h_split"], c + 1)
                else:
                    pe.wait_ge(s["hl_done"], 1)
                first.advance(4)
            pe.wait_ge(s["par_done"], 4)
            pe.wait_ge(s["dh_done"], 4)
            transpose(B[4][0:72, 0:P], hlast[:, 0:72]).then_inc(s["last_ps"], 1)
            transpose(B[5][0:72, 0:P], hlast[:, 72:144]).then_inc(s["last_ps"], 1)
            pe.wait_ge(s["map_in"], 48)
            for j in range(1, CH_FIRST):
                if j > 1:
                    first.advance(KC)
                for n in [2 * k + m for k in MAP_TILES[j] for m in range(2)]:
                    k = n // 2
                    pe.wait_ge(s["xw_ready"], n + 1)
                    M.matmul(B[n % 2][0:RANK, 0:T], (lw1, la1)[n % 2][:, k, :], xw[:, n % 4, :],
                             start=k == 0, stop=k == KT - 1).then_inc(s["xw_used"], 1)

            AFTER = dict(maps=13, key_norm=6, values=4, bonus=6, scores=3, keys=3, product=2, transpose=2,
                         update=2, chain_rhs=2, chain_u=2, chain_state=1, mean=4, chain_end=3, series=3)

            def mix(r, q):
                st = Stream(q)
                pe.wait_ge(s["s0_in"], r * 32 + 32)
                pe.wait_ge(s["last_done"], 2)
                for b in range(NB):
                    last = transpose(B45[:, P * b:P * (b + 1)], S0n[:, b, :])
                last.then_inc(s["s0_ps"], 1)
                pe.wait_ge(s["lw2_in"], r * 32 + 32)
                pe.wait_ge(s["act_start"], 3)
                M.matmul(B[0][:, 0:T], lw2[:, :], t1[:, :], start=True, stop=True)
                M.matmul(B[1][:, 0:T], la2[:, :], la[:, :], start=True, stop=True).then_inc(s["lora2_ps"], 1)
                st.advance(AFTER["maps"])
                pe.wait_ge(s["ksq_ready"], r + 1)
                M.matmul(B[2][:, 0:T], ones2, sq[:, :], start=True, stop=True).then_inc(s["kk_ps"], 1)
                st.advance(AFTER["key_norm"])
                pe.wait_ge(s["s0t_ready"], r * 2 + 1)
                pe.wait_ge(s["vbd_ready"], r * 2 + 2)
                for g in range(G):
                    last = transpose(B45[:, P * g:P * (g + 1)], flat(vBD, g))
                last.then_inc(s["vt_ps"], 1)
                st.advance(AFTER["values"])
                pe.wait_ge(s["rk_ready"], r + 1)
                M.matmul(B[3][:, 0:T], ones2, sq[:, :], start=True, stop=True).then_inc(s["rk_ps"], 1)
                st.advance(AFTER["bonus"])
                pe.wait_ge(s["vs_ready"], r * 2 + 2)
                pe.wait_ge(s["rh_ready"], r * 2 + 2)
                pe.wait_ge(s["dpl_ready"], r + 1)
                for b in range(NB):
                    last = M.matmul(B45[:, P * b:P * b + 2 * TB + C], S0T[:, b, :], zr[:, b, :], start=True, stop=True)
                last.then_inc(s["z_ps"], 1)
                pe.wait_ge(s["bbd_ready"], r * 2 + 2)
                pe.wait_ge(s["kbd_ready"], r * 2 + 2)
                for g in range(G):
                    last = M.matmul(B01[:, P * g:P * (g + 1)].rearrange("p (a c) -> p a c", a=2), flat(bBD, g),
                                    ar[:, :, tok(g)], start=True, stop=True)
                last.then_inc(s["score_ps"], 1)
                pe.wait_ge(s["bv_ready"], r + 1)
                for g in range(G):
                    last = M.matmul(B23[:, P * g:P * (g + 1)].rearrange("p (a c) -> p a c", a=2), flat(kBD, g),
                                    ar[:, :, tok(g)], start=True, stop=True)
                last.then_inc(s["score_ps"], 1)
                pe.wait_ge(s["zabd_ready"], r * 2 + 2)
                for g in range(G):
                    last = M.matmul(B[4][:, tok(g)], flat(aBD, g), bU[:, tok(g)], start=True, stop=True)
                last.then_inc(s["score_ps"], 1)
                st.advance(AFTER["scores"])
                pe.wait_ge(s["ark_ready"], r + 1)
                for g in range(G):
                    last = transpose(B45[:, P * g:P * (g + 1)], flat(bBD, g))
                last.then_inc(s["bt_ps"], 1)
                st.advance(AFTER["keys"])
                for g in range(G):
                    last = transpose(B23[:, P * g:P * (g + 1)], flat(kBD, g))
                last.then_inc(s["kt_ps"], 1)

                def products(n):
                    pe.wait_ge(s["y_ready"], r * (LEVELS + ROUNDS + 1) + (ROUNDS + n + 1))
                    for g in range(G if n < SMALL else GP):
                        last = M.matmul(B[0][:, tok(g)], flat(ABD, g), Y[:, g, :], start=True, stop=True)
                    last.then_inc(s["t_ps"], 1)

                def inverse_transpose(n):
                    pe.wait_ge(s["ybd_ready"], r * (2 * LEVELS + 2) + 2 * n + 2)
                    for g in range(G if n < SMALL else GP):
                        last = transpose(B45[:, P * g:P * (g + 1)], flat(YBD, g))
                    last.then_inc(s["x_ps"], 1)

                def update(n):
                    pe.wait_ge(s["t_ready"], r * LEVELS + n + 1)
                    pe.wait_ge(s["x_ready"], r * LEVELS + n + 1)
                    for g in range(G if n < SMALL else GP):
                        last = M.matmul(B[1][:, tok(g)], flat(XBD, g), Tm[:, g, :], start=True, stop=True)
                    last.then_inc(s["m_ps"], 1)

                for i in range(ROUNDS):
                    pe.wait_ge(s["y_ready"], r * (LEVELS + ROUNDS + 1) + i + 1)
                    for g in range(G):
                        last = M.matmul(B[0][:, tok(g)], flat(ABD, g), Y[:, g, :], start=True, stop=True)
                    last.then_inc(s["t_ps"], 1)
                    st.advance(AFTER["series"])
                for n in range(LEVELS):
                    products(n)
                    st.advance(AFTER["product"])
                    inverse_transpose(n)
                    st.advance(AFTER["transpose"])
                    update(n)
                    st.advance(AFTER["update"])
                pe.wait_ge(s["tail_ready"], r * 2 + 2)
                for n in range(2):
                    last = transpose(B[5][:, P * n:P * (n + 1)], tail4[:, n].rearrange("p h c -> p (h c)"))
                last.then_inc(s["tail_ps"], 1)
                for g in range(GP):
                    M.matmul(B[2][:, 0:C], flat(AKBD, g), Vs[:, g, :], start=True, stop=g == 0)
                    if g == 0:
                        M.matmul(B[2][:, C:2 * C], flat(AKBD, G - 1), Vs[:, G - 1, :], start=True, stop=False)
                        last = M.matmul(B[2][:, C:2 * C], ZaBD[:, :, :].rearrange("p h c -> p (h c)"), istk, start=False, stop=True)
                    else:
                        pe.wait_ge(s["s_ready"], r * GP + g)
                        last = M.matmul(B[2][:, 0:C], flat(aBD, g), Ss[:, g - 1, :], start=False, stop=True)
                    last.then_inc(s["rhs_ps"], 1)
                    st.advance(AFTER["chain_rhs"])
                    if g == 0:
                        pe.wait_ge(s["ybd_ready"], r * (2 * LEVELS + 2) + 2 * LEVELS + 2)
                    pe.wait_ge(s["rhs_ready"], r * GP + g + 1)
                    last = M.matmul(B[3][:, 0:C], flat(YBD, g), RHS[:, 0, :], start=True, stop=True)
                    if g == 0:
                        last = M.matmul(B[3][:, C:2 * C], flat(YBD, G - 1), RHS[:, 1, :], start=True, stop=True)
                    last.then_inc(s["u_ps"], 1)
                    st.advance(AFTER["chain_u"])
                    M.matmul(B[0][:, 0:C], flat(KtBD, g), Vs[:, g, :], start=True, stop=False)
                    pe.wait_ge(s["u_ready"], r * GP + g + 1)
                    M.matmul(B[0][:, 0:C], flat(BtBD, g), Us[:, g, :], start=False, stop=True).then_inc(s["s_ps"], 1)
                    st.advance(AFTER["chain_state"] if g < GP - 1 else AFTER["chain_end"])
                pe.wait_ge(s["ubd_ready"], r * 2 + 2)
                for g in range(G):
                    if g == 1:
                        pe.wait_ge(s["sbd_ready"], r * 2 + 2)
                    o = B[4][:, tok(g)]
                    M.matmul(o, flat(VtBD, g), ARK[:, g, :], start=True, stop=False)
                    if g == G - 1:
                        M.matmul(o, ident, Zs[:, 1, :], start=False, stop=False)
                    elif g:
                        M.matmul(o, flat(SBD, g - 1), ar[:, 1, tok(g)], start=False, stop=False)
                    last = M.matmul(o, flat(UBD, g), ARB[:, g, :], start=False, stop=True)
                last.then_inc(s["o_ps"], 1)
                pe.wait_ge(s["endbd_ready"], r * 2 + 2)
                transpose(B[0][:, 0:P], EndBD[:, :, :].rearrange("p h c -> p (h c)")).then_inc(s["end_ps"], 1)
                for name in ("xpb_ready", "xpk_ready"):
                    pe.wait_ge(s[name], r + 1)
                M.matmul(B[3][:, :], flat(UBD, G - 1), xpB[:, :, :].rearrange("p b c -> p (b c)"), start=True, stop=False)
                M.matmul(B[3][:, :], flat(VtBD, G - 1), xpK[:, :, :].rearrange("p b c -> p (b c)"), start=False, stop=True
                         ).then_inc(s["send_ps"], 1)
                pe.wait_ge(s["o_ready"], r + 1)
                M.matmul(B[5][:, 0:T], mean2, O_s[:, :], start=True, stop=True).then_inc(s["mean_ps"], 1)
                st.advance(AFTER["mean"])
                pe.wait_ge(s["dsq_ready"], r + 1)
                M.matmul(B[2][:, 0:T], mean2, dsq[:, :], start=True, stop=True).then_inc(s["var_ps"], 1)
                st.advance(TILES_STEP * KT - st.at)

            with pe.Fori(1, PAIRS) as q:
                mix(q - 1, q)
            mix(PAIRS - 1, PAIRS)

            def last_rows():
                pe.wait_ge(s["acc_free"], ACC_ALL)
                for k in range(8):
                    last = transpose(B[4 + k // 4][0:NB * TB + BUF, P * (k % 4):P * (k % 4 + 1)], uS[:, k, TP - BUF:T])
                    if k % 4 == 3:
                        last.then_inc(s["utok_ps"], 1)

            def early_gate(g, h):
                if g >= 2:
                    pe.wait_ge(s["gates_ready"], g - 1)
                chunk(BASE_EARLY, 2 * g + h, acc[g % 2], hh, hl, TS, T, KC * h, h == 0, h == 1)

            def early_branch(b, i):
                bank = B[i] if b else (acc[0], acc[1], B[4], B[5])[i]
                hi, lo = ((yah, yal), (ybh, ybl))[b]
                chunk(BASE_EARLY + 2 * EARLY, EARLY * b + i, bank, hi, lo, T, T, 0, True, True)

            def pool_map(m):
                pe.wait_ge(s["mixed"], 4 * (m // 2) + 4)
                if m >= 2:
                    pe.wait_ge(s["yb_ready"], m - 1)
                for k in range(2):
                    last = M.matmul(B[2 + m % 2][:, 0:T], pw[:, m // 2 * 2 + k, P * (m % 2):P * (m % 2) + P],
                                    uS[:, m // 2 * 2 + k, :], start=k == 0, stop=k == 1)
                last.then_inc(s["pyb_ps"], 1)

            pe.wait_ge(s["acc_free"], ACC_ALL - 1)
            early_gate(0, 0)
            last_rows()
            early_gate(0, 1)
            pe.wait_ge(s["pool_in"], 16)
            for k in range(8):
                w = NB * BUF
                last = transpose(B[k // 4][:, w * (k % 4):w * (k % 4 + 1)], spt[:, P * k:P * (k + 1)])
                if k % 4 == 3:
                    last.then_inc(s["utok_ps"], 1)
            for g in range(1, 4):
                for h in range(2):
                    early_gate(g, h)
            pe.wait_ge(s["yal_ready"], 1)
            pe.wait_ge(s["gates_ready"], 3)
            early_branch(0, 0)
            pe.wait_ge(s["gates_ready"], 4)
            early_branch(0, 1)
            pe.wait_ge(s["map_in"], 64)
            for m in range(4):
                pool_map(m)
            pe.wait_ge(s["utok_ev"], 2)
            early_branch(0, 2)
            for m in range(4, 8):
                pool_map(m)
            early_branch(0, 3)
            pe.wait_ge(s["ybl_ready"], 8)
            for i in range(EARLY):
                early_branch(1, i)

            def merge_tile(n, m):
                banks = (acc[0], acc[1], B[0], B[1]) if m == 0 else (B[2], B[3], B[4], B[5])
                count = n * (2 * CH_MERGE) + BASE_MERGE
                pe.wait_ge(s["m_ready"], n * 2 + m - 1)
                for g in range(2):
                    for h in range(2):
                        chunk(count, CH_MERGE * m + 2 * g + h, banks[g], hh, hl, TS, T, KC * h, h == 0, h == 1)
                chunk(count, CH_MERGE * m + 4, banks[2], yah, yal, T, T, 0, True, True)
                chunk(count, CH_MERGE * m + 5, banks[3], ybh, ybl, T, T, 0, True, True)

            with pe.Fori(EARLY // 2, KT // 2) as n:
                for m in range(2):
                    merge_tile(n, m)

            def out_tile(n, m, free, first=False):
                if free:
                    pe.wait_ge(s["o2_ready"], n * 2 + m - 1)
                for h in range(2):
                    if first:
                        pe.wait_ge(s["ml_ready"], KC * h + KC)
                    chunk(n * 4 + BASE_OUT, 2 * m + h, acc[m], mh, ml, T, T, KC * h, h == 0, h == 1)

            for m in range(2):
                out_tile(0, m, False, first=m == 0)
            sizes = (P, P, NB * TB)
            pe.wait_ge(s["x2_in"], 96)
            for k in range(KT):
                if k >= 4:
                    pe.wait_ge(s["xT_ready"], k - 3)
                for t in range(3):
                    last = transpose(B[k % 4][:, P * t:P * t + sizes[t]], xt2[0:sizes[t], t, P * k:P * (k + 1)])
                last.then_inc(s["xT_ps"], 1)
            pe.wait_ge(s["x2_in"], 96)
            for k in range(2):
                for t in range(3):
                    last = transpose(B[4 + k][:, P * t:P * t + sizes[t]], pt[0:sizes[t], t, P * k:P * (k + 1)])
                last.then_inc(s["pT_ps"], 1)
            with pe.Fori(1, KT // 2) as n:
                for m in range(2):
                    out_tile(n, m, True)
            pe.wait_ge(s["sacc_ready"], KT)
            pe.wait_ge(s["xT_ready"], KT + 2)
            M.matmul(B[5][:, 0:T], meand, sacc[:, :], start=True, stop=True).then_inc(s["ssq_ps"], 1)

            def embedding(n, m):
                pe.wait_ge(s[f"wple_in{m}"], n * 16 - (EMB // 2 - 1) * 16)
                for k in range(2):
                    last = M.matmul(B[m][:, 0:T], wple[:, m, P * k:P * (k + 1)], pT[:, k, :], start=k == 0, stop=k == 1)
                last.then_inc(s["ple_ps"], 1)

            def gate_tile(n, m, embed=True):
                for h in range(2):
                    chunk(n * 4 + BASE_GATE, 2 * m + h, acc[m], x1h, x1l, T, T, KC * h, h == 0, h == 1)
                if embed:
                    embedding(n, m)

            def tokens(i, m, free):
                pe.wait_ge(s["yo_ready"], i + 1)
                if free is not None:
                    pe.wait_ge(s["ytk_ready"], free)
                for t in range(3):
                    last = transpose(B[2 + m][0:sizes[t], P * t:P * (t + 1)], yo[:, m, P * t:P * t + sizes[t]])
                last.then_inc(s["yt_ps"], 1)

            pe.wait_ge(s["o2_ready"], KT)
            def early_embedding(i):
                if i >= 4:
                    pe.wait_ge(s["emb_done"], i - 3)
                for k in range(2):
                    w = wple[:, i, P * k:P * (k + 1)] if i < 2 else wple0[:, i - 2, P * k:P * (k + 1)]
                    last = M.matmul(B[i % 4][:, 0:T], w, pT[:, k, :], start=k == 0, stop=k == 1)
                last.then_inc(s["ple_ps"], 1)

            pe.wait_ge(s["map_in"], 16 * (4 + EMB))
            for i in range(4):
                early_embedding(i)
            for k in range(KC):
                if k % 2 == 0:
                    early_embedding(4 + k // 2)
                pe.wait_ge(s["x1l_ready"], k + 1)
                chunk(BASE_GATE, 0, acc[0], x1h, x1l, T, T, 0, True, False, part=[k])
            for k in range(KC):
                pe.wait_ge(s["x1l_ready"], KC + k + 1)
                chunk(BASE_GATE, 1, acc[0], x1h, x1l, T, T, KC, False, True, part=[k])
            gate_tile(0, 1, embed=False)
            tokens(0, 0, None)
            pe.wait_ge(s["yo_ready"], 1)
            gate_tile(1, 0, embed=False)
            tokens(1, 1, None)
            gate_tile(1, 1, embed=False)
            tokens(2, 0, 2)
            for start, stop in ((2, EMB // 2), (EMB // 2, KT // 2)):
                with pe.Fori(start, stop) as n:
                    gate_tile(n, 0, embed=start > 2)
                    tokens(n * 2 - 1, 1, n * 4 - 4)
                    gate_tile(n, 1, embed=start > 2)
                    tokens(n * 2, 0, n * 4 - 2)
            tokens(KT - 1, 1, 2 * KT - 4)


OUTS = [((1, TP, D), "float32"), ((NB, TB, D), "float32"), ((1, 1, 16, HD, HD), "float32"), ((1, 1, D), "float32"),
        ((1, 1, BUF, R), "float32"), ((1, NB, 16, HD, HD), "float32"), ((1, NB, D), "float32"), ((1, NB, BUF, R), "float32")]
INS = ["x_prompt", "x_sample", "state_wkv", "state_shift", "state_pool", "p_prompt", "p_sample", "norm_pre", "norm_post",
       "w_in", "mu_rkv", "mu_lora", "w0", "w1", "w2", "a0", "a1", "a2", "k_k", "k_a", "r_k", "ln_w", "ln_b", "pool_w",
       "pool_scale", "w_branch", "w_out", "w_ple", "w_ple_gate"]


def kernel(**inputs):
    import ml_dtypes
    from concourse import bacc
    from concourse.bass_utils import run_bass_kernel_spmd

    nc = bacc.Bacc("TRN2", target_bir_lowering=False, num_devices=1)
    const_f, const_m = shape_constants()
    arrays = {f"in_{n}": np.ascontiguousarray(inputs[n]) for n in INS}
    arrays["in_const_f"] = const_f
    arrays["in_const_m"] = const_m.astype(ml_dtypes.bfloat16)
    args = [nc.dram_tensor(n, a.shape, mybir.dt.from_np(a.dtype), kind="ExternalInput").ap() for n, a in arrays.items()]
    for i, (shape, dtype) in enumerate(OUTS):
        args.append(nc.dram_tensor(f"out_{i}", shape, mybir.dt.from_np(np.dtype(dtype)), kind="ExternalOutput").ap())
    build(nc, *args)
    r = run_bass_kernel_spmd(nc, [arrays], core_ids=[0])
    return tuple(r.results[0][f"out_{i}"] for i in range(len(OUTS)))
```
